# Optimizing a Trainium2 kernel written in Bass

```python
import functools
import jax, jax.numpy as jnp
from jax import lax
import numpy as np

D_MODEL = 1024
BATCH = 1
SEQ = 256
DEPTH = 2
DEC_BATCH = 8
DEC_SEQ = 4
PAST_LEN = 256
PAGE_SIZE = 128

HEAD_DIM = 64
ATT_HEADS = 8
KV_HEADS = 4
GQA_GROUP = ATT_HEADS // KV_HEADS
ATT_WIDTH = ATT_HEADS * HEAD_DIM
KV_WIDTH = KV_HEADS * HEAD_DIM
MOBA_BLOCK = 256
MOBA_TOPK = 3
Q_BLOCK = 64
ROPE_THETA = 10000.0
HG_HEADS = 4
HG_DK = 64
HG_DV = 64
HG_WIDTH = HG_HEADS * HG_DV
HG_CHUNK = 64
CONV_CH = 256
CONV_W = 3
MIX_WIDTH = ATT_WIDTH + HG_WIDTH + CONV_CH
N_MEM = 256
XA_HEADS = 4
XA_HEAD_DIM = 64
XA_WIDTH = XA_HEADS * XA_HEAD_DIM
D_FF = 2816
FFN_CONV_W = 3
EPS = 1e-6
IN_SPLITS = (ATT_WIDTH, KV_WIDTH, KV_WIDTH, HG_HEADS * HG_DK, HG_HEADS * HG_DK,
             HG_HEADS * HG_DV, HG_HEADS * HG_DV, CONV_CH, CONV_CH, CONV_CH)
IN_WIDTH = ATT_WIDTH + 2 * KV_WIDTH + 2 * HG_HEADS * HG_DK + 2 * HG_HEADS * HG_DV + 3 * CONV_CH

kernel_name = 'moba_hgrn2_shortconv_hybrid_step'

def rmsnorm(x, g):
    xf = x.astype(jnp.float32)
    y = xf * lax.rsqrt(jnp.mean(xf * xf, axis=-1, keepdims=True) + EPS)
    return (y * g.astype(jnp.float32)).astype(x.dtype)

def rope(x, pos):
    half = HEAD_DIM // 2
    inv = ROPE_THETA ** (-jnp.arange(half, dtype=jnp.float32) / half)
    ang = pos.astype(jnp.float32)[:, None] * inv[None, :]
    cos = jnp.cos(ang)[None, :, None, :]
    sin = jnp.sin(ang)[None, :, None, :]
    xf = x.astype(jnp.float32)
    x1, x2 = xf[..., :half], xf[..., half:]
    return jnp.concatenate([x1 * cos - x2 * sin, x2 * cos + x1 * sin], axis=-1).astype(x.dtype)

def causal_dwconv(u, prev, w):
    T = u.shape[1]
    W = w.shape[0]
    full = jnp.concatenate([prev.astype(u.dtype), u], axis=1)
    y = full[:, 0:T] * w[0]
    for j in range(1, W):
        y = y + full[:, j:j + T] * w[j]
    return y, full[:, full.shape[1] - (W - 1):]

def block_mean(kb):
    return jnp.mean(kb.astype(jnp.float32), axis=3).astype(kb.dtype)

def moba_attend(qg, kb, vb, kmean, n_past, own_k, own_v, own_mask, k_eff):
    scale = HEAD_DIM ** -0.5
    parts = []
    if k_eff > 0:
        n_cand = kmean.shape[2]
        gate = jnp.einsum('bkgqd,bknd->bkgqn', qg, kmean).astype(jnp.float32)
        gate = jnp.where(jnp.arange(n_cand) < n_past, gate, -jnp.inf)
        _, sel = lax.top_k(gate, k_eff)
        valid = jnp.arange(k_eff) < n_past
        bi = jnp.arange(kb.shape[0])[:, None, None, None]
        hi = jnp.arange(KV_HEADS)[None, :, None, None]
        for r in range(k_eff):
            k_sel = kb[bi, hi, sel[..., r]]
            s = jnp.einsum('bkgqd,bkgqmd->bkgqm', qg, k_sel).astype(jnp.float32) * scale
            parts.append(jnp.where(valid[r], s, -jnp.inf))
    s_own = jnp.einsum('bkgqd,bkmd->bkgqm', qg, own_k).astype(jnp.float32) * scale
    parts.append(jnp.where(own_mask, s_own, -jnp.inf))
    p = jax.nn.softmax(jnp.concatenate(parts, axis=-1), axis=-1).astype(own_v.dtype)
    out = jnp.einsum('bkgqm,bkmd->bkgqd', p[..., k_eff * MOBA_BLOCK:], own_v)
    for r in range(k_eff):
        v_sel = vb[bi, hi, sel[..., r]]
        out = out + jnp.einsum('bkgqm,bkgqmd->bkgqd', p[..., r * MOBA_BLOCK:(r + 1) * MOBA_BLOCK], v_sel)
    return out

def moba_prompt(q, k, v):
    B, T = q.shape[0], q.shape[1]
    nb = -(-T // MOBA_BLOCK)
    pad = nb * MOBA_BLOCK - T
    kp = jnp.pad(k, ((0, 0), (0, pad), (0, 0), (0, 0)))
    vp = jnp.pad(v, ((0, 0), (0, pad), (0, 0), (0, 0)))
    kb = kp.reshape(B, nb, MOBA_BLOCK, KV_HEADS, HEAD_DIM).transpose(0, 3, 1, 2, 4)
    vb = vp.reshape(B, nb, MOBA_BLOCK, KV_HEADS, HEAD_DIM).transpose(0, 3, 1, 2, 4)
    kmean = block_mean(kb)
    k_eff = min(MOBA_TOPK, nb - 1)
    nq = T // Q_BLOCK
    qg = q.reshape(B, nq, Q_BLOCK, KV_HEADS, GQA_GROUP, HEAD_DIM).transpose(1, 0, 3, 4, 2, 5)

    def one(args):
        qi, qc = args
        q0 = qi * Q_BLOCK
        b = q0 // MOBA_BLOCK
        own_k = lax.dynamic_index_in_dim(kb, b, axis=2, keepdims=False)
        own_v = lax.dynamic_index_in_dim(vb, b, axis=2, keepdims=False)
        kpos = b * MOBA_BLOCK + jnp.arange(MOBA_BLOCK)
        qpos = q0 + jnp.arange(Q_BLOCK)
        mask = kpos[None, :] <= qpos[:, None]
        return moba_attend(qc, kb, vb, kmean, b, own_k, own_v, mask, k_eff)

    out = lax.map(one, (jnp.arange(nq, dtype=jnp.int32), qg))
    return out.transpose(1, 0, 4, 2, 3, 5).reshape(B, T, ATT_WIDTH)

def moba_sample(q, k, v, k_past, v_past):
    DB, S = q.shape[0], q.shape[1]
    P = k_past.shape[1]
    nb = P // MOBA_BLOCK
    start = nb * MOBA_BLOCK
    qg = q.reshape(DB, S, KV_HEADS, GQA_GROUP, HEAD_DIM).transpose(0, 2, 3, 1, 4)
    k_eff = min(MOBA_TOPK, nb)
    kb = vb = kmean = None
    if k_eff > 0:
        kb = k_past[:, :start].reshape(DB, nb, MOBA_BLOCK, KV_HEADS, HEAD_DIM).transpose(0, 3, 1, 2, 4)
        vb = v_past[:, :start].reshape(DB, nb, MOBA_BLOCK, KV_HEADS, HEAD_DIM).transpose(0, 3, 1, 2, 4)
        kmean = block_mean(kb)
    own_k = jnp.concatenate([k_past[:, start:].astype(k.dtype), k], axis=1).transpose(0, 2, 1, 3)
    own_v = jnp.concatenate([v_past[:, start:].astype(v.dtype), v], axis=1).transpose(0, 2, 1, 3)
    kpos = start + jnp.arange(own_k.shape[2])
    qpos = P + jnp.arange(S)
    mask = kpos[None, :] <= qpos[:, None]
    out = moba_attend(qg, kb, vb, kmean, nb, own_k, own_v, mask, k_eff)
    return out.transpose(0, 3, 1, 2, 4).reshape(DB, S, ATT_WIDTH)

def hgrn2_recurrence(q, k, v, logf, s0):
    B, T = q.shape[0], q.shape[1]
    L = min(HG_CHUNK, T)
    n = -(-T // L)
    pad = n * L - T

    def chunks(a):
        a = jnp.pad(a.astype(jnp.float32), ((0, 0), (0, pad), (0, 0), (0, 0)))
        return a.reshape(B, n, L, a.shape[2], a.shape[3]).transpose(1, 0, 3, 2, 4)

    tri = jnp.tril(jnp.ones((L, L), dtype=bool))

    def step(S, inp):
        qc, kc, vc, lc = inp
        A = jnp.cumsum(lc, axis=2)
        o_inter = jnp.einsum('bhld,bhdv->bhlv', qc * jnp.exp(A), S)
        diff = A[:, :, :, None, :] - A[:, :, None, :, :]
        decay = jnp.exp(jnp.where(tri[:, :, None], diff, -jnp.inf))
        scores = jnp.einsum('bhtd,bhsd,bhtsd->bhts', qc, kc, decay)
        o_intra = jnp.einsum('bhts,bhsv->bhtv', scores, vc)
        A_end = A[:, :, -1:, :]
        S_new = jnp.exp(A_end[:, :, 0, :, None]) * S + jnp.einsum('bhsd,bhsv->bhdv', kc * jnp.exp(A_end - A), vc)
        return S_new, o_inter + o_intra

    S_fin, o = lax.scan(step, s0.astype(jnp.float32), (chunks(q), chunks(k), chunks(v), chunks(logf)))
    o = o.transpose(1, 0, 3, 2, 4).reshape(B, n * L, HG_HEADS, HG_DV)[:, :T]
    return o, S_fin

def hgrn2_mixer(hq, hf, hi, hg, lb, norm_g, s0):
    B, T = hq.shape[0], hq.shape[1]
    q = jax.nn.silu(hq).reshape(B, T, HG_HEADS, HG_DK)
    z = hf.astype(jnp.float32).reshape(B, T, HG_HEADS, HG_DK)
    lbh = lb.reshape(HG_HEADS, HG_DK)
    logf = jnp.log(lbh + (1.0 - lbh) * jax.nn.sigmoid(z))
    k = (1.0 - lbh) * jax.nn.sigmoid(-z)
    v = hi.reshape(B, T, HG_HEADS, HG_DV)
    o, S = hgrn2_recurrence(q, k, v, logf, s0)
    o = rmsnorm(o, norm_g.reshape(HG_HEADS, HG_DV))
    o = o.reshape(B, T, HG_WIDTH) * jax.nn.silu(hg.astype(jnp.float32))
    return o.astype(hq.dtype), S

def mixer_layer(x, pos, attn, hg_state, conv_prev, g, w_in_l, w_out_l, lb, norm_g, cw):
    B, T = x.shape[0], x.shape[1]
    h = rmsnorm(x, g) @ w_in_l
    idx = [int(i) for i in np.cumsum(IN_SPLITS)[:-1]]
    q, k, v, hq, hf, hi, hg, cb, cc, ch = jnp.split(h, idx, axis=-1)
    q = rope(q.reshape(B, T, ATT_HEADS, HEAD_DIM), pos)
    k = rope(k.reshape(B, T, KV_HEADS, HEAD_DIM), pos)
    v = v.reshape(B, T, KV_HEADS, HEAD_DIM)
    a = attn(q, k, v)
    o_h, S = hgrn2_mixer(hq, hf, hi, hg, lb, norm_g, hg_state)
    yc, conv_new = causal_dwconv(cc * ch, conv_prev, cw)
    o_c = cb * yc
    y = jnp.concatenate([a, o_h, o_c.astype(a.dtype)], axis=-1) @ w_out_l
    return x + y, k, v, S, conv_new

def memory_kv(mem, g, wk, wv):
    B = mem.shape[0]
    m = rmsnorm(mem, g)
    return ((m @ wk).reshape(B, N_MEM, XA_HEADS, XA_HEAD_DIM),
            (m @ wv).reshape(B, N_MEM, XA_HEADS, XA_HEAD_DIM))

def cross_attn(x, g, wq, wo, mk, mv):
    B, T = x.shape[0], x.shape[1]
    q = (rmsnorm(x, g) @ wq).reshape(B, T, XA_HEADS, XA_HEAD_DIM)
    s = jnp.einsum('bthd,bmhd->bhtm', q, mk.astype(q.dtype)).astype(jnp.float32) * XA_HEAD_DIM ** -0.5
    p = jax.nn.softmax(s, axis=-1).astype(q.dtype)
    o = jnp.einsum('bhtm,bmhd->bthd', p, mv.astype(q.dtype)).reshape(B, T, XA_WIDTH)
    return o @ wo

def conv_ffn(x, g, w_up_l, cw, w_down_l, prev):
    u = rmsnorm(x, g) @ w_up_l
    u, new = causal_dwconv(u, prev, cw)
    a, b = jnp.split(u, 2, axis=-1)
    return (jax.nn.silu(a) * b) @ w_down_l, new

def setup_inputs(seed: int = 0) -> dict:
    key = jax.random.key(seed)
    keys = jax.random.split(key, 32)
    c = [0]

    def nxt():
        kk = keys[c[0]]
        c[0] += 1
        return kk

    def nrm(shape, scale):
        return jax.random.normal(nxt(), shape, jnp.float32) * scale

    def gain(shape):
        return 1.0 + nrm(shape, 0.02)

    n_pages = PAST_LEN // PAGE_SIZE
    n_used = DEC_BATCH * n_pages
    n_pool = (5 * n_used + 3) // 4
    x_prompt = nrm((BATCH, SEQ, D_MODEL), 1.0)
    x_sample = nrm((DEC_BATCH, DEC_SEQ, D_MODEL), 1.0)
    cache_k = nrm((DEPTH, n_pool, PAGE_SIZE, KV_HEADS, HEAD_DIM), 1.0)
    cache_v = nrm((DEPTH, n_pool, PAGE_SIZE, KV_HEADS, HEAD_DIM), 1.0)
    cache_mem_k = nrm((DEPTH, DEC_BATCH, N_MEM, XA_HEADS, XA_HEAD_DIM), 1.0)
    cache_mem_v = nrm((DEPTH, DEC_BATCH, N_MEM, XA_HEADS, XA_HEAD_DIM), 1.0)
    state_hgrn = nrm((DEPTH, DEC_BATCH, HG_HEADS, HG_DK, HG_DV), 0.3)
    state_conv = nrm((DEPTH, DEC_BATCH, CONV_W - 1, CONV_CH), 1.0)
    state_ffn = nrm((DEPTH, DEC_BATCH, FFN_CONV_W - 1, 2 * D_FF), 1.0)
    page_table = jax.random.permutation(nxt(), n_pool)[:n_used].reshape(DEC_BATCH, n_pages).astype(jnp.int32)
    mem_prompt = nrm((BATCH, N_MEM, D_MODEL), 1.0)
    return {
        'x_prompt': x_prompt, 'x_sample': x_sample,
        'cache_k': cache_k, 'cache_v': cache_v,
        'cache_mem_k': cache_mem_k, 'cache_mem_v': cache_mem_v,
        'state_hgrn': state_hgrn, 'state_conv': state_conv, 'state_ffn': state_ffn,
        'page_table': page_table, 'mem_prompt': mem_prompt,
        'g_mix': gain((DEPTH, D_MODEL)),
        'w_in': nrm((DEPTH, D_MODEL, IN_WIDTH), D_MODEL ** -0.5),
        'w_out': nrm((DEPTH, MIX_WIDTH, D_MODEL), MIX_WIDTH ** -0.5),
        'hg_lb_logits': nrm((DEPTH, HG_HEADS * HG_DK), 0.5),
        'hg_norm_g': gain((DEPTH, HG_WIDTH)),
        'conv_w': nrm((DEPTH, CONV_W, CONV_CH), CONV_W ** -0.5),
        'g_xattn': gain((DEPTH, D_MODEL)),
        'g_mem': gain((DEPTH, D_MODEL)),
        'w_xq': nrm((DEPTH, D_MODEL, XA_WIDTH), D_MODEL ** -0.5),
        'w_mk': nrm((DEPTH, D_MODEL, XA_WIDTH), D_MODEL ** -0.5),
        'w_mv': nrm((DEPTH, D_MODEL, XA_WIDTH), D_MODEL ** -0.5),
        'w_xo': nrm((DEPTH, XA_WIDTH, D_MODEL), XA_WIDTH ** -0.5),
        'g_ffn': gain((DEPTH, D_MODEL)),
        'w_up': nrm((DEPTH, D_MODEL, 2 * D_FF), D_MODEL ** -0.5),
        'ffn_conv_w': nrm((DEPTH, FFN_CONV_W, 2 * D_FF), FFN_CONV_W ** -0.5),
        'w_down': nrm((DEPTH, D_FF, D_MODEL), D_FF ** -0.5),
        'g_final': gain((D_MODEL,)),
    }

def reference(x_prompt, x_sample, cache_k, cache_v, cache_mem_k, cache_mem_v, state_hgrn, state_conv,
              state_ffn, page_table, mem_prompt, g_mix, w_in, w_out, hg_lb_logits, hg_norm_g, conv_w,
              g_xattn, g_mem, w_xq, w_mk, w_mv, w_xo, g_ffn, w_up, ffn_conv_w, w_down, g_final):
    B, T = x_prompt.shape[0], x_prompt.shape[1]
    DB, S = x_sample.shape[0], x_sample.shape[1]
    past = page_table.shape[1] * cache_k.shape[2]
    pos_p = jnp.arange(T, dtype=jnp.int32)
    pos_s = past + jnp.arange(S, dtype=jnp.int32)
    lb_p = jax.nn.softmax(hg_lb_logits.astype(jnp.float32), axis=0)
    lower = jnp.cumsum(lb_p, axis=0) - lb_p[0:1]
    xp, xs = x_prompt, x_sample
    kp_l, vp_l, ks_l, vs_l, hp_l, hs_l, cp_l, cs_l, fp_l, fs_l, mk_l, mv_l = ([] for _ in range(12))
    for l in range(DEPTH):
        mix = (g_mix[l], w_in[l], w_out[l], lower[l], hg_norm_g[l], conv_w[l])
        xp, k1, v1, h1, c1 = mixer_layer(xp, pos_p, moba_prompt,
                                         jnp.zeros((B, HG_HEADS, HG_DK, HG_DV), jnp.float32),
                                         jnp.zeros((B, CONV_W - 1, CONV_CH), xp.dtype), *mix)
        mk, mv = memory_kv(mem_prompt, g_mem[l], w_mk[l], w_mv[l])
        xp = xp + cross_attn(xp, g_xattn[l], w_xq[l], w_xo[l], mk, mv)
        f1, fs1 = conv_ffn(xp, g_ffn[l], w_up[l], ffn_conv_w[l], w_down[l],
                           jnp.zeros((B, FFN_CONV_W - 1, 2 * D_FF), xp.dtype))
        xp = xp + f1
        k_past = cache_k[l][page_table].reshape(DB, past, KV_HEADS, HEAD_DIM)
        v_past = cache_v[l][page_table].reshape(DB, past, KV_HEADS, HEAD_DIM)
        attn_s = functools.partial(moba_sample, k_past=k_past, v_past=v_past)
        xs, k2, v2, h2, c2 = mixer_layer(xs, pos_s, attn_s, state_hgrn[l], state_conv[l], *mix)
        xs = xs + cross_attn(xs, g_xattn[l], w_xq[l], w_xo[l], cache_mem_k[l], cache_mem_v[l])
        f2, fs2 = conv_ffn(xs, g_ffn[l], w_up[l], ffn_conv_w[l], w_down[l], state_ffn[l])
        xs = xs + f2
        kp_l.append(k1); vp_l.append(v1); ks_l.append(k2); vs_l.append(v2)
        hp_l.append(h1); hs_l.append(h2); cp_l.append(c1); cs_l.append(c2)
        fp_l.append(fs1); fs_l.append(fs2); mk_l.append(mk); mv_l.append(mv)
    y_prompt = rmsnorm(xp, g_final)
    y_sample = rmsnorm(xs, g_final)
    return (y_prompt, y_sample,
            jnp.stack(kp_l), jnp.stack(vp_l), jnp.stack(ks_l), jnp.stack(vs_l),
            jnp.stack(hp_l), jnp.stack(hs_l), jnp.stack(cp_l), jnp.stack(cs_l),
            jnp.stack(fp_l), jnp.stack(fs_l), jnp.stack(mk_l), jnp.stack(mv_l))


_drawn_inputs = setup_inputs


def setup_inputs(seed=0):
    import zlib

    import numpy as np

    out = dict(_drawn_inputs(seed))
    spreads = {}
    factors = {'hg_norm_g': 6.758, 'g_xattn': 8.0, 'g_mem': 2.846, 'g_final': 9.552, 'g_ffn': 2.689}
    for name, (base, spread) in spreads.items():
        noise = np.random.default_rng([zlib.crc32(name.encode()), seed]).standard_normal(out[name].shape)
        drawn = base * np.exp(spread * noise) if base else spread * noise
        out[name] = __import__('jax').numpy.asarray(drawn.astype(out[name].dtype))
    for name, factor in factors.items():
        out[name] = (out[name] * factor).astype(out[name].dtype)
    return out
```

```python
from contextlib import ExitStack

import concourse.bass as bass
import numpy as np
from concourse import mybir

ALU = mybir.AluOpType
ACT = mybir.ActivationFunctionType
AX_X = mybir.AxisListType.X
F32 = mybir.dt.float32
I32 = mybir.dt.int32

P = 128
D_MODEL, SEQ, DEPTH = 1024, 256, 2
DEC_BATCH, DEC_SEQ, PAGE, N_PAGES = 8, 4, 128, 2
HD = 64
N_MEM = 256
D_FF = 2816
EPS = 1e-6
SCALE = HD ** -0.5
NS = DEC_BATCH * DEC_SEQ
N = SEQ + NS
KT_D = D_MODEL // P
FT = D_FF // P
UG = 4
UJ = 2 * FT // UG
BIG = 1e30

W_Q, W_K, W_V, W_HQ, W_HF, W_HI, W_HG, W_CB, W_CC, W_CH = (
    0, 512, 768, 1024, 1280, 1536, 1792, 2048, 2304, 2560)
IN_CHUNKS = [("hf", W_HF), ("hq", W_HQ), ("hi", W_HI), ("k", W_K), ("q0", W_Q), ("q1", W_Q + 256),
             ("v", W_V), ("cc", W_CC), ("ch", W_CH), ("cb", W_CB), ("hg", W_HG)]

CHUNKS = ([("in", n) for n in range(len(IN_CHUNKS))] + [("mk", 0), ("mv", 0)]
          + [("out", n) for n in range(4)] + [("xq", 0), ("xo", 0)]
          + [("up", n) for n in range(FT)] + [("down", n) for n in range(12)])
SLOTS = 4


def dmas_of(kind, i):
    if kind == "in" and IN_CHUNKS[i][0] in ("q0", "q1"):
        return 4
    return 5 if kind == "out" else 1


DOWN_K = [(0, 8), (8, 16), (16, 22)]

LEVELS = [1, 2, 4, 8, 16, 32, 64]

C_IDENT, C_PERM, C_ONES, C_BLK, C_COS, C_SIN = 0, 128, 256, 384, 512, 512 + N
C_MASKA = C_SIN + N
C_MASKS = C_MASKA + 384
C_SEL = C_MASKS + NS
C_N = C_SEL + DEC_BATCH
M_LEVEL = {m: P + 64 * i for i, m in enumerate(LEVELS)}
M_N = P + 64 * len(LEVELS)


def constants():
    f = np.zeros((P, C_N), np.float32)
    p = np.arange(P)
    f[:, C_IDENT:C_IDENT + P] = np.eye(P)
    half = HD // 2
    for d in range(P):
        if d % HD < half:
            f[d + half, C_PERM + d] = -1.0
        else:
            f[d - half, C_PERM + d] = 1.0
    f[:, C_ONES:C_ONES + P] = 1.0
    f[:, C_BLK:C_BLK + P] = (p[:, None] // HD == p[None, :] // HD)
    pos = np.concatenate([np.arange(SEQ), SEQ + np.tile(np.arange(DEC_SEQ), DEC_BATCH)]).astype(np.float32)
    inv = np.float32(10000.0) ** (-np.arange(half, dtype=np.float32) / np.float32(half))
    ang = (pos[None, :] * inv[p % half][:, None]).astype(np.float32).astype(np.float64)
    f[:, C_COS:C_COS + N] = np.cos(ang)
    f[:, C_SIN:C_SIN + N] = np.sin(ang)
    q = np.arange(P)[:, None]
    k = np.arange(P)[None, :]
    causal = np.where(k <= q, 0.0, -BIG)
    f[:, C_MASKA:C_MASKA + P] = causal
    f[:, C_MASKA + 2 * P:C_MASKA + 3 * P] = causal
    row = np.arange(P)[:, None]
    t = np.arange(NS)[None, :]
    f[:, C_MASKS:C_MASKS + NS] = np.where((t // 4 == row // 16) & (t % 4 <= row % 4), 0.0, -BIG)
    f[:NS, C_SEL:C_SEL + DEC_BATCH] = (np.arange(NS)[:, None] // 4 == np.arange(DEC_BATCH)[None, :])
    m = np.zeros((P, M_N), np.int32)
    m[:, :P] = np.eye(P)
    for h in LEVELS:
        c = np.arange(64)[None, :]
        s = np.arange(P)[:, None]
        m[:, M_LEVEL[h]:M_LEVEL[h] + 64] = (s // (2 * h) == c // h) & (s % (2 * h) < h)
    return f, m


R_MIX, R_XATTN, R_MEM, R_FFN, R_LB, R_NORM, R_CONV = 0, 8, 16, 24, 32, 34, 36
R_LAYER = 42
R_FINAL = DEPTH * R_LAYER


def layer_schedule(l):
    s = []

    def a(who, step, *args):
        s.append((step, args, who))

    def level(m):
        a("D", "level", m, 0)
        a("D", "level", m, 1)
        a("op", "merge", m)

    def scores(g):
        a("D", "as", g, 0)
        a("D", "as", g, 1)

    def turn_probs(g):
        a("op", "anorm", g)
        a("A", "at", g, 0)
        a("A", "at", g, 1)

    first = l == 0
    a("D", "in", "hf", 0)
    a("D", "in", "hf", 1)
    a("D", "ssq", 0)
    if first:
        a("op", "bounds")
    for b, (part, m) in enumerate([("hq", 0), ("hq", 1), ("hi", 0), ("hi", 1)]):
        a("D", "in", part, m)
        a("A", "turn_past", b)
    a("op", "gates")
    if first:
        a("op", "mem_rms")
    a("D", "in", "k", 0)
    for t in range(3):
        a("A", "turn_hi", t)
    a("D", "in", "k", 1)
    for i in (0, 1):
        a("D", "diag", i)
    for i in (0, 1):
        a("D", "diag_s", i)
    a("D", "in", "q0", 0)
    a("A", "turn_past", 4)
    a("D", "in", "q0", 1)
    a("D", "rope", "k", 0)
    a("D", "rope", "k", 1)
    level(1)
    a("D", "in", "q1", 0)
    a("A", "turn_past", 5)
    for t in range(3):
        a("A", "turn_k", t)
    a("D", "in", "q1", 1)
    a("D", "rope", "q", 0)
    a("D", "rope", "q", 1)
    level(2)
    a("D", "in", "v", 0)
    a("D", "rope", "q", 2)
    a("A", "turn_past", 6)
    a("D", "in", "v", 1)
    a("D", "rope", "q", 3)
    level(4)
    a("D", "cstate_in")
    a("D", "in", "cc", 0)
    for t in range(3):
        a("A", "turn_v", t)
    scores(0)
    a("A", "turn_past", 7)
    if first:
        for k in range(KT_D // 2):
            a("A", "turn_mem", k)
    a("D", "in", "cc", 1)
    level(8)
    a("D", "in", "ch", 0)
    turn_probs(0)
    a("D", "in", "ch", 1)
    scores(1)
    a("A", "ao", 0)
    if first:
        for k in range(KT_D // 2, KT_D):
            a("A", "turn_mem", k)
    level(16)
    a("D", "in", "cb", 0)
    turn_probs(1)
    a("D", "in", "cb", 1)
    scores(2)
    a("A", "ao", 1)
    level(32)
    a("D", "in", "hg", 0)
    turn_probs(2)
    a("D", "in", "hg", 1)
    scores(3)
    a("A", "ao", 2)
    level(64)
    a("op", "conv")
    a("A", "mk", 0)
    turn_probs(3)
    a("op", "sq", 0)
    a("D", "ss", 0)
    a("D", "cross", 0)
    a("D", "cross", 1)
    a("op", "merge", P)
    a("A", "mk", 1)
    a("A", "ao", 3)
    a("op", "snorm", 0)
    a("A", "st", 0)
    for t in range(3):
        a("A", "turn_ke", t)
    a("D", "ho", 0)
    a("D", "ho", 1)
    a("A", "mv", 0)
    a("op", "sq", 1)
    a("D", "ss", 1)
    a("D", "hn", 0)
    a("D", "hn", 1)
    a("A", "so", 0)
    a("A", "mv", 1)
    a("A", "hstate")
    a("op", "snorm", 1)
    a("A", "st", 1)
    a("A", "turn_mk", 0)
    a("A", "turn_mk", 1)
    a("D", "hstate_s", 0)
    a("D", "hstate_s", 1)
    a("A", "so", 1)
    for m in range(8):
        a("D", "out", m)
        a("A", "turn_cmem", m)
        if m == 0:
            a("A", "cstate_out")
    a("D", "xq", 0)
    a("D", "xq", 1)
    a("D", "ssq", 1)
    a("A", "ustate_in", 0)
    a("op", "yq")
    a("A", "xs", 0)
    a("A", "xs", 1)
    a("A", "ys")
    a("A", "ustate_in", 1)
    a("op", "xnorm", 0)
    a("A", "xt", 0)
    a("op", "xnorm", 1)
    a("A", "xt", 1)
    a("A", "xs", 2)
    a("op", "ynorm")
    a("A", "yt")
    a("A", "xov", 0)
    a("A", "xs", 3)
    a("A", "yo", 0)
    a("op", "xnorm", 2)
    a("A", "xt", 2)
    a("op", "xnorm", 3)
    a("A", "xt", 3)
    a("A", "yo", 1)
    a("A", "xov", 1)
    for m in range(8):
        a("D", "xo", m)
    for i in range(FT):
        a("D", "up", i, 0)
        a("D", "up", i, 1)
        if i == 0:
            a("D", "ssq", 2)
        if i:
            a("op", "gate", i - 1)
    a("op", "gate", FT - 1)
    for m in range(8):
        a("D", "down", m)
        if m < 3:
            a("A", "ustate_out", m)
    return s


def emptied_order(steps):
    out = []
    for step in steps:
        at = len(out)
        if step[1] == "ssq" and step[0] < DEPTH:
            while out[at - 1][1] in ("in", "xq", "up"):
                at -= 1
        out.insert(at, step)
    return out


PROLOGUE = [("turn_x", (k,), "D") for k in range(KT_D)] + [("par", (), "D"), ("fpar", (), "D")]
EPILOGUE = [("ssq", (3,), "D")] + [("y", (t, h), "A") for t in range(3) for h in range(2)]


class Banks:

    def __init__(self):
        self.steps = [(-1, *x) for x in PROLOGUE]
        for l in range(DEPTH):
            self.steps += [(l, *x) for x in layer_schedule(l)]
        self.steps += [(DEPTH, *x) for x in EPILOGUE]
        self.emptying_steps = emptied_order(self.steps)
        fills = [x for x in self.steps if x[3] != "op"]
        self.of = {x[:3]: n for n, x in enumerate(fills)}
        emptied = {}
        for who, steps in (("A", self.steps), ("D", self.emptying_steps)):
            own = [x for x in steps if x[3] == who]
            emptied.update({x[:3]: (who, n + 1) for n, x in enumerate(own)})
        self.before = [emptied[x[:3]] for x in fills]


def decoder_kernel(nc, a, out):
    (y_prompt, y_sample, k_prompt, v_prompt, k_sample, v_sample, hgrn_prompt, hgrn_sample,
     conv_prompt, conv_sample, ffn_prompt, ffn_sample, mem_k_prompt, mem_v_prompt) = out
    banks = Banks()
    with ExitStack() as ctx:
        def sb(name, *shape, dt=F32):
            return ctx.enter_context(nc.sbuf_tensor(name, list(shape), dt))

        def sem(name):
            return ctx.enter_context(nc.semaphore(name))

        ps = ctx.enter_context(nc.psum_tensor("banks", [P, 8, 512], F32))
        con = sb("con", P, C_N)
        mask = sb("mask", P, M_N, dt=I32)
        pages = sb("pages", 1, DEC_BATCH * N_PAGES, dt=I32)
        X = sb("X", P, KT_D, N)
        XG = sb("XG", P, KT_D, N)
        acc = sb("acc", P, N)
        sqr = sb("sqr", P, N)
        ring = sb("ring", P, SLOTS, 2048)
        rawk = sb("rawk", P, 2, 2, 256)
        keysT = sb("keysT", P, 2, DEC_BATCH, 256)
        vals = sb("vals", P, DEC_BATCH, 2, 256)
        memT = sb("memT", P, KT_D, N_MEM)
        mkT = sb("mkT", P, 2, N_MEM)
        mv = sb("mv", P, 2, 256)
        mix = sb("mix", P, KT_D, N)
        par = sb("par", P, DEPTH * R_LAYER + 8)
        fpar = sb("fpar", P, DEPTH * 3, 2 * FT)
        Rn = sb("Rn", P, N)
        vv = sb("vv", P, N)
        ln = sb("ln", P, N)
        small = sb("small", P, 96)
        ustr = sb("ustr", UG * 16, UJ * P)
        ust = sb("ust", P, UJ, UG, 16)
        phase = sb("phase", P, 18600)
        used = [0]

        def ph(*shape, parts=P):
            n = int(np.prod(shape))
            v = phase[0:parts, used[0]:used[0] + n]
            used[0] += n
            assert used[0] <= 18600, used[0]
            if len(shape) > 1:
                names = "abcd"[:len(shape)]
                v = v.rearrange(f"p ({' '.join(names)}) -> p {' '.join(names)}", **dict(zip(names, shape)))
            return v

        prob = ph(2, 512)
        probT = ph(2, 512)
        qT = ph(4, N)
        kT = ph(2, N)
        sc = ph(2, 6, P)
        scs = ph(2, 2, NS)
        hf = ph(2, N)
        hq = ph(2, N)
        hk = ph(2, N)
        hi = ph(2, N)
        hgs = ph(2, N)
        e1 = ph(2, N)
        e2 = ph(2, N)
        vh = ph(3, 256)
        vn = ph(3, 256)
        turned = ph(3, 256)
        ke = ph(3, 256)
        s0 = ph(2, 8, HD)
        cb = ph(2, N)
        uc = ph(2, 306)
        yc = ph(2, 306)
        qs = ph(8 * 144)
        qa = ph(P)
        probs = ph(N)
        probsT = ph(384)
        hsp = ph(2, HD)
        cst = probsT[0:16, 0:256]
        cvo = ph(256, parts=18)
        mko = ph(2, 256)
        vt = prob.rearrange("p i n -> p (i n)")[:, 0:2 * N].rearrange("p (k n) -> p k n", k=2)
        clast = ph(2, 18)
        t4 = ph(2, 8)
        used[0] = 0
        hT = ph(FT, N)
        uab = [[ph(306), ph(306)] for _ in range(2)]
        yab = [[ph(306), ph(306)] for _ in range(2)]
        sil = [ph(306) for _ in range(2)]
        ulast = ph(UJ, UG, 18)
        ulo = ph(UJ * P, parts=UG * 18)
        used[0] = 0
        yrow = ph(3, D_MODEL)
        used[0] = 0
        xin = ph(2, D_MODEL)
        xsin = ph(D_MODEL, parts=NS)
        rows = ph(P, parts=DEPTH * R_LAYER + 8)
        frows = ph(DEPTH * 3, P, parts=2 * FT)
        memin = mix[:].rearrange("p k n -> p (k n)")[:, 0:2 * D_MODEL].rearrange("p (t d) -> p t d", t=2)
        mg = XG[:, :, 0:N_MEM]
        vexp = XG[0:NS].rearrange("p k n -> p (k n)")[:, 0:2048].rearrange("p (h b v) -> p h b v", h=4, b=8)
        newS = sb("newS", P, 2, 8, HD)

        ident = con[:, C_IDENT:C_IDENT + P]
        perm = con[:, C_PERM:C_PERM + P]
        ones = con[:, C_ONES:C_ONES + P]
        blk = con[:, C_BLK:C_BLK + P]

        filled = sem("filled")
        emptied = {"A": sem("emptied_by_act"), "D": sem("emptied_by_dve")}
        loaded = [sem(f"loaded{i}") for i in range(SLOTS)]
        x_in = sem("x_in")
        par_in = sem("par_in")
        fpar_in = sem("fpar_in")
        con_in = sem("con_in")
        mem_in = sem("mem_in")
        rawk_in = [sem("rawk0_in"), sem("rawk1_in")]
        vals_in = sem("vals_in")
        s0_in = sem("s0_in")
        cstate_in = sem("cstate_in")
        ustate_in = sem("ustate_in")
        pages_in = sem("pages_in")
        stored = sem("stored")
        s = {n: sem(n) for n in (
            "sumsq", "xg_tile", "mg_ready", "rms_guess", "sigmoids", "gates_ready", "silu_gate_in",
            "h_level", "roped", "conv_done", "att_max", "att_exp", "att_p", "s_q", "s_max", "s_exp", "s_p",
            "zeros", "vexp_ready", "h_square", "h_out", "news_ready", "y_q", "y_max", "y_p", "x_max", "x_p",
            "u_pads", "u_c0", "u_ya", "u_silu", "u_last", "h_tile", "mem_square", "mem_v", "mem_guess",
            "mem_scaled", "lb_d", "lb_exp", "lb_ready", "y_tile")}
        block = ctx.enter_context(nc.Block())

        dma_count = {}
        total = [0] * SLOTS
        for l in range(DEPTH):
            for n, (kind, i) in enumerate(CHUNKS):
                slot = (l * len(CHUNKS) + n) % SLOTS
                total[slot] += 16 * dmas_of(kind, i)
                dma_count[l, n] = total[slot]
        index = {c: n for n, c in enumerate(CHUNKS)}

        def fill_no(l, step, *args):
            return banks.of[l, step, args] + 1

        def pe_done(eng, l, step, *args):
            eng.wait_ge(filled, fill_no(l, step, *args))

        def wait_emptied(eng, l, step, *args):
            who, count = banks.before[banks.of[l, step, args]]
            eng.wait_ge(emptied[who], count)

        def bank(l, step, *args):
            return ps[:, banks.of[l, step, args] % 8, :]

        def last_use(l, n):
            kind, i = CHUNKS[n]
            if kind == "in":
                return fill_no(l, "in", IN_CHUNKS[i][0], 1)
            if kind in ("out",):
                return fill_no(l, "out", 2 * i + 1)
            if kind == "xo":
                return fill_no(l, "xo", 7)
            if kind == "up":
                return fill_no(l, "up", i // 2 * 2 + 1, i % 2)
            if kind == "down":
                return fill_no(l, "down", i // 3 * 2 + 1)
            return fill_no(l, kind, 1)

        STORES_MIXER = 2 + 2 + 2 + 2 + 2 + 4
        STORES_LAYER = STORES_MIXER + 2 * UG

        @block.sync
        def _(sp):
            sp.dma_start(con[:, 0:C_BLK], a["const_f"][:, 0:C_BLK]).then_inc(x_in, 16)
            sp.dma_start(xin[:, 0], a["x_prompt"][0, 0:P]).then_inc(x_in, 16)
            sp.dma_start(xsin, a["x_sample"].rearrange("b s d -> (b s) d")).then_inc(x_in, 16)
            for l in range(DEPTH):
                for n, (kind, i) in enumerate(CHUNKS):
                    g = l * len(CHUNKS) + n
                    slot = ring[:, g % SLOTS]
                    if g >= SLOTS:
                        sp.wait_ge(filled, last_use(*divmod(g - SLOTS, len(CHUNKS))))
                    got = loaded[g % SLOTS]

                    def load(src, dst=slot.rearrange("p (k c) -> p k c", c=256)):
                        sp.dma_start(dst, src).then_inc(got, 16)

                    if kind == "in":
                        c0 = IN_CHUNKS[i][1]
                        w = a["w_in"][l][:, c0:c0 + 256].rearrange("(k p) c -> p k c", p=P)
                        if IN_CHUNKS[i][0] in ("q0", "q1"):
                            dst = slot.rearrange("p (k c) -> p k c", c=256)
                            for g in range(2):
                                for half in range(2):
                                    c, d = (2 * half + g) * HD, (2 * g + half) * HD
                                    load(w[:, :, c:c + HD], dst[:, :, d:d + HD])
                        else:
                            load(w)
                    elif kind in ("mk", "mv", "xq"):
                        load(a["w_" + kind][l].rearrange("(k p) c -> p k c", p=P))
                    elif kind == "out":
                        w = a["w_out"][l][:, 256 * i:256 * i + 256]
                        dst = slot.rearrange("p (k c) -> p k c", c=256)
                        heads = w[0:512].rearrange("(p i g d) c -> p i d g c", p=2, i=2, g=2)
                        for p in range(2):
                            for half in range(2):
                                load(heads[p, half], dst[64 * half:64 * half + 64, 2 * p:2 * p + 2])
                        load(w[512:1024].rearrange("(k p) c -> p k c", p=P), dst[:, 4:8])
                    elif kind == "xo":
                        load(a["w_xo"][l].rearrange("(k p) c -> p k c", p=P), slot.rearrange("p (k c) -> p k c", k=2))
                    elif kind == "up":
                        c0 = (i % 2) * D_FF + (i // 2) * 256
                        load(a["w_up"][l][:, c0:c0 + 256].rearrange("(k p) c -> p k c", p=P))
                    else:
                        k0, k1 = DOWN_K[i % 3]
                        c0 = 256 * (i // 3)
                        load(a["w_down"][l][P * k0:P * k1, c0:c0 + 256].rearrange("(k p) c -> p k c", p=P),
                             slot.rearrange("p (k c) -> p k c", c=256)[:, 0:k1 - k0])

        @block.gpsimd
        def _(pool):
            g_ = nc.gpsimd
            rawk_use = [0, 0]

            def load_rawk(l, n):
                b, half = n % 8, n % 2
                if n >= 2:
                    pe_done(pool, l, *(("turn_past", n - 2) if n - 2 < 8 else ("turn_cmem", n - 10)))
                elif l:
                    pe_done(pool, l - 1, "turn_cmem", 6 + n)
                if n < 8:
                    for j in range(N_PAGES):
                        page = pool.value_load(pages[0:1, b * N_PAGES + j:b * N_PAGES + j + 1],
                                               min_val=0, max_val=a["cache_k"].shape[1] - 1)
                        src = a["cache_k"][l][bass.ds(page, 1)].rearrange("a r h d -> r (a h d)")
                        pool.dma_start(rawk[:, half, j], src).then_inc(rawk_in[half], 16)
                else:
                    src = a["cache_mem_k"][l, b].rearrange("(t p) h d -> p t (h d)", p=P)
                    pool.dma_start(rawk[:, half], src).then_inc(rawk_in[half], 16)

            def layer_loads(l):
                load_rawk(l, 0)
                load_rawk(l, 1)
                if l:
                    pe_done(pool, l - 1, "yo", 1)
                for i in range(DEC_BATCH * N_PAGES):
                    page = pool.value_load(pages[0:1, i:i + 1], min_val=0, max_val=a["cache_v"].shape[1] - 1)
                    src = a["cache_v"][l][bass.ds(page, 1)].rearrange("a r h d -> r (a h d)")
                    pool.dma_start(vals[:, i // N_PAGES, i % N_PAGES], src).then_inc(vals_in, 16)
                for g in range(UG):
                    src = a["state_ffn"][l].rearrange("b w f -> (b w) f")[:, g * UJ * P:(g + 1) * UJ * P]
                    pool.dma_start(ustr[16 * g:16 * g + 16], src).then_inc(ustate_in, 16)

            def store(dst, src):
                pool.dma_start(dst, src).then_inc(stored, 16)

            pool.dma_start(pages[:], a["page_table"].rearrange("b n -> (b n)").rearrange("(a n) -> a n", a=1)).then_inc(pages_in, 16)
            pool.wait_ge(pages_in, 16)
            layer_loads(0)
            for l, step, args, who in banks.steps:
                if l < 0:
                    continue
                if (step, args) == ("ssq", (0,)):
                    pe_done(pool, l, "ssq", 0)
                    if l:
                        pool.wait_ge(stored, 16 * l * STORES_LAYER)
                    for h in range(4):
                        pool.dma_start(s0[64 * (h % 2):64 * (h % 2) + 64, h // 2],
                                       a["state_hgrn"][l][:, h].rearrange("b d v -> d b v")).then_inc(s0_in, 16)
                    pool.dma_start(cst, a["state_conv"][l].rearrange("b w c -> (b w) c")).then_inc(cstate_in, 16)
                    g_.memset(sc, 0.0)
                    g_.memset(scs[0:NS], 0.0)
                    g_.memset(qs, 0.0)
                    g_.memset(qa, 0.0).then_inc(s["zeros"], 1)
                elif (step, args) == ("turn_k", (2,)):
                    wait_emptied(pool, l, "turn_k", 2)
                    store(k_prompt[l, 0].rearrange("(t p) h d -> p t (h d)", p=P), turned[:, 0:2])
                    store(k_sample[l].rearrange("b s h d -> (b s) (h d)"), turned[0:NS, 2])
                elif (step, args) == ("turn_v", (2,)):
                    wait_emptied(pool, l, "turn_v", 2)
                    store(v_prompt[l, 0].rearrange("(t p) h d -> p t (h d)", p=P), vn[:, 0:2])
                    store(v_sample[l].rearrange("b s h d -> (b s) (h d)"), vn[0:NS, 2])
                elif (step, args) == ("in", ("hg", 1)):
                    pe_done(pool, l, "in", "hg", 1)
                    for k in range(KT_D):
                        c = l * R_LAYER + R_MEM + k
                        if l == 0 and k == 0:
                            wait_emptied(pool, -1, "par")
                            wait_emptied(pool, 0, "turn_mem", KT_D - 1)
                        last = g_.tensor_scalar(mg[:, k], memT[:, k], par[:, c:c + 1], None, ALU.mult)
                    last.then_inc(s["mg_ready"], 1)
                elif (step, args) == ("turn_mk", (1,)):
                    wait_emptied(pool, l, "turn_mk", 1)
                    store(mem_k_prompt[l, 0].rearrange("(t p) h d -> p t (h d)", p=P), mko)
                    store(mem_v_prompt[l, 0].rearrange("(t p) h d -> p t (h d)", p=P), mv[:])
                    wait_emptied(pool, l, "turn_hi", 2)
                    pool.wait_ge(con_in, 32)
                    pool.drain()
                    for h in range(4):
                        last = g_.tensor_tensor(
                            vexp[:, h], vh[0:NS, 2, h * HD:(h + 1) * HD].unsqueeze(1).broadcast_to([NS, 8, HD]),
                            con[0:NS, C_SEL:C_SEL + 8].unsqueeze(2).broadcast_to([NS, 8, HD]), ALU.mult)
                    last.then_inc(s["vexp_ready"], 1)
                elif step == "turn_past":
                    if args[0] < 8:
                        load_rawk(l, args[0] + 2)
                elif step == "turn_cmem" and args[0] < 6:
                    load_rawk(l, args[0] + 10)
                elif step == "cstate_out":
                    wait_emptied(pool, l, "cstate_out")
                    store(conv_prompt[l, 0], cvo[0:2])
                    store(conv_sample[l].rearrange("b w c -> (b w) c"), cvo[2:18])
                elif step == "sq":
                    p = args[0]
                    if p:
                        pe_done(pool, l, "ss", 0)
                    else:
                        pool.wait_ge(s["zeros"], l + 1)
                    pool.wait_ge(s["roped"], 6 * l + 6)
                    pool.drain()
                    for i in (0, 1):
                        rows_i = slice(64 * i, 64 * i + 64)
                        src = qT[rows_i, 2 * p:2 * p + 2, SEQ:N].rearrange("p g (b s) -> p b g s", b=8)
                        dst = qs[rows_i].rearrange("p (b x) -> p b x", x=144)[:, :, 8 * i:8 * i + 8]
                        g_.tensor_copy(dst.rearrange("p b (g s) -> p b g s", g=2), src)
                        dst = qa[rows_i].rearrange("p (b x) -> p b x", x=16)[:, :, 8 * i:8 * i + 8]
                        last = g_.tensor_copy(dst.rearrange("p b (g s) -> p b g s", g=2), src)
                    last.then_inc(s["s_q"], 1)
                elif (step, args) == ("so", (1,)):
                    pe_done(pool, l, "so", 1)
                    for b in range(DEC_BATCH):
                        src = a["cache_mem_v"][l, b].rearrange("(t p) h d -> p t (h d)", p=P)
                        pool.dma_start(vals[:, b], src).then_inc(vals_in, 16)
                elif step == "hstate":
                    wait_emptied(pool, l, "hstate")
                    for i in (0, 1):
                        store(hgrn_prompt[l, 0].rearrange("(k i) d v -> i d k v", k=2)[i], hsp[64 * i:64 * i + 64])
                elif (step, args) == ("hstate_s", (1,)):
                    wait_emptied(pool, l, "hstate_s", 1)
                    for h in range(4):
                        store(hgrn_sample[l][:, h].rearrange("b d v -> d b v"), newS[64 * (h % 2):64 * (h % 2) + 64, h // 2])
                elif step == "yq":
                    pe_done(pool, l, "ss", 1)
                    g_.memset(qs, 0.0)
                    wait_emptied(pool, l, "xq", 1)
                    pool.drain()
                    for p in (0, 1):
                        for i in (0, 1):
                            rows_i = slice(64 * i, 64 * i + 64)
                            src = qT[rows_i, p, SEQ:N].rearrange("p (b s) -> p b s", b=8)
                            dst = qs[rows_i, 576 * p:576 * p + 576].rearrange("p (b x) -> p b x", x=72)[:, :, 4 * i:4 * i + 4]
                            last = g_.tensor_copy(dst, src)
                    last.then_inc(s["y_q"], 1)
                elif step == "up":
                    i, ab = args
                    n = 2 * FT * l + 2 * i + ab
                    u = uab[i % 2][ab]
                    if (i, ab) == (0, 0):
                        pe_done(pool, l, "ssq", 2)
                        pool.wait_ge(stored, 16 * (l * STORES_LAYER + STORES_MIXER))
                        wait_emptied(pool, l, "ustate_in", 1)
                    if i >= 2:
                        pool.wait_ge(s["h_tile"], FT * l + i - 1)
                        pool.wait_ge(s["u_c0"], n - 3)
                    g, j = divmod(FT * ab + i, UJ)
                    g_.memset(u[:, 0:2], 0.0)
                    g_.tensor_copy(u[:, 258:306].rearrange("p (b x) -> p b x", x=6)[:, :, 0:2],
                                   ust[:, j, g].rearrange("p (b w) -> p b w", w=2)).then_inc(s["u_pads"], 1)
                    wait_emptied(pool, l, "up", i, ab)
                    g_.tensor_copy(ulast[:, j, g, 0:2], u[:, 256:258])
                    g_.tensor_copy(ulast[:, j, g, 2:18].rearrange("p (b w) -> p b w", w=2),
                                   u[:, 258:306].rearrange("p (b x) -> p b x", x=6)[:, :, 4:6]).then_inc(s["u_last"], 1)
                    if (i, ab) == (1, 1) and l + 1 < DEPTH:
                        layer_loads(l + 1)
                elif (step, args) == ("ustate_out", (2,)):
                    wait_emptied(pool, l, "ustate_out", 2)
                    for g in range(UG):
                        cols = slice(g * UJ * P, (g + 1) * UJ * P)
                        store(ffn_prompt[l, 0][:, cols], ulo[18 * g:18 * g + 2])
                        store(ffn_sample[l].rearrange("b w f -> (b w) f")[:, cols], ulo[18 * g + 2:18 * g + 18])
                elif (step, args) == ("y", (2, 1)):
                    wait_emptied(pool, l, "y", 2, 1)
                    store(y_prompt[0].rearrange("(t p) d -> p t d", p=P), yrow[:, 0:2])
                    store(y_sample.rearrange("b s d -> (b s) d"), yrow[0:NS, 2])
            pool.wait_ge(stored, 16 * (DEPTH * STORES_LAYER + 2))

        @block.scalar
        def _(act):
            ac = nc.scalar.activation
            act.dma_start(xin[:, 1], a["x_prompt"][0, P:SEQ]).then_inc(x_in, 16)
            for l in range(DEPTH):
                for r, name, k in ((R_MIX, "g_mix", 8), (R_XATTN, "g_xattn", 8), (R_MEM, "g_mem", 8),
                                   (R_FFN, "g_ffn", 8), (R_LB, "hg_lb_logits", 2), (R_NORM, "hg_norm_g", 2)):
                    r0 = l * R_LAYER + r
                    act.dma_start(rows[r0:r0 + k], a[name][l].rearrange("(k p) -> k p", p=P)).then_inc(par_in, 16)
                r0 = l * R_LAYER + R_CONV
                act.dma_start(rows[r0:r0 + 6], a["conv_w"][l].rearrange("w (k p) -> (w k) p", p=P)).then_inc(par_in, 16)
            act.dma_start(rows[R_FINAL:R_FINAL + 8], a["g_final"].rearrange("(k p) -> k p", p=P)).then_inc(par_in, 16)
            for l in range(DEPTH):
                act.dma_start(frows[:, 3 * l:3 * l + 3], a["ffn_conv_w"][l].rearrange("w (k p) -> k w p", p=P)).then_inc(fpar_in, 16)
            act.dma_start(con[:, C_BLK:], a["const_f"][:, C_BLK:]).then_inc(con_in, 16)
            act.dma_start(mask[:], a["const_i"]).then_inc(con_in, 16)
            act.dma_start(memin, a["mem_prompt"][0].rearrange("(t p) d -> p t d", p=P)).then_inc(mem_in, 16)

            def take(l, step, args, dst, src):
                act.wait_ge(filled, fill_no(l, step, *args))
                return nc.scalar.copy(dst, src)

            def guess(src_ready, count):
                ac(ln[:], vv[:], ACT.Ln)
                act.drain()
                ac(Rn[:], ln[:], ACT.Exp, scale=-0.5).then_inc(s["rms_guess"], 1)

            def gained(l, stage):
                for k in range(KT_D):
                    if l == 0 and stage == 0:
                        wait_emptied(act, -1, "turn_x", k)
                    else:
                        before = (l, ("", "out", "xo")[stage]) if stage else (l - 1, "down")
                        wait_emptied(act, *before, k)
                    c = l * R_LAYER + (R_MIX, R_XATTN, R_FFN)[stage] + k
                    ac(XG[:, k], X[:, k], ACT.Identity, scale=par[:, c:c + 1]).then_inc(s["xg_tile"], 1)

            for l, step, args, who in banks.emptying_steps:
                if step == "par":
                    wait_emptied(act, l, "par")
                    gained(0, 0)
                elif step == "bounds":
                    act.wait_ge(s["lb_d"], 1)
                    ac(small[:, 8:12], small[:, 4:8], ACT.Exp).then_inc(s["lb_exp"], 1)
                elif step == "mem_rms":
                    act.wait_ge(mem_in, 16)
                    junk = keysT[:].rearrange("p k b n -> p (k b n)")
                    act.drain()
                    for t in (0, 1):
                        last = ac(junk[:, 3072:4096], memin[:, t], ACT.Square, accum_out=small[:, 80 + t:81 + t])
                        act.drain()
                    last.then_inc(s["mem_square"], 1)
                    act.wait_ge(s["mem_v"], 1)
                    ac(small[:, 84:86], small[:, 82:84], ACT.Ln)
                    act.drain()
                    ac(small[:, 86:88], small[:, 84:86], ACT.Exp, scale=-0.5).then_inc(s["mem_guess"], 1)
                elif step == "turn_mem":
                    take(l, step, args, memT[:, args[0]], bank(l, step, *args)[:, 0:N_MEM]).then_inc(emptied["A"], 1)
                elif step == "ssq" or step == "hn":
                    wait_emptied(act, l, step, *args)
                    guess(None, 0)
                elif step == "gates":
                    if l:
                        act.wait_ge(stored, 16 * l * STORES_LAYER)
                    wait_emptied(act, l, "in", "hf", 1)
                    ac(hf, e1, ACT.Sigmoid)
                    ac(hk, e1, ACT.Sigmoid, scale=-1.0)
                    wait_emptied(act, l, "in", "hq", 1)
                    ac(hq, e2, ACT.Sigmoid).then_inc(s["sigmoids"], 1)
                elif (step, args) == ("in", ("hg", 1)):
                    wait_emptied(act, l, "in", "hg", 1)
                    act.wait_ge(s["gates_ready"], l + 1)
                    ac(e1, hgs, ACT.Sigmoid).then_inc(s["silu_gate_in"], 1)
                elif step in ("turn_hi", "turn_k", "turn_v", "turn_ke"):
                    t = args[0]
                    n = P if t < 2 else NS
                    if step == "turn_k" and t == 0 and l:
                        pass
                    if step == "turn_ke" and t == 0:
                        pass
                    dst = {"turn_hi": vh, "turn_k": turned, "turn_v": vn, "turn_ke": ke}[step]
                    take(l, step, args, dst[0:n, t], bank(l, step, *args)[0:n, 0:256]).then_inc(emptied["A"], 1)
                elif step == "mk":
                    take(l, step, args, mkT[:, args[0]], bank(l, step, *args)[:, 0:N_MEM]).then_inc(emptied["A"], 1)
                elif step == "mv":
                    if l and args[0] == 0:
                        act.wait_ge(stored, 16 * l * STORES_LAYER)
                    take(l, step, args, mv[:, args[0]], bank(l, step, *args)[:, 0:256]).then_inc(emptied["A"], 1)
                elif step == "turn_mk":
                    take(l, step, args, mko[:, args[0]], bank(l, step, *args)[:, 0:256]).then_inc(emptied["A"], 1)
                elif step in ("turn_past", "turn_cmem"):
                    src = bank(l, step, *args).rearrange("p (k m) -> p k m", k=2)
                    take(l, step, args, keysT[:, :, args[0]], src).then_inc(emptied["A"], 1)
                elif step == "cstate_out":
                    take(l, step, args, cvo[0:18], bank(l, step)[0:18, 0:256]).then_inc(emptied["A"], 1)
                elif step == "ustate_in":
                    j0, j1 = ((0, 8), (8, UJ))[args[0]]
                    src = bank(l, step, *args)[:, 0:64 * (j1 - j0)].rearrange("p (j x) -> p j x", x=64)
                    take(l, step, args, ust[:, j0:j1].rearrange("p j g r -> p j (g r)"), src).then_inc(emptied["A"], 1)
                elif step == "as":
                    g, i = args
                    c = 16 + 16 * (g % 2) + 2 * i
                    act.wait_ge(s["att_max"], 8 * l + 2 * g + i + 1)
                    ac(prob[:, i, 0:P], prob[:, i, 0:P], ACT.Exp, bias=small[:, c + 4:c + 5], scale=SCALE,
                       accum_out=small[:, c + 8:c + 9])
                    ac(prob[:, i, P:384], prob[:, i, P:384], ACT.Exp, bias=small[:, c + 5:c + 6], scale=SCALE,
                       accum_out=small[:, c + 9:c + 10]).then_inc(s["att_exp"], 1)
                elif step == "at":
                    g, i = args
                    if g:
                        pe_done(act, l, "ao", g - 1)
                    take(l, step, args, probT[:, i, 0:384], bank(l, step, *args)[:, 0:384]).then_inc(emptied["A"], 1)
                elif step == "ao":
                    take(l, step, args, mix[:, args[0], 0:SEQ], bank(l, step, *args)[:, 0:SEQ]).then_inc(emptied["A"], 1)
                elif step == "ss":
                    act.wait_ge(s["s_max"], 2 * l + args[0] + 1)
                    ac(probs, probs, ACT.Exp, bias=small[:, 49:50], scale=SCALE,
                       accum_out=small[:, 50:51]).then_inc(s["s_exp"], 1)
                elif step == "st":
                    if args[0]:
                        pe_done(act, l, "so", 0)
                    b_ = bank(l, step, *args)
                    take(l, step, args, probsT[:, 0:256], b_[:, 0:256])
                    nc.scalar.copy(probsT[0:NS, 256:384], b_[0:NS, 256:384]).then_inc(emptied["A"], 1)
                elif step == "so":
                    p = args[0]
                    act.wait_ge(filled, fill_no(l, step, p))
                    for i in (0, 1):
                        rows_i = slice(64 * i, 64 * i + 64)
                        src = bank(l, step, p)[rows_i, 0:P].rearrange("p (b i g s) -> p i g b s", b=8, i=2, g=2)[:, i]
                        dst = mix[rows_i, 2 * p:2 * p + 2, SEQ:N].rearrange("p g (b s) -> p g b s", b=8)
                        last = nc.scalar.copy(dst, src)
                    last.then_inc(emptied["A"], 1)
                elif step == "hstate":
                    take(l, step, args, hsp.rearrange("p k v -> p (k v)"), bank(l, step)[:, 0:P]).then_inc(emptied["A"], 1)
                elif (step, args) in (("out", (7,)), ("xo", (7,))):
                    gained(l, 1 if step == "out" else 2)
                elif (step, args) == ("down", (7,)) and l + 1 < DEPTH:
                    gained(l + 1, 0)
                elif step == "ys":
                    act.wait_ge(s["y_max"], l + 1)
                    ac(probs[:, 0:256], bank(l, "ys")[:, 0:256], ACT.Exp, bias=small[:, 53:54], scale=SCALE,
                       accum_out=small[:, 54:55]).then_inc(emptied["A"], 1)
                elif step == "xs":
                    h = args[0]
                    c = 60 + 8 * (h % 2)
                    act.wait_ge(s["x_max"], 4 * l + h + 1)
                    if h >= 2:
                        pe_done(act, l, "xt", h - 2)
                    for q in (0, 1):
                        last = ac(prob[:, h % 2, 256 * q:256 * q + 256], bank(l, "xs", h)[:, 256 * q:256 * q + 256],
                                  ACT.Exp, bias=small[:, c + 2 + q:c + 3 + q], scale=SCALE,
                                  accum_out=small[:, c + 4 + q:c + 5 + q])
                    last.then_inc(emptied["A"], 1)
                elif step == "xt":
                    h = args[0]
                    if h >= 2:
                        pe_done(act, l, "xov", 0)
                    take(l, step, args, probT[:, h % 2], bank(l, step, h)).then_inc(emptied["A"], 1)
                elif step == "xov":
                    take(l, step, args, mix[:, args[0], 0:SEQ], bank(l, step, *args)[:, 0:SEQ]).then_inc(emptied["A"], 1)
                elif step == "yt":
                    take(l, step, args, probsT[:, 0:256], bank(l, step)[:, 0:256]).then_inc(emptied["A"], 1)
                elif step == "yo":
                    p = args[0]
                    act.wait_ge(filled, fill_no(l, step, p))
                    for i in (0, 1):
                        rows_i = slice(64 * i, 64 * i + 64)
                        src = bank(l, step, p)[rows_i, 0:64].rearrange("p (b i s) -> p i b s", b=8, i=2)[:, i]
                        dst = mix[rows_i, p, SEQ:N].rearrange("p (b s) -> p b s", b=8)
                        last = nc.scalar.copy(dst, src)
                    last.then_inc(emptied["A"], 1)
                elif step == "up":
                    i, ab = args
                    wait_emptied(act, l, "up", i, ab)
                    act.wait_ge(s["u_pads"], 2 * FT * l + 2 * i + ab + 1)
                    if i >= 2:
                        act.wait_ge(s["h_tile"], FT * l + i - 1)
                    c = FT * ab + i
                    ac(yab[i % 2][ab][:, 0:304], uab[i % 2][ab][:, 0:304], ACT.Identity,
                       scale=fpar[:, 3 * l, c:c + 1]).then_inc(s["u_c0"], 1)
                elif step == "gate":
                    i = args[0]
                    act.wait_ge(s["u_ya"], FT * l + i + 1)
                    ac(sil[i % 2][:, 0:304], yab[i % 2][0][:, 0:304], ACT.Silu).then_inc(s["u_silu"], 1)
                elif step == "ustate_out":
                    q = args[0]
                    n = P * (min(UJ, 4 * q + 4) - 4 * q)
                    take(l, step, args, ulo[0:UG * 18, 512 * q:512 * q + n],
                         bank(l, step, q)[0:UG * 18, 0:n]).then_inc(emptied["A"], 1)
                elif step == "y":
                    t, h = args
                    n = P if t < 2 else NS
                    if (t, h) == (0, 0):
                        act.wait_ge(stored, 16 * DEPTH * STORES_LAYER)
                    take(l, step, args, yrow[0:n, t, 512 * h:512 * h + 512], bank(l, step, t, h)[0:n]).then_inc(emptied["A"], 1)

        @block.tensor
        def _(pe):
            mm = nc.tensor.matmul
            tr = nc.tensor.transpose
            rawk_n = [0, 0]

            def chunk(l, kind, i, part=None):
                n = index[kind, i]
                g = l * len(CHUNKS) + n
                pe.wait_ge(loaded[g % SLOTS], dma_count[l, n])
                return ring[:, g % SLOTS].rearrange("p (k c) -> p k c", c=256)

            def xg(l, stage, k):
                pe.wait_ge(s["xg_tile"], 24 * l + 8 * stage + k + 1)
                return XG[:, k]

            def project(out_, w, cols, l, stage):
                for k in range(KT_D):
                    last = mm(out_[:, 0:N], w[:, k, cols], xg(l, stage, k), start=k == 0, stop=k == KT_D - 1)
                return last

            def turn(out_, src, n, parts=P):
                for m in (0, 1):
                    last = tr(out_[0:n, P * m:P * m + P], src[:, m], ident[:])
                return last

            fill = -1
            for l, step, args, who in banks.steps:
                if who == "op":
                    continue
                fill += 1
                if fill >= 8:
                    w_, count = banks.before[fill - 8]
                    pe.wait_ge(emptied[w_], count)
                o = ps[:, fill % 8, :]
                if step == "par":
                    pe.wait_ge(par_in, 16 * (7 * DEPTH + 1))
                    last = tr(o[:, 0:R_FINAL + 8], rows, ident[0:R_FINAL + 8, 0:R_FINAL + 8])
                elif step == "fpar":
                    pe.wait_ge(fpar_in, 16 * DEPTH)
                    for r in range(DEPTH * 3):
                        last = tr(o[:, 2 * FT * r:2 * FT * (r + 1)], frows[:, r], ident[0:2 * FT, 0:2 * FT])
                elif step == "turn_x":
                    k = args[0]
                    pe.wait_ge(x_in, 64)
                    for t in (0, 1):
                        tr(o[:, P * t:P * t + P], xin[:, t, P * k:P * k + P], ident[:])
                    last = tr(o[:, SEQ:N], xsin[0:NS, P * k:P * k + P], ident[0:NS, 0:NS])
                elif step == "turn_mem":
                    k = args[0]
                    pe.wait_ge(s["mem_scaled"], 1)
                    for t in (0, 1):
                        last = tr(o[:, P * t:P * t + P], memin[:, t, P * k:P * k + P], ident[:])
                elif step == "ssq":
                    pe.wait_ge(s["sumsq"], 3 * l + args[0] + 1 if l < DEPTH else 3 * DEPTH + 1)
                    last = mm(o[:, 0:N], ones, acc[:], start=True, stop=True)
                elif step == "in":
                    part, m = args
                    i = [c[0] for c in IN_CHUNKS].index(part)
                    w = chunk(l, "in", i)
                    last = project(o, w, slice(P * m, P * m + P), l, 0)
                elif step == "rope":
                    kind, m = args
                    src = kT[:, m] if kind == "k" else qT[:, m]
                    if kind == "k":
                        wait_emptied(pe, l, "in", "k", m)
                    else:
                        wait_emptied(pe, l, "in", f"q{m // 2}", m % 2)
                    last = mm(o[:, 0:N], perm, src, start=True, stop=True)
                elif step in ("turn_hi", "turn_k", "turn_v", "turn_ke"):
                    t = args[0]
                    cols = slice(P * t, P * t + P) if t < 2 else slice(SEQ, N)
                    n = P if t < 2 else NS
                    if step == "turn_hi":
                        wait_emptied(pe, l, "in", "hi", 1)
                        src = hi
                    elif step == "turn_k":
                        pe.wait_ge(s["roped"], 6 * l + 2)
                        src = kT
                    elif step == "turn_v":
                        wait_emptied(pe, l, "in", "v", 1)
                        src = vt
                    else:
                        pe.wait_ge(s["h_level"], 9 * l + 9)
                        src = hk
                    last = turn(o, src[:, :, cols], n)
                elif step == "cstate_in":
                    pe.wait_ge(cstate_in, 16 * (l + 1))
                    for m in (0, 1):
                        last = tr(o[:, 16 * m:16 * m + 16], cst[0:16, P * m:P * m + P], ident[0:16, 0:16])
                elif step == "cstate_out":
                    pe.wait_ge(s["conv_done"], l + 1)
                    for m in (0, 1):
                        last = tr(o[0:18, P * m:P * m + P], clast[:, m], ident[:])
                elif step == "mk":
                    m = args[0]
                    w = chunk(l, "mk", 0)
                    pe.wait_ge(s["mg_ready"], l + 1)
                    for k in range(KT_D):
                        last = mm(o[:, 0:N_MEM], w[:, k, P * m:P * m + P], mg[:, k], start=k == 0, stop=k == KT_D - 1)
                elif step == "mv":
                    t = args[0]
                    w = chunk(l, "mv", 0)
                    for k in range(KT_D):
                        last = mm(o[:, 0:256], mg[:, k, P * t:P * t + P], w[:, k], start=k == 0, stop=k == KT_D - 1)
                elif step == "turn_mk":
                    wait_emptied(pe, l, "mk", 1)
                    last = turn(o, mkT[:, :, P * args[0]:P * args[0] + P], P)
                elif step in ("turn_past", "turn_cmem"):
                    b = args[0]
                    rawk_n[b % 2] += 32 if step == "turn_past" else 16
                    pe.wait_ge(rawk_in[b % 2], rawk_n[b % 2])
                    for p in (0, 1):
                        for j in (0, 1):
                            last = tr(o[:, 256 * p + P * j:256 * p + P * j + P], rawk[:, b % 2, j, P * p:P * p + P], ident[:])
                elif step == "ustate_in":
                    if args[0] == 0:
                        pe.wait_ge(ustate_in, 16 * UG * (l + 1))
                    j0, j1 = ((0, 8), (8, UJ))[args[0]]
                    for j in range(j0, j1):
                        last = tr(o[:, 64 * (j - j0):64 * (j - j0) + 64], ustr[:, P * j:P * j + P], ident[0:64, 0:64])
                elif step == "as":
                    g, i = args
                    pe.wait_ge(s["roped"], 6 * l + 6)
                    r = slice(64 * i, 64 * i + 64)
                    mm(o[:, 0:P], qT[r, g, 0:P], kT[r, g // 2, 0:P], start=True, stop=True)
                    last = mm(o[:, P:384], qT[r, g, P:SEQ], kT[r, g // 2, 0:SEQ], start=True, stop=True)
                elif step == "at":
                    g, i = args
                    pe.wait_ge(s["att_p"], 4 * l + g + 1)
                    for j in range(3):
                        last = tr(o[:, P * j:P * j + P], prob[:, i, P * j:P * j + P], ident[:])
                elif step == "ao":
                    g = args[0]
                    wait_emptied(pe, l, "at", g, 1)
                    for i in (0, 1):
                        r = slice(64 * i, 64 * i + 64)
                        kv = slice((g // 2 * 2 + i) * HD, (g // 2 * 2 + i) * HD + HD)
                        mm(o[r, 0:P], vn[:, 0, kv], probT[:, i, 0:P], start=True, stop=True)
                        mm(o[r, P:SEQ], vn[:, 0, kv], probT[:, i, P:SEQ], start=True, stop=False)
                        last = mm(o[r, P:SEQ], vn[:, 1, kv], probT[:, i, SEQ:384], start=False, stop=True)
                elif step == "ss":
                    p = args[0]
                    pe.wait_ge(s["s_q"], 2 * l + p + 1)
                    wait_emptied(pe, l, "turn_past", 7)
                    mm(o[:, 256:N], qa, kT[:, p, SEQ:N], start=True, stop=True)
                    for b in range(8):
                        last = mm(o[:, 0:256], qs[:, P * b:P * b + P], keysT[:, p, b], start=b == 0, stop=b == 7)
                elif step == "st":
                    pe.wait_ge(s["s_p"], 2 * l + args[0] + 1)
                    for j in (0, 1):
                        tr(o[:, P * j:P * j + P], probs[:, P * j:P * j + P], ident[:])
                    last = tr(o[0:NS, 256:384], probs[:, 256:N], ident[:])
                elif step == "so":
                    p = args[0]
                    wait_emptied(pe, l, "st", p)
                    pe.wait_ge(vals_in, 16 * (24 * l + 16))
                    c = slice(P * p, P * p + P)
                    for b in range(8):
                        for j in (0, 1):
                            mm(o[:, 16 * b:16 * b + 16], vals[:, b, j, c], probsT[:, P * j + 16 * b:P * j + 16 * b + 16],
                               start=(b, j) == (0, 0), stop=False, skip_group_check=True)
                    last = mm(o[:, 0:P], vn[0:NS, 2, c], probsT[0:NS, 256:384], start=False, stop=True, skip_group_check=True)
                elif step in ("diag", "diag_s"):
                    i = args[0]
                    pe.wait_ge(s["gates_ready"], l + 1)
                    r = slice(64 * i, 64 * i + 64)
                    for t in (0, 1) if step == "diag" else (2,):
                        for p in (0, 1):
                            n, c = (P, slice(P * t, P * t + P)) if t < 2 else (NS, slice(SEQ, N))
                            at = P * (2 * t + p) if t < 2 else NS * p
                            last = mm(o[0:n, at:at + n], hk[r, p, c], hq[r, p, c], start=True, stop=True)
                elif step == "level":
                    m, i = args
                    pe.wait_ge(s["h_level"], 9 * l + LEVELS.index(m) + 1)
                    r = slice(64 * i, 64 * i + 64)
                    for t in (0, 1, 2) if m < DEC_SEQ else (0, 1):
                        for p in (0, 1):
                            n, c = (P, slice(P * t, P * t + P)) if t < 2 else (NS, slice(SEQ, N))
                            at = 64 * (2 * t + p) if t < 2 else 256 + NS // 2 * p
                            q = hq[r, p, c].rearrange("p (n two m) -> p n two m", two=2, m=m)[:, :, 1]
                            last = mm(o[0:n, at:at + n // 2], hk[r, p, c], q, start=True, stop=True)
                elif step == "cross":
                    pe.wait_ge(s["h_level"], 9 * l + 8)
                    r = slice(64 * args[0], 64 * args[0] + 64)
                    for p in (0, 1):
                        last = mm(o[:, P * p:P * p + P], hk[r, p, 0:P], hq[r, p, P:SEQ], start=True, stop=True)
                elif step == "hstate":
                    wait_emptied(pe, l, "turn_ke", 2)
                    for h in range(4):
                        r = slice(64 * (h % 2), 64 * (h % 2) + 64)
                        c = slice(HD * h, HD * h + HD)
                        for t in (0, 1):
                            last = mm(o[r, 64 * (h // 2):64 * (h // 2) + 64], ke[:, t, c], vh[:, t, c], start=t == 0, stop=t == 1)
                elif step == "hstate_s":
                    pe.wait_ge(s["vexp_ready"], l + 1)
                    for i in (0, 1):
                        h = 2 * args[0] + i
                        last = mm(o[64 * i:64 * i + 64, 0:512], ke[0:NS, 2, HD * h:HD * h + HD],
                                  vexp[:, h].rearrange("p b v -> p (b v)"), start=True, stop=True)
                elif step == "ho":
                    p = args[0]
                    wait_emptied(pe, l, "cross", 1)
                    pe.wait_ge(s0_in, 64 * (l + 1))
                    for i in (0, 1):
                        h = 2 * p + i
                        r = slice(64 * i, 64 * i + 64)
                        c = slice(HD * h, HD * h + HD)
                        mm(o[r, 0:P], vh[:, 0, c], sc[:, i, p], start=True, stop=True)
                        mm(o[r, P:SEQ], vh[:, 0, c], sc[:, i, 4 + p], start=True, stop=False)
                        mm(o[r, P:SEQ], vh[:, 1, c], sc[:, i, 2 + p], start=False, stop=True)
                        for b in range(8):
                            mm(o[r, SEQ + 4 * b:SEQ + 4 * b + 4], s0[r, p, b], hq[r, p, SEQ + 4 * b:SEQ + 4 * b + 4],
                               start=b == 0, stop=False, skip_group_check=True)
                        last = mm(o[r, SEQ:N], vh[0:NS, 2, c], scs[0:NS, i, p], start=False, stop=True, skip_group_check=True)
                elif step == "hn":
                    pe.wait_ge(s["h_square"], 2 * l + args[0] + 1)
                    last = mm(o[:, 0:N], blk, hi[:, args[0]], start=True, stop=True)
                elif step == "out":
                    m = args[0]
                    w = chunk(l, "out", m // 2)
                    wait_emptied(pe, l, "ao", 3)
                    wait_emptied(pe, l, "so", 1)
                    pe.wait_ge(s["conv_done"], l + 1)
                    pe.wait_ge(s["h_out"], 2 * l + 2)
                    c = slice(P * (m % 2), P * (m % 2) + P)
                    for k in range(KT_D):
                        last = mm(o[:, 0:N], w[:, k, c], mix[:, k], start=k == 0, stop=k == KT_D - 1)
                elif step == "xq":
                    last = project(o, chunk(l, "xq", 0), slice(P * args[0], P * args[0] + P), l, 1)
                elif step == "ys":
                    pe.wait_ge(s["y_q"], l + 1)
                    wait_emptied(pe, l, "turn_cmem", 7)
                    for p in (0, 1):
                        for b in range(8):
                            last = mm(o[64 * p:64 * p + 64, 0:256], qs[:, 576 * p + 64 * b:576 * p + 64 * b + 64], keysT[:, p, b],
                                      start=b == 0, stop=b == 7)
                elif step == "xs":
                    h = args[0]
                    wait_emptied(pe, l, "xq", 1)
                    r = slice(64 * (h % 2), 64 * (h % 2) + 64)
                    for q in (0, 1):
                        last = mm(o[:, 256 * q:256 * q + 256], qT[r, h // 2, P * q:P * q + P], mkT[r, h // 2], start=True, stop=True)
                elif step == "xt":
                    h = args[0]
                    pe.wait_ge(s["x_p"], 4 * l + h + 1)
                    for j in (0, 1):
                        for q in (0, 1):
                            last = tr(o[:, 256 * j + P * q:256 * j + P * q + P], prob[:, h % 2, 256 * q + P * j:256 * q + P * j + P], ident[:])
                elif step == "xov":
                    p = args[0]
                    wait_emptied(pe, l, "xt", 2 * p + 1)
                    for i in (0, 1):
                        c = slice(HD * (2 * p + i), HD * (2 * p + i) + HD)
                        for j in (0, 1):
                            last = mm(o[64 * i:64 * i + 64, 0:SEQ], mv[:, j, c], probT[:, i, 256 * j:256 * j + 256], start=j == 0, stop=j == 1)
                elif step == "yt":
                    pe.wait_ge(s["y_p"], l + 1)
                    for j in (0, 1):
                        last = tr(o[:, P * j:P * j + P], probs[:, P * j:P * j + P], ident[:])
                elif step == "yo":
                    p = args[0]
                    wait_emptied(pe, l, "yt")
                    pe.wait_ge(vals_in, 16 * 24 * (l + 1))
                    for b in range(8):
                        for j in (0, 1):
                            c = P * j + 64 * p + 8 * b
                            last = mm(o[:, 8 * b:8 * b + 8], vals[:, b, j, P * p:P * p + P], probsT[:, c:c + 8], start=j == 0, stop=j == 1)
                elif step == "xo":
                    m = args[0]
                    chunk(l, "xo", 0)
                    g = l * len(CHUNKS) + index["xo", 0]
                    w = ring[:, g % SLOTS].rearrange("p (k c) -> p k c", k=2)
                    wait_emptied(pe, l, "yo", 1)
                    wait_emptied(pe, l, "xov", 1)
                    for k in (0, 1):
                        last = mm(o[:, 0:N], w[:, k, P * m:P * m + P], mix[:, k], start=k == 0, stop=k == 1)
                elif step == "up":
                    i, ab = args
                    last = project(o, chunk(l, "up", i // 2 * 2 + ab), slice(P * (i % 2), P * (i % 2) + P), l, 2)
                elif step == "down":
                    m = args[0]
                    for c3, (k0, k1) in enumerate(DOWN_K):
                        w = chunk(l, "down", m // 2 * 3 + c3)
                        pe.wait_ge(s["h_tile"], FT * l + k1)
                        for k in range(k0, k1):
                            last = mm(o[:, 0:N], w[:, k - k0, P * (m % 2):P * (m % 2) + P], hT[:, k], start=k == 0, stop=k == FT - 1)
                elif step == "ustate_out":
                    pe.wait_ge(s["u_last"], 2 * FT * (l + 1))
                    for j in range(4 * args[0], min(UJ, 4 * args[0] + 4)):
                        jj = j - 4 * args[0]
                        last = tr(o[0:UG * 18, P * jj:P * jj + P], ulast[:, j].rearrange("p g r -> p (g r)"), ident[:])
                elif step == "y":
                    t, h = args
                    n = P if t < 2 else NS
                    cols = slice(P * t, P * t + P) if t < 2 else slice(SEQ, N)
                    pe.wait_ge(s["y_tile"], 4 * h + 4)
                    for k in range(4 * h, 4 * h + 4):
                        last = tr(o[0:n, P * (k - 4 * h):P * (k - 4 * h) + P], XG[:, k, cols], ident[:])
                else:
                    raise ValueError(step)
                last.then_inc(filled, 1)

        @block.vector
        def _(dve):
            v = nc.vector
            drain = dve.drain
            guesses = [0]

            def put(l, step, *args):
                dve.wait_ge(filled, fill_no(l, step, *args))
                return bank(l, step, *args)

            def squares(k, stage):
                drain()
                if k == 0:
                    v.tensor_tensor(acc[:], X[:, k], X[:, k], ALU.mult)
                else:
                    v.tensor_tensor(sqr[:], X[:, k], X[:, k], ALU.mult)
                    drain()
                    last = v.tensor_tensor(acc[:], acc[:], sqr[:], ALU.add)
                    if k == KT_D - 1:
                        last.then_inc(s["sumsq"], 1)

            def residual(l, step, m):
                b_ = put(l, step, m)
                v.tensor_tensor(X[:, m], X[:, m], b_[:, 0:N], ALU.add).then_inc(emptied["D"], 1)
                squares(m, 0)

            def newton(r, x, t):
                v.tensor_tensor(t, r, r, ALU.mult)
                drain()
                v.tensor_tensor(t, t, x, ALU.mult)
                drain()
                v.tensor_scalar(t, t, -0.5, 1.5, ALU.mult, ALU.add)
                drain()
                v.tensor_tensor(r, r, t, ALU.mult)
                drain()

            def rms(l, step, arg, width):
                b_ = put(l, step, arg)
                drain()
                v.tensor_scalar(vv[:], b_[:, 0:N], 1.0 / width, EPS, ALU.mult, ALU.add).then_inc(emptied["D"], 1)
                guesses[0] += 1
                dve.wait_ge(s["rms_guess"], guesses[0])
                newton(Rn[:], vv[:], sqr[:])

            def softmax_scale(rows_, c, tiles):
                pass

            def sampled(x):
                return x.rearrange("p (b s) -> p b s", b=8)

            def padded(x, at=258):
                return x[:, at:at + 48].rearrange("p (b x) -> p b x", x=6)

            for l, step, args, who in banks.emptying_steps:
                if step == "par":
                    v.tensor_copy(par[:], put(l, step)[:, 0:R_FINAL + 8]).then_inc(emptied["D"], 1)
                elif step == "fpar":
                    v.tensor_copy(fpar[:].rearrange("p a b -> p (a b)"),
                                  put(l, step)[:, 0:DEPTH * 3 * 2 * FT]).then_inc(emptied["D"], 1)
                elif step == "bounds":
                    drain()
                    l0 = par[:, R_LB:R_LB + 2]
                    l1 = par[:, R_LAYER + R_LB:R_LAYER + R_LB + 2]
                    v.tensor_tensor(small[:, 12:14], l0, l1, ALU.max)
                    drain()
                    v.tensor_tensor(small[:, 4:6], l0, small[:, 12:14], ALU.subtract)
                    v.tensor_tensor(small[:, 6:8], l1, small[:, 12:14], ALU.subtract).then_inc(s["lb_d"], 1)
                    dve.wait_ge(s["lb_exp"], 1)
                    v.tensor_tensor(small[:, 12:14], small[:, 8:10], small[:, 10:12], ALU.add)
                    drain()
                    v.reciprocal(small[:, 14:16], small[:, 12:14])
                    drain()
                    v.tensor_tensor(l1, small[:, 10:12], small[:, 14:16], ALU.mult)
                    v.memset(l0, 0.0)
                    drain()
                    v.memset(small[:, 0:2], 1.0)
                    v.tensor_scalar(small[:, 2:4], l1, -1.0, 1.0, ALU.mult, ALU.add)
                    drain()
                elif step == "mem_rms":
                    dve.wait_ge(s["mem_square"], 1)
                    v.tensor_scalar(small[:, 82:84], small[:, 80:82], 1.0 / D_MODEL, EPS, ALU.mult, ALU.add).then_inc(s["mem_v"], 1)
                    dve.wait_ge(s["mem_guess"], 1)
                    drain()
                    newton(small[:, 86:88], small[:, 82:84], small[:, 88:90])
                    for t in (0, 1):
                        last = v.tensor_scalar(memin[:, t], memin[:, t], small[:, 86 + t:87 + t], None, ALU.mult)
                    last.then_inc(s["mem_scaled"], 1)
                elif step == "turn_x":
                    k = args[0]
                    b_ = put(l, step, k)
                    v.tensor_copy(X[:, k], b_[:, 0:N]).then_inc(emptied["D"], 1)
                    squares(k, 0)
                elif step == "ssq":
                    if l and l < DEPTH and args[0] == 0:
                        dve.wait_ge(stored, 16 * l * STORES_LAYER)
                    if args[0] == 2:
                        dve.wait_ge(stored, 16 * (l * STORES_LAYER + STORES_MIXER))
                    rms(l, step, args[0], D_MODEL)
                    if args[0] == 3:
                        for k in range(KT_D):
                            c = R_FINAL + k
                            v.scalar_tensor_tensor(out=XG[:, k], in0=X[:, k], scalar=par[:, c:c + 1], in1=Rn[:],
                                                   op0=ALU.mult, op1=ALU.mult).then_inc(s["y_tile"], 1)
                elif step == "in":
                    part, m = args
                    b_ = put(l, step, *args)
                    dst = {"hf": e1, "hq": e2, "hi": hi, "k": kT, "q0": qT, "q1": qT[:, 2:4], "v": vt, "cc": yc,
                           "cb": cb, "hg": hgs}
                    if part == "ch":
                        v.tensor_tensor(sqr[:], b_[:, 0:N], Rn[:], ALU.mult).then_inc(emptied["D"], 1)
                        drain()
                        v.tensor_tensor(uc[:, m, 2:258], sqr[:, 0:SEQ], yc[:, m, 0:SEQ], ALU.mult)
                        v.tensor_tensor(padded(uc[:, m])[:, :, 2:6], sampled(sqr[:, SEQ:N]), sampled(yc[:, m, SEQ:N]), ALU.mult)
                        drain()
                    else:
                        v.tensor_tensor(dst[part][:, m, 0:N], b_[:, 0:N], Rn[:], ALU.mult).then_inc(emptied["D"], 1)
                elif step == "rope":
                    kind, m = args
                    x = kT[:, m] if kind == "k" else qT[:, m]
                    dve.wait_ge(con_in, 32)
                    b_ = put(l, step, *args)
                    v.tensor_tensor(sqr[:], b_[:, 0:N], con[:, C_SIN:C_SIN + N], ALU.mult).then_inc(emptied["D"], 1)
                    v.tensor_tensor(x, x, con[:, C_COS:C_COS + N], ALU.mult)
                    drain()
                    v.tensor_tensor(x, x, sqr[:], ALU.add).then_inc(s["roped"], 1)
                    drain()
                elif step == "gates":
                    dve.wait_ge(s["sigmoids"], l + 1)
                    for m in (0, 1):
                        lb = par[:, l * R_LAYER + R_LB + m:l * R_LAYER + R_LB + m + 1]
                        oml = small[:, 2 * l + m:2 * l + m + 1]
                        v.tensor_scalar(hf[:, m], hf[:, m], oml, lb, ALU.mult, ALU.add)
                        v.tensor_scalar(hk[:, m], hk[:, m], oml, None, ALU.mult)
                    v.tensor_tensor(hq, hq, e2, ALU.mult).then_inc(s["gates_ready"], 1)
                elif step == "cstate_in":
                    b_ = put(l, step)
                    v.memset(uc[:, :, 0:2], 0.0)
                    for m in (0, 1):
                        last = v.tensor_copy(padded(uc[:, m])[:, :, 0:2], b_[:, 16 * m:16 * m + 16].rearrange("p (b w) -> p b w", w=2))
                    last.then_inc(emptied["D"], 1)
                elif step == "conv":
                    drain()
                    c0 = l * R_LAYER + R_CONV
                    for m in (0, 1):
                        v.tensor_copy(clast[:, m, 0:2], uc[:, m, 256:258])
                        v.tensor_copy(clast[:, m, 2:18].rearrange("p (b w) -> p b w", w=2), padded(uc[:, m])[:, :, 4:6])
                        v.tensor_scalar(yc[:, m, 0:304], uc[:, m, 0:304], par[:, c0 + m:c0 + m + 1], None, ALU.mult)
                    for w in (1, 2):
                        drain()
                        for m in (0, 1):
                            c = c0 + 2 * w + m
                            v.scalar_tensor_tensor(out=yc[:, m, 0:304], in0=uc[:, m, w:304 + w], scalar=par[:, c:c + 1],
                                                   in1=yc[:, m, 0:304], op0=ALU.mult, op1=ALU.add)
                    drain()
                    for m in (0, 1):
                        v.tensor_tensor(mix[:, 6 + m, 0:SEQ], cb[:, m, 0:SEQ], yc[:, m, 0:SEQ], ALU.mult)
                        last = v.tensor_tensor(sampled(mix[:, 6 + m, SEQ:N]), sampled(cb[:, m, SEQ:N]),
                                               padded(yc[:, m], 258)[:, :, 0:4], ALU.mult)
                    last.then_inc(s["conv_done"], 1)
                elif step == "as":
                    g, i = args
                    b_ = put(l, step, g, i)
                    if g:
                        pe_done(dve, l, "at", g - 1, i)
                    c = 16 + 16 * (g % 2) + 2 * i
                    v.tensor_tensor(prob[:, i, 0:384], b_[:, 0:384], con[:, C_MASKA:C_MASKA + 384], ALU.add).then_inc(emptied["D"], 1)
                    drain()
                    v.tensor_reduce(small[:, c:c + 1], prob[:, i, 0:P], AX_X, ALU.max)
                    v.tensor_reduce(small[:, c + 1:c + 2], prob[:, i, P:384], AX_X, ALU.max)
                    drain()
                    v.tensor_scalar(small[:, c + 4:c + 6], small[:, c:c + 2], -SCALE, None, ALU.mult).then_inc(s["att_max"], 1)
                elif step == "anorm":
                    g = args[0]
                    c = 16 + 16 * (g % 2)
                    dve.wait_ge(s["att_exp"], 8 * l + 2 * g + 2)
                    v.reciprocal(small[:, c + 12:c + 16], small[:, c + 8:c + 12])
                    drain()
                    for i in (0, 1):
                        v.tensor_scalar(prob[:, i, 0:P], prob[:, i, 0:P], small[:, c + 12 + 2 * i:c + 13 + 2 * i], None, ALU.mult)
                        last = v.tensor_scalar(prob[:, i, P:384], prob[:, i, P:384], small[:, c + 13 + 2 * i:c + 14 + 2 * i], None, ALU.mult)
                    last.then_inc(s["att_p"], 1)
                elif step == "ss":
                    b_ = put(l, step, *args)
                    if args[0]:
                        pe_done(dve, l, "st", 0)
                    v.tensor_copy(probs[:, 0:256], b_[:, 0:256])
                    v.tensor_tensor(probs[:, 256:N], b_[:, 256:N], con[:, C_MASKS:C_MASKS + NS], ALU.add).then_inc(emptied["D"], 1)
                    drain()
                    v.tensor_reduce(small[:, 48:49], probs, AX_X, ALU.max)
                    drain()
                    v.tensor_scalar(small[:, 49:50], small[:, 48:49], -SCALE, None, ALU.mult).then_inc(s["s_max"], 1)
                elif step == "snorm":
                    dve.wait_ge(s["s_exp"], 2 * l + args[0] + 1)
                    v.reciprocal(small[:, 51:52], small[:, 50:51])
                    drain()
                    v.tensor_scalar(probs, probs, small[:, 51:52], None, ALU.mult).then_inc(s["s_p"], 1)
                elif step == "diag":
                    i = args[0]
                    b_ = put(l, step, i)
                    if i == 0:
                        dve.wait_ge(s["zeros"], l + 1)
                        dve.wait_ge(con_in, 32)
                    v.copy_predicated(sc[:, i, 0:4], mask[:, 0:P].unsqueeze(1).broadcast_to([P, 4, P]),
                                      b_.rearrange("p (x c) -> p x c", x=4)).then_inc(emptied["D"], 1)
                elif step == "diag_s":
                    i = args[0]
                    b_ = put(l, step, i)
                    v.copy_predicated(scs[0:NS, i], mask[0:NS, 0:NS].unsqueeze(1).broadcast_to([NS, 2, NS]),
                                      b_[0:NS, 0:2 * NS].rearrange("p (x c) -> p x c", x=2)).then_inc(emptied["D"], 1)
                    if i:
                        v.tensor_tensor(hq, hq, hf, ALU.mult).then_inc(s["h_level"], 1)
                elif step == "level":
                    m, i = args
                    b_ = put(l, step, m, i)
                    drain()

                    def place(dst, n, x, src):
                        dst = dst.rearrange("p (n two m) -> p n two m", two=2, m=m)[:, :, 1]
                        msk = mask[0:n, M_LEVEL[m]:M_LEVEL[m] + n // 2].unsqueeze(1).broadcast_to([n, x, n // 2])
                        return v.copy_predicated(dst.rearrange("p (x n) m -> p x n m", x=x),
                                                 msk.rearrange("p x (n m) -> p x n m", m=m),
                                                 src.rearrange("p (x n m) -> p x n m", x=x, m=m))
                    if m < DEC_SEQ:
                        place(scs[0:NS, i].rearrange("p x t -> p (x t)"), NS, 2, b_[0:NS, 256:256 + NS])
                    place(sc[:, i, 0:4].rearrange("p x t -> p (x t)"), P, 4, b_[:, 0:256]).then_inc(emptied["D"], 1)
                elif step == "merge":
                    m = args[0]
                    width = N if m < DEC_SEQ else SEQ
                    nb = width // m
                    odd = (LEVELS + [P]).index(m) % 2
                    tot, new = (e2, hf) if odd else (hf, e2)
                    drain()
                    pair = tot[:, :, 0:nb].rearrange("p k (n two) -> p k n two", two=2)
                    shape = [P, 2, nb // 2, m]
                    q = hq[:, :, 0:width].rearrange("p k (n two m) -> p k n two m", two=2, m=m)[:, :, :, 1]
                    k = hk[:, :, 0:width].rearrange("p k (n two m) -> p k n two m", two=2, m=m)[:, :, :, 0]
                    if m < P:
                        v.tensor_tensor(q, q, pair[:, :, :, 0:1].broadcast_to(shape), ALU.mult)
                        v.tensor_tensor(new[:, :, 0:nb // 2], pair[:, :, :, 0], pair[:, :, :, 1], ALU.mult)
                    v.tensor_tensor(k, k, pair[:, :, :, 1:2].broadcast_to(shape), ALU.mult).then_inc(s["h_level"], 1)
                    if m == DEC_SEQ // 2:
                        drain()
                        v.tensor_copy(t4, new[:, :, SEQ // 4:N // 4])
                elif step == "cross":
                    b_ = put(l, step, *args)
                    v.tensor_copy(sc[:, args[0], 4:6], b_[:, 0:256].rearrange("p (x c) -> p x c", x=2)).then_inc(emptied["D"], 1)
                elif step == "hstate_s":
                    k = args[0]
                    if k == 0:
                        dve.wait_ge(s0_in, 64 * (l + 1))
                        drain()
                    v.tensor_tensor(newS[:, k], s0[:, k], t4[:, k].unsqueeze(2).broadcast_to([P, 8, HD]), ALU.mult)
                    b_ = put(l, step, k)
                    drain()
                    v.tensor_tensor(newS[:, k], newS[:, k], b_.rearrange("p (b v) -> p b v", b=8), ALU.add).then_inc(emptied["D"], 1)
                elif step == "ho":
                    k = args[0]
                    b_ = put(l, step, k)
                    v.tensor_copy(e2[:, k], b_[:, 0:N]).then_inc(emptied["D"], 1)
                    drain()
                    v.tensor_tensor(hi[:, k], e2[:, k], e2[:, k], ALU.mult).then_inc(s["h_square"], 1)
                elif step == "hn":
                    k = args[0]
                    if k == 0:
                        dve.wait_ge(s["silu_gate_in"], l + 1)
                        v.tensor_tensor(hgs, hgs, e1, ALU.mult)
                    rms(l, step, k, HD)
                    v.tensor_tensor(e2[:, k], e2[:, k], Rn[:], ALU.mult)
                    drain()
                    c = l * R_LAYER + R_NORM + k
                    v.scalar_tensor_tensor(out=mix[:, 4 + k], in0=e2[:, k], scalar=par[:, c:c + 1], in1=hgs[:, k],
                                           op0=ALU.mult, op1=ALU.mult).then_inc(s["h_out"], 1)
                elif step in ("out", "xo", "down"):
                    residual(l, step, args[0])
                elif step == "xq":
                    b_ = put(l, step, *args)
                    v.tensor_tensor(qT[:, args[0]], b_[:, 0:N], Rn[:], ALU.mult).then_inc(emptied["D"], 1)
                elif step == "ys":
                    b_ = put(l, step)
                    v.tensor_reduce(small[:, 52:53], b_[:, 0:256], AX_X, ALU.max)
                    drain()
                    v.tensor_scalar(small[:, 53:54], small[:, 52:53], -SCALE, None, ALU.mult).then_inc(s["y_max"], 1)
                elif step == "ynorm":
                    wait_emptied(dve, l, "ys")
                    v.reciprocal(small[:, 55:56], small[:, 54:55])
                    drain()
                    v.tensor_scalar(probs[:, 0:256], probs[:, 0:256], small[:, 55:56], None, ALU.mult).then_inc(s["y_p"], 1)
                elif step == "xs":
                    h = args[0]
                    c = 60 + 8 * (h % 2)
                    b_ = put(l, step, h)
                    v.tensor_reduce(small[:, c:c + 2], b_.rearrange("p (q m) -> p q m", q=2), AX_X, ALU.max)
                    drain()
                    v.tensor_scalar(small[:, c + 2:c + 4], small[:, c:c + 2], -SCALE, None, ALU.mult).then_inc(s["x_max"], 1)
                elif step == "xnorm":
                    h = args[0]
                    c = 60 + 8 * (h % 2)
                    wait_emptied(dve, l, "xs", h)
                    v.reciprocal(small[:, c + 6:c + 8], small[:, c + 4:c + 6])
                    drain()
                    for q in (0, 1):
                        t = prob[:, h % 2, 256 * q:256 * q + 256]
                        last = v.tensor_scalar(t, t, small[:, c + 6 + q:c + 7 + q], None, ALU.mult)
                    last.then_inc(s["x_p"], 1)
                elif step == "up":
                    i, ab = args
                    b_ = put(l, step, i, ab)
                    u = uab[i % 2][ab]
                    if i >= 2:
                        dve.wait_ge(s["u_c0"], 2 * FT * l + 2 * i + ab - 3)
                        dve.wait_ge(s["u_last"], 2 * FT * l + 2 * i + ab - 3)
                    v.tensor_tensor(u[:, 2:258], b_[:, 0:SEQ], Rn[:, 0:SEQ], ALU.mult)
                    v.tensor_tensor(padded(u)[:, :, 2:6], sampled(b_[:, SEQ:N]), sampled(Rn[:, SEQ:N]), ALU.mult).then_inc(emptied["D"], 1)
                elif step == "gate":
                    i = args[0]
                    dve.wait_ge(s["u_c0"], 2 * FT * l + 2 * i + 2)
                    y = yab[i % 2]
                    for w in (1, 2):
                        for ab in (0, 1):
                            c = FT * ab + i
                            last = v.scalar_tensor_tensor(out=y[ab][:, 0:304], in0=uab[i % 2][ab][:, w:304 + w], scalar=fpar[:, 3 * l + w, c:c + 1],
                                                          in1=y[ab][:, 0:304], op0=ALU.mult, op1=ALU.add)
                            if (w, ab) == (2, 0):
                                last.then_inc(s["u_ya"], 1)
                        drain()
                    dve.wait_ge(s["u_silu"], FT * l + i + 1)
                    v.tensor_tensor(hT[:, i, 0:SEQ], sil[i % 2][:, 0:SEQ], y[1][:, 0:SEQ], ALU.mult)
                    v.tensor_tensor(sampled(hT[:, i, SEQ:N]), padded(sil[i % 2])[:, :, 0:4], padded(y[1])[:, :, 0:4],
                                    ALU.mult).then_inc(s["h_tile"], 1)


_OUTS = [(1, SEQ, D_MODEL), (DEC_BATCH, DEC_SEQ, D_MODEL), (DEPTH, 1, SEQ, 4, HD), (DEPTH, 1, SEQ, 4, HD),
         (DEPTH, DEC_BATCH, DEC_SEQ, 4, HD), (DEPTH, DEC_BATCH, DEC_SEQ, 4, HD), (DEPTH, 1, 4, HD, HD),
         (DEPTH, DEC_BATCH, 4, HD, HD), (DEPTH, 1, 2, 256), (DEPTH, DEC_BATCH, 2, 256), (DEPTH, 1, 2, 2 * D_FF),
         (DEPTH, DEC_BATCH, 2, 2 * D_FF), (DEPTH, 1, N_MEM, 4, HD), (DEPTH, 1, N_MEM, 4, HD)]


def kernel(**inputs):
    import numpy as _np
    import concourse.bacc as _bacc
    from concourse import mybir as _mybir
    from concourse.bass_utils import run_bass_kernel_spmd as _run

    nc = _bacc.Bacc("TRN2", target_bir_lowering=False, num_devices=1)
    const_f, const_i = constants()
    arrays, aps = {}, {}
    for name, value in {**inputs, "const_f": const_f, "const_i": const_i}.items():
        value = _np.ascontiguousarray(value)
        arrays[f"in_{name}"] = value
        aps[name] = nc.dram_tensor(f"in_{name}", value.shape, _mybir.dt.from_np(value.dtype), kind="ExternalInput").ap()
    outs = [nc.dram_tensor(f"out_{i}", shape, _mybir.dt.float32, kind="ExternalOutput").ap()
            for i, shape in enumerate(_OUTS)]
    decoder_kernel(nc, aps, outs)
    r = _run(nc, [arrays], core_ids=[0])
    return tuple(r.results[0][f"out_{i}"] for i in range(len(_OUTS)))
```

```python
from contextlib import ExitStack

import concourse.bass as bass
import numpy as np
from concourse import mybir

ALU = mybir.AluOpType
ACT = mybir.ActivationFunctionType
AX_X = mybir.AxisListType.X
F32 = mybir.dt.float32
F32R = mybir.dt.float32r
I32 = mybir.dt.int32

P = 128
D_MODEL, SEQ, DEPTH = 1024, 256, 2
DEC_BATCH, DEC_SEQ, PAGE, N_PAGES = 8, 4, 128, 2
HD = 64
N_MEM = 256
D_FF = 2816
EPS = 1e-6
SCALE = HD ** -0.5
NS = DEC_BATCH * DEC_SEQ
N = SEQ + NS
KT_D = D_MODEL // P
FT = D_FF // P
UG = 4
UJ = 2 * FT // UG
BIG = 1e30

W_Q, W_K, W_V, W_HQ, W_HF, W_HI, W_HG, W_CB, W_CC, W_CH = (
    0, 512, 768, 1024, 1280, 1536, 1792, 2048, 2304, 2560)
IN_CHUNKS = [("hf", W_HF), ("hq", W_HQ), ("hi", W_HI), ("k", W_K), ("q0", W_Q), ("q1", W_Q + 256),
             ("v", W_V), ("cc", W_CC), ("ch", W_CH), ("cb", W_CB), ("hg", W_HG)]

CHUNKS = ([("in", n) for n in range(len(IN_CHUNKS))] + [("mk", 0), ("mv", 0)]
          + [("out", n) for n in range(4)] + [("xq", 0), ("xo", 0)]
          + [("up", n) for n in range(FT)] + [("down", n) for n in range(12)])
SLOTS = 4


def dmas_of(kind, i):
    if kind == "in" and IN_CHUNKS[i][0] in ("q0", "q1"):
        return 4
    return {"out": 5, "up": 2}.get(kind, 1)


DOWN_K = [(0, 8), (8, 16), (16, 22)]

LO_DVE = 3
LEVELS = [1, 2, 4, 8, 16, 32, 64]

C_IDENT, C_PERM, C_ONES, C_BLK, C_COS, C_SIN = 0, 128, 256, 384, 512, 512 + N
C_MASKA = C_SIN + N
C_MASKS = C_MASKA + 384
C_SEL = C_MASKS + NS
C_N = C_SEL + DEC_BATCH
M_LEVEL = {m: P + 64 * i for i, m in enumerate(LEVELS)}
M_N = P + 64 * len(LEVELS)


def constants():
    f = np.zeros((P, C_N), np.float32)
    p = np.arange(P)
    f[:, C_IDENT:C_IDENT + P] = np.eye(P)
    half = HD // 2
    for d in range(P):
        if d % HD < half:
            f[d + half, C_PERM + d] = -1.0
        else:
            f[d - half, C_PERM + d] = 1.0
    f[:, C_ONES:C_ONES + P] = 1.0
    f[:, C_BLK:C_BLK + P] = (p[:, None] // HD == p[None, :] // HD)
    pos = np.concatenate([np.arange(SEQ), SEQ + np.tile(np.arange(DEC_SEQ), DEC_BATCH)]).astype(np.float32)
    inv = np.float32(10000.0) ** (-np.arange(half, dtype=np.float32) / np.float32(half))
    ang = (pos[None, :] * inv[p % half][:, None]).astype(np.float32).astype(np.float64)
    f[:, C_COS:C_COS + N] = np.cos(ang)
    f[:, C_SIN:C_SIN + N] = np.sin(ang)
    q = np.arange(P)[:, None]
    k = np.arange(P)[None, :]
    causal = np.where(k <= q, 0.0, -BIG)
    f[:, C_MASKA:C_MASKA + P] = causal
    f[:, C_MASKA + 2 * P:C_MASKA + 3 * P] = causal
    row = np.arange(P)[:, None]
    t = np.arange(NS)[None, :]
    f[:, C_MASKS:C_MASKS + NS] = np.where((t // 4 == row // 16) & (t % 4 <= row % 4), 0.0, -BIG)
    f[:NS, C_SEL:C_SEL + DEC_BATCH] = (np.arange(NS)[:, None] // 4 == np.arange(DEC_BATCH)[None, :])
    m = np.zeros((P, M_N), np.int32)
    m[:, :P] = np.eye(P)
    for h in LEVELS:
        c = np.arange(64)[None, :]
        s = np.arange(P)[:, None]
        m[:, M_LEVEL[h]:M_LEVEL[h] + 64] = (s // (2 * h) == c // h) & (s % (2 * h) < h)
    return f, m


R_MIX, R_XATTN, R_MEM, R_FFN = (0, 8), (16, 8), (32, 8), (48, 8)
R_LB, R_NORM, R_CONV = (64, 2), (68, 2), (72, 6)
R_FINAL = 84


def par_col(r, l, k=0):
    return r[0] + l * r[1] + k


def layer_schedule(l):
    s = []

    def a(who, step, *args):
        s.append((step, args, who))

    def level(m):
        a("D", "level", m, 0)
        a("D", "level", m, 1)
        a("op", "merge", m)

    def scores(g):
        a("D", "as", g, 0)
        a("D", "as", g, 1)

    def turn_probs(g):
        a("A", "at", g, 0)
        a("A", "at", g, 1)

    first = l == 0
    a("D", "in", "hf", 0)
    a("D", "in", "hf", 1)
    a("D", "ssq", 0)
    if first:
        a("D", "par")
        a("D", "fpar")
        a("op", "bounds")
    a("D", "in", "hq", 0)
    a("A", "turn_past", 0)
    a("D", "in", "hq", 1)
    a("D", "in", "hi", 0)
    a("A", "turn_past", 1)
    a("D", "in", "hi", 1)
    a("op", "gates")
    if first:
        a("op", "mem_rms")
    a("D", "in", "k", 0)
    for t in range(3):
        a("A", "turn_hi", t)
    a("D", "in", "k", 1)
    a("A", "turn_past", 2)
    for i in (0, 1):
        a("D", "diag", i)
    for i in (0, 1):
        a("D", "diag_s", i)
    a("D", "in", "q0", 0)
    a("D", "in", "q0", 1)
    a("A", "turn_past", 3)
    a("D", "rope", "k", 0)
    a("D", "rope", "k", 1)
    level(1)
    a("D", "in", "q1", 0)
    for t in range(3):
        a("A", "turn_k", t)
    a("D", "in", "q1", 1)
    a("A", "turn_past", 4)
    a("D", "rope", "q", 0)
    a("D", "rope", "q", 1)
    level(2)
    a("D", "in", "v", 0)
    a("D", "rope", "q", 2)
    a("D", "in", "v", 1)
    a("A", "turn_past", 5)
    a("D", "rope", "q", 3)
    a("op", "sq", 0)
    level(4)
    a("D", "cstate_in")
    a("D", "in", "cc", 0)
    for t in range(3):
        a("A", "turn_v", t)
    scores(0)
    a("D", "in", "cc", 1)
    a("A", "turn_past", 6)
    if first:
        for k in range(KT_D // 2):
            a("A", "turn_mem", k)
    level(8)
    a("op", "anorm", 0)
    a("D", "in", "ch", 0)
    turn_probs(0)
    scores(1)
    a("D", "in", "ch", 1)
    a("A", "ao", 0)
    a("A", "turn_past", 7)
    if first:
        for k in range(KT_D // 2, KT_D):
            a("A", "turn_mem", k)
    level(16)
    a("op", "anorm", 1)
    a("D", "in", "cb", 0)
    turn_probs(1)
    scores(2)
    a("D", "in", "cb", 1)
    a("A", "ao", 1)
    level(32)
    a("op", "anorm", 2)
    a("D", "in", "hg", 0)
    turn_probs(2)
    scores(3)
    a("D", "in", "hg", 1)
    a("A", "ao", 2)
    level(64)
    a("op", "anorm", 3)
    a("D", "ss", 0)
    turn_probs(3)
    a("D", "cross", 0)
    a("D", "cross", 1)
    a("op", "merge", P)
    a("A", "mk", 0)
    a("op", "snorm", 0)
    a("A", "ao", 3)
    for t in range(3):
        a("A", "turn_ke", t)
    a("op", "sq", 1)
    a("op", "conv")
    a("A", "mk", 1)
    a("A", "st", 0)
    a("D", "ho", 0)
    a("D", "ho", 1)
    a("D", "ss", 1)
    a("op", "snorm", 1)
    a("A", "mv", 0)
    a("D", "hn", 0)
    a("D", "hn", 1)
    a("A", "so", 0)
    a("A", "st", 1)
    a("A", "mv", 1)
    a("A", "hstate")
    a("A", "so", 1)
    for m in range(8):
        a("D", "out", m)
        if m < 6:
            a("A", "turn_cmem", m)
        if m == 6:
            a("D", "hstate_s", 0)
            a("D", "hstate_s", 1)
    a("D", "xq", 0)
    a("D", "xq", 1)
    a("D", "ssq", 1)
    a("op", "yq")
    a("A", "turn_cmem", 6)
    for t in (0, 1):
        a("A", "turn_mk", t)
    a("A", "cstate_out")
    a("A", "turn_cmem", 7)
    a("A", "ustate_in", 0)
    a("A", "ustate_in", 1)
    a("A", "xs", 0)
    a("A", "xs", 1)
    a("op", "xnorm", 0)
    a("A", "ys")
    a("op", "xnorm", 1)
    a("A", "xt", 0)
    a("A", "xt", 1)
    a("A", "xs", 2)
    a("op", "ynorm")
    a("A", "xov", 0)
    a("A", "yt")
    a("A", "xs", 3)
    a("op", "xnorm", 2)
    a("op", "xnorm", 3)
    a("op", "round", "up", 0)
    a("op", "rest", "up", 0)
    a("A", "yo", 0)
    a("A", "xt", 2)
    a("A", "xt", 3)
    a("op", "round", "up", 1)
    a("op", "rest", "up", 1)
    a("A", "yo", 1)
    a("A", "xov", 1)
    a("op", "round", "up", 2)
    for m in range(8):
        a("D", "xo", m)
    a("op", "pads", 0)
    a("op", "rest", "up", 2)
    for i in range(FT):
        ahead = ("up", i + 2) if i + 2 < FT else ("down", i + 2 - FT)
        if i:
            a("op", "round", *ahead)
        a("D", "up", i, 0)
        if i:
            a("op", "convolve", i - 1)
        a("D", "up", i, 1)
        if i + 1 < FT:
            a("op", "pads", i + 1)
        if i:
            a("op", "gate", i - 1)
            a("op", "rest", *ahead)
        if i == 0:
            a("D", "ssq", 2)
    a("op", "convolve", FT - 1)
    a("op", "gate", FT - 1)
    a("op", "round", "down", 2)
    a("op", "rest", "down", 2)
    for m in range(0, 8, 2):
        for c in range(3 * m // 2 + 3, min(3 * m // 2 + 6, 12)):
            a("op", "round", "down", c)
            a("op", "rest", "down", c)
        a("D", "down", m)
        a("D", "down", m + 1)
        if m < 6:
            a("A", "ustate_out", m // 2)
    return s


def emptied_order(steps):
    out = []
    for step in steps:
        at = len(out)
        if step[1] == "ssq_final":
            at -= 3
        if step[1] == "ssq" and step[0] < DEPTH:
            while out[at - 1][1] in ("in", "xq", "up", "round", "rest", "pads"):
                at -= 1
        out.insert(at, step)
    return out


PROLOGUE = [("turn_x", (k,), "D") for k in range(KT_D)] + [("par_mix", (), "D")]
EPILOGUE = ([("y", (t, 0), "AD"[t % 2]) for t in range(3)] + [("ssq_final", (), "D")]
            + [("y", (t, 1), "AD"[t % 2]) for t in range(3)])


class Banks:

    def __init__(self):
        self.steps = [(-1, *x) for x in PROLOGUE]
        for l in range(DEPTH):
            self.steps += [(l, *x) for x in layer_schedule(l)]
        self.steps += [(DEPTH, *x) for x in EPILOGUE]
        self.emptying_steps = emptied_order(self.steps)
        fills = [x for x in self.steps if x[3] != "op"]
        self.of = {x[:3]: n for n, x in enumerate(fills)}
        emptied = {}
        for who, steps in (("A", self.steps), ("D", self.emptying_steps)):
            own = [x for x in steps if x[3] == who]
            emptied.update({x[:3]: (who, n + 1) for n, x in enumerate(own)})
        self.before = [emptied[x[:3]] for x in fills]


def decoder_kernel(nc, a, out):
    (y_prompt, y_sample, k_prompt, v_prompt, k_sample, v_sample, hgrn_prompt, hgrn_sample,
     conv_prompt, conv_sample, ffn_prompt, ffn_sample, mem_k_prompt, mem_v_prompt) = out
    banks = Banks()
    with ExitStack() as ctx:
        def sb(name, *shape, dt=F32):
            return ctx.enter_context(nc.sbuf_tensor(name, list(shape), dt))

        def sem(name):
            return ctx.enter_context(nc.semaphore(name))

        ps = ctx.enter_context(nc.psum_tensor("banks", [P, 8, 512], F32))
        shared = {"XG": (KT_D, N), "ring": (SLOTS, 2048), "keysT": (2, DEC_BATCH, 256),
                  "vals": (DEC_BATCH, 2, 256), "rawk": (2, 2, 256), "mix": (KT_D, N), "phase": (18600,)}
        with ExitStack() as plain:
            as_f32 = {n: plain.enter_context(nc.sbuf_tensor(n, [P, *shape], F32)) for n, shape in shared.items()}
        rounded = {n: sb(n + "_r", P, *shape, dt=F32R) for n, shape in shared.items()}
        XG = as_f32["XG"]
        ring = as_f32["ring"]
        keysT = as_f32["keysT"]
        vals = as_f32["vals"]
        rawk = as_f32["rawk"]
        mix = as_f32["mix"]
        phase = as_f32["phase"]
        con = sb("con", P, C_N)
        mask = sb("mask", P, M_N, dt=I32)
        pages = sb("pages", 1, DEC_BATCH * N_PAGES, dt=I32)
        X = sb("X", P, KT_D, N)
        acc = sb("acc", P, N)
        sqr = sb("sqr", P, N)
        memT = sb("memT", P, KT_D, N_MEM)
        mkT = sb("mkT", P, 2, N_MEM)
        mv = sb("mv", P, 2, 256)
        par = sb("par", P, R_FINAL + 8)
        fpar = sb("fpar", P, DEPTH * 3, 2 * FT)
        Rn = sb("Rn", P, N)
        vv = sb("vv", P, N)
        small = sb("small", P, 96)
        ustr = sb("ustr", UG * 16, UJ * P)
        ust = sb("ust", P, UJ, UG, 16)
        used = [0]

        def ph(*shape, parts=P):
            n = int(np.prod(shape))
            v = phase[0:parts, used[0]:used[0] + n]
            used[0] += n
            assert used[0] <= 18600, used[0]
            if len(shape) > 1:
                names = "abcd"[:len(shape)]
                v = v.rearrange(f"p ({' '.join(names)}) -> p {' '.join(names)}", **dict(zip(names, shape)))
            return v

        prob = ph(2, 512)
        probT = ph(2, 512)
        qT = ph(4, N)
        kT = ph(2, N)
        sc = ph(2, 6, P)
        scs = ph(2, 2, NS)
        hf = ph(2, N)
        hq = ph(2, N)
        hk = ph(2, N)
        hi = ph(2, N)
        hgs = ph(2, N)
        e1 = ph(2, N)
        e2 = ph(2, N)
        vh = ph(3, 256)
        vn = ph(3, 256)
        turned = ph(3, 256)
        ke = ph(3, 256)
        s0 = ph(2, 8, HD)
        cb = ph(2, N)
        uc = ph(2, 306)
        yc = ph(2, 306)
        qs = ph(8 * 144)
        qa = ph(P)
        probs = ph(N)
        probsT = ph(384)
        hsp = ph(2, HD)
        cst = probsT[0:16, 0:256]
        cvo = ph(256, parts=18)
        mko = ph(2, 256)
        vt = prob.rearrange("p i n -> p (i n)")[:, 0:2 * N].rearrange("p (k n) -> p k n", k=2)
        clast = ph(2, 18)
        t4 = ph(2, 8)
        used[0] = 0
        hT = ph(FT, N)
        uab = [[ph(306), ph(306)] for _ in range(2)]
        yab = [[ph(306), ph(306)] for _ in range(2)]
        sil = [ph(306) for _ in range(2)]
        ulast = ph(UJ, UG, 18)
        ulo = ph(UJ * P, parts=UG * 18)
        hT_lo = rounded["phase"][:, 0:FT * N].rearrange("p (k n) -> p k n", k=FT)
        hT_hi = rounded["phase"][:, used[0]:used[0] + FT * N].rearrange("p (k n) -> p k n", k=FT)
        ph(FT, N)
        used[0] = 0
        yrow = ph(3, D_MODEL)
        used[0] = 0
        xin = ph(2, D_MODEL)
        xsin = ph(D_MODEL, parts=NS)
        rows = ph(P, parts=R_FINAL + 8)
        frows = ph(DEPTH * 3, P, parts=2 * FT)
        memin = mix[:].rearrange("p k n -> p (k n)")[:, 0:2 * D_MODEL].rearrange("p (t d) -> p t d", t=2)
        mg = XG[:, :, 0:N_MEM]
        vexp = XG[0:NS].rearrange("p k n -> p (k n)")[:, 0:2048].rearrange("p (h b v) -> p h b v", h=4, b=8)
        rawk_r = rounded["rawk"][:].rearrange("p a b c -> p (a b c)")
        xg_hi = [rounded["mix"][:, 2 + k] if k < 6 else rawk_r[:, N * (k - 6):N * (k - 5)] for k in range(KT_D)]
        xg_lo = rounded["XG"]
        ring_lo = rounded["ring"]
        ring_hi = ([rounded["keysT"][:, i].rearrange("p b n -> p (b n)") for i in (0, 1)]
                   + [rounded["vals"][:, 4 * i:4 * i + 4].rearrange("p b j c -> p (b j c)") for i in (0, 1)])
        newS = sb("newS", P, 2, 8, HD)

        ident = con[:, C_IDENT:C_IDENT + P]
        perm = con[:, C_PERM:C_PERM + P]
        ones = con[:, C_ONES:C_ONES + P]
        blk = con[:, C_BLK:C_BLK + P]

        filled = sem("filled")
        emptied = {"A": sem("emptied_by_act"), "D": sem("emptied_by_dve")}
        loaded = [sem(f"loaded{i}") for i in range(SLOTS)]
        x_in = sem("x_in")
        mix_in = sem("mix_in")
        par_in = sem("par_in")
        fpar_in = sem("fpar_in")
        con_in = sem("con_in")
        mem_in = sem("mem_in")
        rawk_in = [sem("rawk0_in"), sem("rawk1_in")]
        vals_in = sem("vals_in")
        s0_in = sem("s0_in")
        cstate_in = sem("cstate_in")
        ustate_in = sem("ustate_in")
        pages_in = sem("pages_in")
        y_stored = sem("y_stored")
        stored = sem("stored")
        s = {n: sem(n) for n in (
            "sumsq", "xg_tile", "mg_even", "mg_odd", "rms_guess", "sigmoids", "gates_ready", "silu_gate_in",
            "h_level", "roped", "conv_done", "att_max", "att_exp", "att_p", "s_q", "s_max", "s_exp", "s_p",
            "zeros", "vexp_ready", "h_square", "h_out", "news_ready", "y_q", "y_max", "y_p", "x_max", "x_p",
            "down_used", "xg_hi", "xg_lo", "h_hi", "h_lo", "u_pads", "u_c0", "u_ya", "u_conv", "u_silu", "u_last", "h_tile", "mem_square", "mem_v", "mem_guess",
            "mem_scaled", "lb_d", "lb_exp", "lb_ready", "y_guess", "y_rms")}
        w_hi = sem("w_hi")
        w_lo_dve = sem("w_lo_dve")
        w_lo_pool = sem("w_lo_pool")
        block = ctx.enter_context(nc.Block())

        dma_count = {}
        total = [0] * SLOTS
        for l in range(DEPTH):
            for n, (kind, i) in enumerate(CHUNKS):
                slot = (l * len(CHUNKS) + n) % SLOTS
                total[slot] += 16 * dmas_of(kind, i)
                dma_count[l, n] = total[slot]
        index = {c: n for n, c in enumerate(CHUNKS)}
        N_SPLIT = len(CHUNKS) - index["up", 0]

        def split_chunk(l, kind, i):
            n = index[kind, i]
            slot = (l * len(CHUNKS) + n) % SLOTS
            tiles = DOWN_K[i % 3][1] - DOWN_K[i % 3][0] if kind == "down" else KT_D
            split = n - index["up", 0]
            return N_SPLIT * l + split + 1, slot, ring_hi[split % SLOTS], tiles

        def fill_no(l, step, *args):
            return banks.of[l, step, args] + 1

        def pe_done(eng, l, step, *args):
            eng.wait_ge(filled, fill_no(l, step, *args))

        def wait_emptied(eng, l, step, *args):
            who, count = banks.before[banks.of[l, step, args]]
            eng.wait_ge(emptied[who], count)

        def bank(l, step, *args):
            return ps[:, banks.of[l, step, args] % 8, :]

        def last_use(l, n):
            kind, i = CHUNKS[n]
            if kind == "in":
                return fill_no(l, "in", IN_CHUNKS[i][0], 1)
            if kind in ("out",):
                return fill_no(l, "out", 2 * i + 1)
            if kind == "xo":
                return fill_no(l, "xo", 7)
            if kind == "up":
                return fill_no(l, "up", i, 1)
            if kind == "down":
                return fill_no(l, "down", i // 3 * 2 + 1)
            return fill_no(l, kind, 1)

        STORES_MIXER = 2 + 2 + 2 + 2 + 2 + 4
        STORES_LAYER = STORES_MIXER + 2 * UG

        @block.sync
        def _(sp):
            sp.dma_start(con[:, 0:C_BLK], a["const_f"][:, 0:C_BLK]).then_inc(x_in, 16)
            sp.dma_start(xin[:, 0], a["x_prompt"][0, 0:P]).then_inc(x_in, 16)
            sp.dma_start(xsin, a["x_sample"].rearrange("b s d -> (b s) d")).then_inc(x_in, 16)
            sp.dma_start(rows[0:DEPTH * 8], a["g_mix"].rearrange("l (k p) -> (l k) p", p=P)).then_inc(mix_in, 16)
            for l in range(DEPTH):
                for n, (kind, i) in enumerate(CHUNKS):
                    g = l * len(CHUNKS) + n
                    slot = ring[:, g % SLOTS]
                    if g >= SLOTS:
                        l_, n_ = divmod(g - SLOTS, len(CHUNKS))
                        kind_, i_ = CHUNKS[n_]
                        if kind_ == "down" and i_ % 3 < 2:
                            sp.wait_ge(s["down_used"], 8 * l_ + i_ // 3 * 2 + i_ % 3 + 1)
                        else:
                            sp.wait_ge(filled, last_use(l_, n_))
                    got = loaded[g % SLOTS]

                    def load(src, dst=slot.rearrange("p (k c) -> p k c", c=256)):
                        sp.dma_start(dst, src).then_inc(got, 16)

                    if kind == "in":
                        c0 = IN_CHUNKS[i][1]
                        w = a["w_in"][l][:, c0:c0 + 256].rearrange("(k p) c -> p k c", p=P)
                        if IN_CHUNKS[i][0] in ("q0", "q1"):
                            dst = slot.rearrange("p (k c) -> p k c", c=256)
                            for g in range(2):
                                for half in range(2):
                                    c, d = (2 * half + g) * HD, (2 * g + half) * HD
                                    load(w[:, :, c:c + HD], dst[:, :, d:d + HD])
                        else:
                            load(w)
                    elif kind in ("mk", "mv", "xq"):
                        load(a["w_" + kind][l].rearrange("(k p) c -> p k c", p=P))
                    elif kind == "out":
                        w = a["w_out"][l][:, 256 * i:256 * i + 256]
                        dst = slot.rearrange("p (k c) -> p k c", c=256)
                        heads = w[0:512].rearrange("(p i g d) c -> p i d g c", p=2, i=2, g=2)
                        for p in range(2):
                            for half in range(2):
                                load(heads[p, half], dst[64 * half:64 * half + 64, 2 * p:2 * p + 2])
                        load(w[512:1024].rearrange("(k p) c -> p k c", p=P), dst[:, 4:8])
                    elif kind == "xo":
                        load(a["w_xo"][l].rearrange("(k p) c -> p k c", p=P), slot.rearrange("p (k c) -> p k c", k=2))
                    elif kind == "up":
                        dst = slot.rearrange("p (k c) -> p k c", c=256)
                        for ab in (0, 1):
                            c0 = ab * D_FF + i * P
                            load(a["w_up"][l][:, c0:c0 + P].rearrange("(k p) c -> p k c", p=P), dst[:, :, P * ab:P * ab + P])
                    else:
                        k0, k1 = DOWN_K[i % 3]
                        c0 = 256 * (i // 3)
                        load(a["w_down"][l][P * k0:P * k1, c0:c0 + 256].rearrange("(k p) c -> p k c", p=P),
                             slot.rearrange("p (k c) -> p k c", c=256)[:, 0:k1 - k0])

            for t in range(3):
                for h in (0, 1):
                    wait_emptied(sp, DEPTH, "y", t, h)
                if t < 2:
                    sp.dma_start(y_prompt[0, P * t:P * t + P], yrow[:, t]).then_inc(y_stored, 16)
                else:
                    sp.dma_start(y_sample.rearrange("b s d -> (b s) d"), yrow[0:NS, 2]).then_inc(y_stored, 16)
            sp.wait_ge(y_stored, 16 * 3)

        @block.gpsimd
        def _(pool):
            g_ = nc.gpsimd
            rawk_use = [0, 0]

            def load_rawk(l, n):
                b, half = n % 8, n % 2
                if n >= 2:
                    pe_done(pool, l, *(("turn_past", n - 2) if n - 2 < 8 else ("turn_cmem", n - 10)))
                elif l:
                    pe_done(pool, l - 1, "turn_cmem", 6 + n)
                if n < 8:
                    for j in range(N_PAGES):
                        page = pool.value_load(pages[0:1, b * N_PAGES + j:b * N_PAGES + j + 1],
                                               min_val=0, max_val=a["cache_k"].shape[1] - 1)
                        src = a["cache_k"][l][bass.ds(page, 1)].rearrange("a r h d -> r (a h d)")
                        pool.dma_start(rawk[:, half, j], src).then_inc(rawk_in[half], 16)
                else:
                    src = a["cache_mem_k"][l, b].rearrange("(t p) h d -> p t (h d)", p=P)
                    pool.dma_start(rawk[:, half], src).then_inc(rawk_in[half], 16)

            def layer_loads(l):
                load_rawk(l, 0)
                load_rawk(l, 1)
                for g in range(UG):
                    src = a["state_ffn"][l].rearrange("b w f -> (b w) f")[:, g * UJ * P:(g + 1) * UJ * P]
                    pool.dma_start(ustr[16 * g:16 * g + 16], src).then_inc(ustate_in, 16)

            def load_vals(l, b):
                for i in (N_PAGES * b, N_PAGES * b + 1):
                    page = pool.value_load(pages[0:1, i:i + 1], min_val=0, max_val=a["cache_v"].shape[1] - 1)
                    src = a["cache_v"][l][bass.ds(page, 1)].rearrange("a r h d -> r (a h d)")
                    pool.dma_start(vals[:, i // N_PAGES, i % N_PAGES], src).then_inc(vals_in, 16)

            def store(dst, src):
                pool.dma_start(dst, src).then_inc(stored, 16)

            pool.dma_start(pages[:], a["page_table"].rearrange("b n -> (b n)").rearrange("(a n) -> a n", a=1)).then_inc(pages_in, 16)
            pool.wait_ge(pages_in, 16)
            layer_loads(0)
            for l, step, args, who in banks.steps:
                if l < 0:
                    continue
                if (step, args) == ("ssq", (0,)):
                    pe_done(pool, l, "ssq", 0) if l else pe_done(pool, 0, "fpar")
                    if l:
                        pool.wait_ge(stored, 16 * l * STORES_LAYER)
                    for h in range(4):
                        pool.dma_start(s0[64 * (h % 2):64 * (h % 2) + 64, h // 2],
                                       a["state_hgrn"][l][:, h].rearrange("b d v -> d b v")).then_inc(s0_in, 16)
                    pool.dma_start(cst, a["state_conv"][l].rearrange("b w c -> (b w) c")).then_inc(cstate_in, 16)
                    g_.memset(sc, 0.0)
                    g_.memset(scs[0:NS], 0.0)
                    g_.memset(qs, 0.0)
                    g_.memset(qa, 0.0).then_inc(s["zeros"], 1)
                elif (step, args) == ("turn_k", (2,)):
                    wait_emptied(pool, l, "turn_k", 2)
                    store(k_prompt[l, 0].rearrange("(t p) h d -> p t (h d)", p=P), turned[:, 0:2])
                    store(k_sample[l].rearrange("b s h d -> (b s) (h d)"), turned[0:NS, 2])
                elif (step, args) == ("turn_v", (2,)):
                    wait_emptied(pool, l, "turn_v", 2)
                    store(v_prompt[l, 0].rearrange("(t p) h d -> p t (h d)", p=P), vn[:, 0:2])
                    store(v_sample[l].rearrange("b s h d -> (b s) (h d)"), vn[0:NS, 2])
                elif (step, args) == ("in", ("hg", 1)):
                    pe_done(pool, l, "in", "hg", 1)
                    if l == 0:
                        wait_emptied(pool, 0, "turn_mem", KT_D - 1)
                    pool.drain()
                    for k in range(1, KT_D, 2):
                        c = par_col(R_MEM, l, k)
                        g_.tensor_scalar(mg[:, k], memT[:, k], par[:, c:c + 1], None, ALU.mult).then_inc(s["mg_odd"], 1)
                elif (step, args) == ("turn_mk", (1,)):
                    wait_emptied(pool, l, "turn_mk", 1)
                    store(mem_k_prompt[l, 0].rearrange("(t p) h d -> p t (h d)", p=P), mko)
                elif (step, args) == ("mv", (1,)):
                    wait_emptied(pool, l, "mv", 1)
                    store(mem_v_prompt[l, 0].rearrange("(t p) h d -> p t (h d)", p=P), mv[:])
                    wait_emptied(pool, l, "turn_hi", 2)
                    pool.wait_ge(con_in, 32)
                    pool.drain()
                    for h in range(4):
                        last = g_.tensor_tensor(
                            vexp[:, h], vh[0:NS, 2, h * HD:(h + 1) * HD].unsqueeze(1).broadcast_to([NS, 8, HD]),
                            con[0:NS, C_SEL:C_SEL + 8].unsqueeze(2).broadcast_to([NS, 8, HD]), ALU.mult)
                    last.then_inc(s["vexp_ready"], 1)
                elif step == "turn_past":
                    load_rawk(l, args[0] + 2)
                    load_vals(l, args[0])
                elif step == "turn_cmem":
                    b = args[0]
                    if b < 6:
                        load_rawk(l, b + 10)
                    if b == 0:
                        pe_done(pool, l, "so", 1)
                    src = a["cache_mem_v"][l, b].rearrange("(t p) h d -> p t (h d)", p=P)
                    pool.dma_start(vals[:, b], src).then_inc(vals_in, 16)
                elif step == "cstate_out":
                    wait_emptied(pool, l, "cstate_out")
                    store(conv_prompt[l, 0], cvo[0:2])
                    store(conv_sample[l].rearrange("b w c -> (b w) c"), cvo[2:18])
                elif step == "sq":
                    p = args[0]
                    if p:
                        pe_done(pool, l, "ss", 0)
                    else:
                        pool.wait_ge(s["zeros"], l + 1)
                    pool.wait_ge(s["roped"], 6 * l + 6)
                    pool.drain()
                    for i in (0, 1):
                        rows_i = slice(64 * i, 64 * i + 64)
                        src = qT[rows_i, 2 * p:2 * p + 2, SEQ:N].rearrange("p g (b s) -> p b g s", b=8)
                        dst = qs[rows_i].rearrange("p (b x) -> p b x", x=144)[:, :, 8 * i:8 * i + 8]
                        g_.tensor_copy(dst.rearrange("p b (g s) -> p b g s", g=2), src)
                        dst = qa[rows_i].rearrange("p (b x) -> p b x", x=16)[:, :, 8 * i:8 * i + 8]
                        last = g_.tensor_copy(dst.rearrange("p b (g s) -> p b g s", g=2), src)
                    last.then_inc(s["s_q"], 1)
                elif (step, args) == ("hstate_s", (1,)):
                    wait_emptied(pool, l, "hstate_s", 1)
                    for h in range(4):
                        store(hgrn_sample[l][:, h].rearrange("b d v -> d b v"), newS[64 * (h % 2):64 * (h % 2) + 64, h // 2])
                elif (step, args) == ("hstate", ()):
                    wait_emptied(pool, l, "hstate")
                    for i in (0, 1):
                        store(hgrn_prompt[l, 0].rearrange("(k i) d v -> i d k v", k=2)[i], hsp[64 * i:64 * i + 64])
                    pe_done(pool, l, "ss", 1)
                    g_.memset(qs, 0.0)
                elif step == "yq":
                    wait_emptied(pool, l, "xq", 1)
                    pool.drain()
                    for p in (0, 1):
                        for i in (0, 1):
                            rows_i = slice(64 * i, 64 * i + 64)
                            src = qT[rows_i, p, SEQ:N].rearrange("p (b s) -> p b s", b=8)
                            dst = qs[rows_i, 576 * p:576 * p + 576].rearrange("p (b x) -> p b x", x=72)[:, :, 4 * i:4 * i + 4]
                            last = g_.tensor_copy(dst, src)
                    last.then_inc(s["y_q"], 1)
                elif step == "rest":
                    count, slot, hi_part, tiles = split_chunk(l, *args)
                    pool.wait_ge(w_hi, count)
                    cols = slice(LO_DVE * 256, tiles * 256)
                    pool.drain()
                    g_.tensor_tensor(ring_lo[:, slot, cols], ring[:, slot, cols], hi_part[:, cols].bitcast(F32),
                                     ALU.subtract).then_inc(w_lo_pool, 1)
                elif step == "xo":
                    k = args[0]
                    pool.wait_ge(s["xg_hi"], KT_D * l + k + 1)
                    pool.drain()
                    g_.tensor_tensor(xg_lo[:, k], XG[:, k], xg_hi[k].bitcast(F32), ALU.subtract).then_inc(s["xg_lo"], 1)
                elif step == "gate":
                    i = args[0]
                    pool.wait_ge(s["h_hi"], FT * l + i + 1)
                    pool.drain()
                    g_.tensor_tensor(hT_lo[:, i], hT[:, i], hT_hi[:, i].bitcast(F32), ALU.subtract).then_inc(s["h_lo"], 1)
                elif step == "pads":
                    i = args[0]
                    if i == 0:
                        pe_done(pool, l, "xo", 7)
                        pool.wait_ge(stored, 16 * (l * STORES_LAYER + STORES_MIXER))
                        wait_emptied(pool, l, "ustate_in", 1)
                    if i >= 2:
                        pool.wait_ge(s["u_conv"], FT * l + i - 1)
                        pool.wait_ge(s["u_c0"], 2 * (FT * l + i - 1))
                    for ab in (0, 1):
                        g, j = divmod(FT * ab + i, UJ)
                        u = uab[i % 2][ab]
                        g_.memset(u[:, 0:2], 0.0)
                        g_.tensor_copy(u[:, 258:306].rearrange("p (b x) -> p b x", x=6)[:, :, 0:2],
                                       ust[:, j, g].rearrange("p (b w) -> p b w", w=2)).then_inc(s["u_pads"], 1)
                elif step == "up":
                    i, ab = args
                    u = uab[i % 2][ab]
                    g, j = divmod(FT * ab + i, UJ)
                    wait_emptied(pool, l, "up", i, ab)
                    g_.tensor_copy(ulast[:, j, g, 0:2], u[:, 256:258])
                    g_.tensor_copy(ulast[:, j, g, 2:18].rearrange("p (b w) -> p b w", w=2),
                                   u[:, 258:306].rearrange("p (b x) -> p b x", x=6)[:, :, 4:6]).then_inc(s["u_last"], 1)
                elif (step, args) == ("down", (0,)) and l + 1 < DEPTH:
                    pe_done(pool, l, "up", FT - 1, 1)
                    layer_loads(l + 1)
                elif (step, args) == ("ustate_out", (2,)):
                    wait_emptied(pool, l, "ustate_out", 2)
                    for g in range(UG):
                        cols = slice(g * UJ * P, (g + 1) * UJ * P)
                        store(ffn_prompt[l, 0][:, cols], ulo[18 * g:18 * g + 2])
                        store(ffn_sample[l].rearrange("b w f -> (b w) f")[:, cols], ulo[18 * g + 2:18 * g + 18])
            pool.wait_ge(stored, 16 * DEPTH * STORES_LAYER)

        @block.scalar
        def _(act):
            ac = nc.scalar.activation
            act.dma_start(xin[:, 1], a["x_prompt"][0, P:SEQ]).then_inc(x_in, 16)
            for (r0, k), name in ((R_XATTN, "g_xattn"), (R_MEM, "g_mem"), (R_FFN, "g_ffn"),
                                  (R_LB, "hg_lb_logits"), (R_NORM, "hg_norm_g")):
                act.dma_start(rows[r0:r0 + DEPTH * k], a[name].rearrange("l (k p) -> (l k) p", p=P)).then_inc(par_in, 16)
            act.dma_start(rows[R_CONV[0]:R_FINAL], a["conv_w"].rearrange("l w (k p) -> (l w k) p", p=P)).then_inc(par_in, 16)
            act.dma_start(rows[R_FINAL:R_FINAL + 8], a["g_final"].rearrange("(k p) -> k p", p=P)).then_inc(par_in, 16)
            act.dma_start(frows, a["ffn_conv_w"].rearrange("l w (k p) -> k (l w) p", p=P)).then_inc(fpar_in, 16)
            act.dma_start(con[:, C_BLK:], a["const_f"][:, C_BLK:]).then_inc(con_in, 16)
            act.dma_start(mask[:], a["const_i"]).then_inc(con_in, 16)
            act.dma_start(memin, a["mem_prompt"][0].rearrange("(t p) d -> p t d", p=P)).then_inc(mem_in, 16)

            def take(l, step, args, dst, src):
                act.wait_ge(filled, fill_no(l, step, *args))
                return nc.scalar.copy(dst, src)

            def guess():
                ac(Rn[:], vv[:], ACT.Abs_reciprocal_sqrt).then_inc(s["rms_guess"], 1)

            def gained(l, stage, k):
                if stage == 3:
                    wait_emptied(act, l, "down", k)
                elif l == 0 and stage == 0:
                    wait_emptied(act, -1, "turn_x", k)
                else:
                    before = (l, ("", "out", "xo")[stage]) if stage else (l - 1, "down")
                    wait_emptied(act, *before, k)
                c = R_FINAL + k if stage == 3 else par_col((R_MIX, R_XATTN, R_FFN)[stage], l, k)
                ac(XG[:, k], X[:, k], ACT.Identity, scale=par[:, c:c + 1]).then_inc(s["xg_tile"], 1)
                if stage == 2:
                    ac(xg_hi[k], X[:, k], ACT.Identity, scale=par[:, c:c + 1]).then_inc(s["xg_hi"], 1)

            for l, step, args, who in banks.emptying_steps:
                if step == "par_mix":
                    wait_emptied(act, l, step)
                    for k in range(KT_D):
                        gained(0, 0, k)
                elif step == "bounds":
                    wait_emptied(act, 0, "par")
                    act.wait_ge(s["lb_d"], 1)
                    ac(small[:, 8:12], small[:, 4:8], ACT.Exp).then_inc(s["lb_exp"], 1)
                elif step == "mem_rms":
                    act.wait_ge(mem_in, 16)
                    junk = keysT[:].rearrange("p k b n -> p (k b n)")
                    act.drain()
                    for t in (0, 1):
                        last = ac(junk[:, 3072:4096], memin[:, t], ACT.Square, accum_out=small[:, 80 + t:81 + t])
                        act.drain()
                    last.then_inc(s["mem_square"], 1)
                    act.wait_ge(s["mem_v"], 1)
                    ac(small[:, 86:88], small[:, 82:84], ACT.Abs_reciprocal_sqrt).then_inc(s["mem_guess"], 1)
                elif step == "ssq_final":
                    wait_emptied(act, l, step)
                    for n, c in ((P, slice(0, 2)), (NS, slice(2, 3))):
                        last = ac(small[0:n, 92 + c.start:92 + c.stop], small[0:n, 88 + c.start:88 + c.stop],
                                  ACT.Abs_reciprocal_sqrt)
                    last.then_inc(s["y_guess"], 1)
                elif step == "turn_mem":
                    take(l, step, args, memT[:, args[0]], bank(l, step, *args)[:, 0:N_MEM]).then_inc(emptied["A"], 1)
                elif step == "ssq" or step == "hn":
                    wait_emptied(act, l, step, *args)
                    guess()
                elif step == "gates":
                    if l:
                        act.wait_ge(stored, 16 * l * STORES_LAYER)
                    wait_emptied(act, l, "in", "hf", 1)
                    ac(hf, e1, ACT.Sigmoid)
                    ac(hk, e1, ACT.Sigmoid, scale=-1.0)
                    wait_emptied(act, l, "in", "hq", 1)
                    ac(hq, e2, ACT.Sigmoid).then_inc(s["sigmoids"], 1)
                elif (step, args) == ("in", ("hg", 1)):
                    wait_emptied(act, l, "in", "hg", 1)
                    for k in range(0, KT_D, 2):
                        c = par_col(R_MEM, l, k)
                        ac(mg[:, k], memT[:, k], ACT.Identity, scale=par[:, c:c + 1]).then_inc(s["mg_even"], 1)
                    act.wait_ge(s["gates_ready"], l + 1)
                    ac(e1, hgs, ACT.Sigmoid).then_inc(s["silu_gate_in"], 1)
                elif step in ("turn_hi", "turn_k", "turn_v", "turn_ke"):
                    t = args[0]
                    n = P if t < 2 else NS
                    if step == "turn_k" and t == 0 and l:
                        pass
                    if step == "turn_ke" and t == 0:
                        pass
                    dst = {"turn_hi": vh, "turn_k": turned, "turn_v": vn, "turn_ke": ke}[step]
                    take(l, step, args, dst[0:n, t], bank(l, step, *args)[0:n, 0:256]).then_inc(emptied["A"], 1)
                elif step == "mk":
                    take(l, step, args, mkT[:, args[0]], bank(l, step, *args)[:, 0:N_MEM]).then_inc(emptied["A"], 1)
                elif step == "mv":
                    if l and args[0] == 0:
                        act.wait_ge(stored, 16 * l * STORES_LAYER)
                    take(l, step, args, mv[:, args[0]], bank(l, step, *args)[:, 0:256]).then_inc(emptied["A"], 1)
                elif step == "turn_mk":
                    take(l, step, args, mko[:, args[0]], bank(l, step, *args)[:, 0:256]).then_inc(emptied["A"], 1)
                elif step in ("turn_past", "turn_cmem"):
                    src = bank(l, step, *args).rearrange("p (k m) -> p k m", k=2)
                    take(l, step, args, keysT[:, :, args[0]], src).then_inc(emptied["A"], 1)
                elif step == "cstate_out":
                    take(l, step, args, cvo[0:18], bank(l, step)[0:18, 0:256]).then_inc(emptied["A"], 1)
                elif step == "ustate_in":
                    j0, j1 = ((0, 8), (8, UJ))[args[0]]
                    src = bank(l, step, *args)[:, 0:64 * (j1 - j0)].rearrange("p (j x) -> p j x", x=64)
                    take(l, step, args, ust[:, j0:j1].rearrange("p j g r -> p j (g r)"), src).then_inc(emptied["A"], 1)
                elif step == "as":
                    g, i = args
                    c = 16 + 16 * (g % 2) + 2 * i
                    act.wait_ge(s["att_max"], 8 * l + 2 * g + i + 1)
                    ac(prob[:, i, 0:P], prob[:, i, 0:P], ACT.Exp, bias=small[:, c + 4:c + 5], scale=SCALE,
                       accum_out=small[:, c + 8:c + 9])
                    ac(prob[:, i, P:384], prob[:, i, P:384], ACT.Exp, bias=small[:, c + 5:c + 6], scale=SCALE,
                       accum_out=small[:, c + 9:c + 10]).then_inc(s["att_exp"], 1)
                elif step == "at":
                    g, i = args
                    if g:
                        pe_done(act, l, "ao", g - 1)
                    take(l, step, args, probT[:, i, 0:384], bank(l, step, *args)[:, 0:384]).then_inc(emptied["A"], 1)
                elif step == "ao":
                    take(l, step, args, mix[:, args[0], 0:SEQ], bank(l, step, *args)[:, 0:SEQ]).then_inc(emptied["A"], 1)
                elif step == "ss":
                    act.wait_ge(s["s_max"], 2 * l + args[0] + 1)
                    ac(probs, probs, ACT.Exp, bias=small[:, 49:50], scale=SCALE,
                       accum_out=small[:, 50:51]).then_inc(s["s_exp"], 1)
                elif step == "st":
                    if args[0]:
                        pe_done(act, l, "so", 0)
                    b_ = bank(l, step, *args)
                    take(l, step, args, probsT[:, 0:256], b_[:, 0:256])
                    nc.scalar.copy(probsT[0:NS, 256:384], b_[0:NS, 256:384]).then_inc(emptied["A"], 1)
                elif step == "so":
                    p = args[0]
                    act.wait_ge(filled, fill_no(l, step, p))
                    for i in (0, 1):
                        rows_i = slice(64 * i, 64 * i + 64)
                        src = bank(l, step, p)[rows_i, 0:P].rearrange("p (b i g s) -> p i g b s", b=8, i=2, g=2)[:, i]
                        dst = mix[rows_i, 2 * p:2 * p + 2, SEQ:N].rearrange("p g (b s) -> p g b s", b=8)
                        last = nc.scalar.copy(dst, src)
                    last.then_inc(emptied["A"], 1)
                elif step == "hstate":
                    take(l, step, args, hsp.rearrange("p k v -> p (k v)"), bank(l, step)[:, 0:P]).then_inc(emptied["A"], 1)
                elif (step, args) == ("out", (7,)):
                    pe_done(act, l, "hstate_s", 1)
                    for k in range(KT_D):
                        gained(l, 1, k)
                elif step == "xo":
                    if args[0] == 0:
                        pe_done(act, l, "turn_cmem", 7)
                    gained(l, 2, args[0])
                elif step == "down":
                    if l + 1 < DEPTH:
                        gained(l + 1, 0, args[0])
                    else:
                        gained(l, 3, args[0])
                elif step == "round":
                    count, slot, hi_part, tiles = split_chunk(l, *args)
                    if args == ("up", 0):
                        pe_done(act, l, "ys")
                    if args == ("up", 2):
                        pe_done(act, l, "yo", 1)
                    n = index[args]
                    act.wait_ge(loaded[(l * len(CHUNKS) + n) % SLOTS], dma_count[l, n])
                    nc.scalar.copy(hi_part[:, 0:tiles * 256], ring[:, slot, 0:tiles * 256]).then_inc(w_hi, 1)
                elif step == "ys":
                    act.wait_ge(s["y_max"], l + 1)
                    ac(probs[:, 0:256], bank(l, "ys")[:, 0:256], ACT.Exp, bias=small[:, 53:54], scale=SCALE,
                       accum_out=small[:, 54:55]).then_inc(emptied["A"], 1)
                elif step == "xs":
                    h = args[0]
                    c = 60 + 8 * (h % 2)
                    act.wait_ge(s["x_max"], 4 * l + h + 1)
                    if h >= 2:
                        pe_done(act, l, "xt", h - 2)
                    for q in (0, 1):
                        last = ac(prob[:, h % 2, 256 * q:256 * q + 256], bank(l, "xs", h)[:, 256 * q:256 * q + 256],
                                  ACT.Exp, bias=small[:, c + 2 + q:c + 3 + q], scale=SCALE,
                                  accum_out=small[:, c + 4 + q:c + 5 + q])
                    last.then_inc(emptied["A"], 1)
                elif step == "xt":
                    h = args[0]
                    if h >= 2:
                        pe_done(act, l, "xov", 0)
                    take(l, step, args, probT[:, h % 2], bank(l, step, h)).then_inc(emptied["A"], 1)
                elif step == "xov":
                    take(l, step, args, mix[:, args[0], 0:SEQ], bank(l, step, *args)[:, 0:SEQ]).then_inc(emptied["A"], 1)
                elif step == "yt":
                    take(l, step, args, probsT[:, 0:256], bank(l, step)[:, 0:256]).then_inc(emptied["A"], 1)
                elif step == "yo":
                    p = args[0]
                    act.wait_ge(filled, fill_no(l, step, p))
                    for i in (0, 1):
                        rows_i = slice(64 * i, 64 * i + 64)
                        src = bank(l, step, p)[rows_i, 0:64].rearrange("p (b i s) -> p i b s", b=8, i=2)[:, i]
                        dst = mix[rows_i, p, SEQ:N].rearrange("p (b s) -> p b s", b=8)
                        last = nc.scalar.copy(dst, src)
                    last.then_inc(emptied["A"], 1)
                elif step == "up":
                    i, ab = args
                    wait_emptied(act, l, "up", i, ab)
                    act.wait_ge(s["u_pads"], 2 * FT * l + 2 * i + ab + 1)
                    if i >= 2:
                        act.wait_ge(s["h_tile"], FT * l + i - 1)
                    c = FT * ab + i
                    ac(yab[i % 2][ab][:, 0:304], uab[i % 2][ab][:, 0:304], ACT.Identity,
                       scale=fpar[:, 3 * l, c:c + 1]).then_inc(s["u_c0"], 1)
                elif step == "convolve":
                    i = args[0]
                    act.wait_ge(s["u_ya"], FT * l + i + 1)
                    ac(sil[i % 2][:, 0:304], yab[i % 2][0][:, 0:304], ACT.Silu).then_inc(s["u_silu"], 1)
                elif step == "gate":
                    i = args[0]
                    act.wait_ge(s["h_tile"], FT * l + i + 1)
                    nc.scalar.copy(hT_hi[:, i], hT[:, i]).then_inc(s["h_hi"], 1)
                elif step == "ustate_out":
                    q = args[0]
                    n = P * (min(UJ, 4 * q + 4) - 4 * q)
                    take(l, step, args, ulo[0:UG * 18, 512 * q:512 * q + n],
                         bank(l, step, q)[0:UG * 18, 0:n]).then_inc(emptied["A"], 1)
                elif step == "y":
                    t, h = args
                    n = P if t < 2 else NS
                    if t == 1:
                        continue
                    act.wait_ge(s["y_rms"], 1)
                    pe_done(act, l, step, t, h)
                    ac(yrow[0:n, t, 512 * h:512 * h + 512], bank(l, step, t, h)[0:n], ACT.Identity,
                       scale=small[0:n, 92 + t:93 + t]).then_inc(emptied["A"], 1)

        @block.tensor
        def _(pe):
            mm = nc.tensor.matmul
            tr = nc.tensor.transpose
            rawk_n = [0, 0]

            def chunk(l, kind, i, part=None):
                n = index[kind, i]
                g = l * len(CHUNKS) + n
                pe.wait_ge(loaded[g % SLOTS], dma_count[l, n])
                return ring[:, g % SLOTS].rearrange("p (k c) -> p k c", c=256)

            def parts_of(l, kind, i):
                count, slot, hi_part, _ = split_chunk(l, kind, i)
                pe.wait_ge(w_lo_dve, count)
                pe.wait_ge(w_lo_pool, count)
                return [w.rearrange("p (k c) -> p k c", c=256) for w in (hi_part, ring_lo[:, slot])]

            def xg(l, stage, k):
                pe.wait_ge(s["xg_tile"], 24 * l + 8 * stage + k + 1)
                return XG[:, k]

            def project(out_, w, cols, l, stage):
                for k in range(KT_D):
                    last = mm(out_[:, 0:N], w[:, k, cols], xg(l, stage, k), start=k == 0, stop=k == KT_D - 1)
                return last

            def split_product(out_, hi_w, lo_w, hi_x, lo_x, start, stop):
                mm(out_, hi_w, hi_x, start=start, stop=False)
                mm(out_, hi_w, lo_x, start=False, stop=False)
                return mm(out_, lo_w, hi_x, start=False, stop=stop)

            def turn(out_, src, n, parts=P):
                for m in (0, 1):
                    last = tr(out_[0:n, P * m:P * m + P], src[:, m], ident[:])
                return last

            fill = -1
            for l, step, args, who in banks.steps:
                if who == "op":
                    continue
                fill += 1
                if fill >= 8:
                    w_, count = banks.before[fill - 8]
                    pe.wait_ge(emptied[w_], count)
                o = ps[:, fill % 8, :]
                if step == "par_mix":
                    pe.wait_ge(mix_in, 16)
                    last = tr(o[:, 0:DEPTH * 8], rows[0:DEPTH * 8], ident[0:DEPTH * 8, 0:DEPTH * 8])
                elif step == "par":
                    pe.wait_ge(par_in, 16 * 7)
                    last = tr(o[:, 0:R_FINAL + 8], rows, ident[0:R_FINAL + 8, 0:R_FINAL + 8])
                elif step == "fpar":
                    pe.wait_ge(fpar_in, 16)
                    for r in range(DEPTH * 3):
                        last = tr(o[:, 2 * FT * r:2 * FT * (r + 1)], frows[:, r], ident[0:2 * FT, 0:2 * FT])
                elif step == "turn_x":
                    k = args[0]
                    pe.wait_ge(x_in, 64)
                    for t in (0, 1):
                        tr(o[:, P * t:P * t + P], xin[:, t, P * k:P * k + P], ident[:])
                    last = tr(o[:, SEQ:N], xsin[0:NS, P * k:P * k + P], ident[0:NS, 0:NS])
                elif step == "turn_mem":
                    k = args[0]
                    pe.wait_ge(s["mem_scaled"], 1)
                    for t in (0, 1):
                        last = tr(o[:, P * t:P * t + P], memin[:, t, P * k:P * k + P], ident[:])
                elif step == "ssq_final":
                    pe.wait_ge(s["sumsq"], 3 * DEPTH + 1)
                    for t in range(3):
                        n = P if t < 2 else NS
                        last = mm(o[0:n, t:t + 1], acc[:, P * t:P * t + n], ones[:, 0:1], start=True, stop=True)
                elif step == "ssq":
                    pe.wait_ge(s["sumsq"], 3 * l + args[0] + 1)
                    last = mm(o[:, 0:N], ones, acc[:], start=True, stop=True)
                elif step == "in":
                    part, m = args
                    i = [c[0] for c in IN_CHUNKS].index(part)
                    w = chunk(l, "in", i)
                    last = project(o, w, slice(P * m, P * m + P), l, 0)
                elif step == "rope":
                    kind, m = args
                    src = kT[:, m] if kind == "k" else qT[:, m]
                    if kind == "k":
                        wait_emptied(pe, l, "in", "k", m)
                    else:
                        wait_emptied(pe, l, "in", f"q{m // 2}", m % 2)
                    last = mm(o[:, 0:N], perm, src, start=True, stop=True)
                elif step in ("turn_hi", "turn_k", "turn_v", "turn_ke"):
                    t = args[0]
                    cols = slice(P * t, P * t + P) if t < 2 else slice(SEQ, N)
                    n = P if t < 2 else NS
                    if step == "turn_hi":
                        wait_emptied(pe, l, "in", "hi", 1)
                        src = hi
                    elif step == "turn_k":
                        pe.wait_ge(s["roped"], 6 * l + 2)
                        src = kT
                    elif step == "turn_v":
                        wait_emptied(pe, l, "in", "v", 1)
                        src = vt
                    else:
                        pe.wait_ge(s["h_level"], 9 * l + 9)
                        src = hk
                    last = turn(o, src[:, :, cols], n)
                elif step == "cstate_in":
                    pe.wait_ge(cstate_in, 16 * (l + 1))
                    for m in (0, 1):
                        last = tr(o[:, 16 * m:16 * m + 16], cst[0:16, P * m:P * m + P], ident[0:16, 0:16])
                elif step == "cstate_out":
                    pe.wait_ge(s["conv_done"], l + 1)
                    for m in (0, 1):
                        last = tr(o[0:18, P * m:P * m + P], clast[:, m], ident[:])
                elif step == "mk":
                    m = args[0]
                    w = chunk(l, "mk", 0)
                    for k in range(KT_D):
                        pe.wait_ge(s["mg_odd" if k % 2 else "mg_even"], KT_D // 2 * l + k // 2 + 1)
                        last = mm(o[:, 0:N_MEM], w[:, k, P * m:P * m + P], mg[:, k], start=k == 0, stop=k == KT_D - 1)
                elif step == "mv":
                    t = args[0]
                    w = chunk(l, "mv", 0)
                    for k in range(KT_D):
                        last = mm(o[:, 0:256], mg[:, k, P * t:P * t + P], w[:, k], start=k == 0, stop=k == KT_D - 1)
                elif step == "turn_mk":
                    wait_emptied(pe, l, "mk", 1)
                    last = turn(o, mkT[:, :, P * args[0]:P * args[0] + P], P)
                elif step in ("turn_past", "turn_cmem"):
                    b = args[0]
                    rawk_n[b % 2] += 32 if step == "turn_past" else 16
                    pe.wait_ge(rawk_in[b % 2], rawk_n[b % 2])
                    for p in (0, 1):
                        for j in (0, 1):
                            last = tr(o[:, 256 * p + P * j:256 * p + P * j + P], rawk[:, b % 2, j, P * p:P * p + P], ident[:])
                elif step == "ustate_in":
                    if args[0] == 0:
                        pe.wait_ge(ustate_in, 16 * UG * (l + 1))
                    j0, j1 = ((0, 8), (8, UJ))[args[0]]
                    for j in range(j0, j1):
                        last = tr(o[:, 64 * (j - j0):64 * (j - j0) + 64], ustr[:, P * j:P * j + P], ident[0:64, 0:64])
                elif step == "as":
                    g, i = args
                    pe.wait_ge(s["roped"], 6 * l + 6)
                    r = slice(64 * i, 64 * i + 64)
                    mm(o[:, 0:P], qT[r, g, 0:P], kT[r, g // 2, 0:P], start=True, stop=True)
                    last = mm(o[:, P:384], qT[r, g, P:SEQ], kT[r, g // 2, 0:SEQ], start=True, stop=True)
                elif step == "at":
                    g, i = args
                    pe.wait_ge(s["att_p"], 4 * l + g + 1)
                    for j in range(3):
                        last = tr(o[:, P * j:P * j + P], prob[:, i, P * j:P * j + P], ident[:])
                elif step == "ao":
                    g = args[0]
                    wait_emptied(pe, l, "at", g, 1)
                    for i in (0, 1):
                        r = slice(64 * i, 64 * i + 64)
                        kv = slice((g // 2 * 2 + i) * HD, (g // 2 * 2 + i) * HD + HD)
                        mm(o[r, 0:P], vn[:, 0, kv], probT[:, i, 0:P], start=True, stop=True)
                        mm(o[r, P:SEQ], vn[:, 0, kv], probT[:, i, P:SEQ], start=True, stop=False)
                        last = mm(o[r, P:SEQ], vn[:, 1, kv], probT[:, i, SEQ:384], start=False, stop=True)
                elif step == "ss":
                    p = args[0]
                    pe.wait_ge(s["s_q"], 2 * l + p + 1)
                    wait_emptied(pe, l, "turn_past", 7)
                    mm(o[:, 256:N], qa, kT[:, p, SEQ:N], start=True, stop=True)
                    for b in range(8):
                        last = mm(o[:, 0:256], qs[:, P * b:P * b + P], keysT[:, p, b], start=b == 0, stop=b == 7)
                elif step == "st":
                    pe.wait_ge(s["s_p"], 2 * l + args[0] + 1)
                    for j in (0, 1):
                        tr(o[:, P * j:P * j + P], probs[:, P * j:P * j + P], ident[:])
                    last = tr(o[0:NS, 256:384], probs[:, 256:N], ident[:])
                elif step == "so":
                    p = args[0]
                    wait_emptied(pe, l, "st", p)
                    pe.wait_ge(vals_in, 16 * (24 * l + 16))
                    c = slice(P * p, P * p + P)
                    for b in range(8):
                        for j in (0, 1):
                            mm(o[:, 16 * b:16 * b + 16], vals[:, b, j, c], probsT[:, P * j + 16 * b:P * j + 16 * b + 16],
                               start=(b, j) == (0, 0), stop=False, skip_group_check=True)
                    last = mm(o[:, 0:P], vn[0:NS, 2, c], probsT[0:NS, 256:384], start=False, stop=True, skip_group_check=True)
                elif step in ("diag", "diag_s"):
                    i = args[0]
                    pe.wait_ge(s["gates_ready"], l + 1)
                    r = slice(64 * i, 64 * i + 64)
                    for t in (0, 1) if step == "diag" else (2,):
                        for p in (0, 1):
                            n, c = (P, slice(P * t, P * t + P)) if t < 2 else (NS, slice(SEQ, N))
                            at = P * (2 * t + p) if t < 2 else NS * p
                            last = mm(o[0:n, at:at + n], hk[r, p, c], hq[r, p, c], start=True, stop=True)
                elif step == "level":
                    m, i = args
                    pe.wait_ge(s["h_level"], 9 * l + LEVELS.index(m) + 1)
                    r = slice(64 * i, 64 * i + 64)
                    for t in (0, 1, 2) if m < DEC_SEQ else (0, 1):
                        for p in (0, 1):
                            n, c = (P, slice(P * t, P * t + P)) if t < 2 else (NS, slice(SEQ, N))
                            at = 64 * (2 * t + p) if t < 2 else 256 + NS // 2 * p
                            q = hq[r, p, c].rearrange("p (n two m) -> p n two m", two=2, m=m)[:, :, 1]
                            last = mm(o[0:n, at:at + n // 2], hk[r, p, c], q, start=True, stop=True)
                elif step == "cross":
                    pe.wait_ge(s["h_level"], 9 * l + 8)
                    r = slice(64 * args[0], 64 * args[0] + 64)
                    for p in (0, 1):
                        last = mm(o[:, P * p:P * p + P], hk[r, p, 0:P], hq[r, p, P:SEQ], start=True, stop=True)
                elif step == "hstate":
                    wait_emptied(pe, l, "turn_ke", 2)
                    for h in range(4):
                        r = slice(64 * (h % 2), 64 * (h % 2) + 64)
                        c = slice(HD * h, HD * h + HD)
                        for t in (0, 1):
                            last = mm(o[r, 64 * (h // 2):64 * (h // 2) + 64], ke[:, t, c], vh[:, t, c], start=t == 0, stop=t == 1)
                elif step == "hstate_s":
                    pe.wait_ge(s["vexp_ready"], l + 1)
                    for i in (0, 1):
                        h = 2 * args[0] + i
                        last = mm(o[64 * i:64 * i + 64, 0:512], ke[0:NS, 2, HD * h:HD * h + HD],
                                  vexp[:, h].rearrange("p b v -> p (b v)"), start=True, stop=True)
                elif step == "ho":
                    p = args[0]
                    wait_emptied(pe, l, "cross", 1)
                    pe.wait_ge(s0_in, 64 * (l + 1))
                    for i in (0, 1):
                        h = 2 * p + i
                        r = slice(64 * i, 64 * i + 64)
                        c = slice(HD * h, HD * h + HD)
                        mm(o[r, 0:P], vh[:, 0, c], sc[:, i, p], start=True, stop=True)
                        mm(o[r, P:SEQ], vh[:, 0, c], sc[:, i, 4 + p], start=True, stop=False)
                        mm(o[r, P:SEQ], vh[:, 1, c], sc[:, i, 2 + p], start=False, stop=True)
                        for b in range(8):
                            mm(o[r, SEQ + 4 * b:SEQ + 4 * b + 4], s0[r, p, b], hq[r, p, SEQ + 4 * b:SEQ + 4 * b + 4],
                               start=b == 0, stop=False, skip_group_check=True)
                        last = mm(o[r, SEQ:N], vh[0:NS, 2, c], scs[0:NS, i, p], start=False, stop=True, skip_group_check=True)
                elif step == "hn":
                    pe.wait_ge(s["h_square"], 2 * l + args[0] + 1)
                    last = mm(o[:, 0:N], blk, hi[:, args[0]], start=True, stop=True)
                elif step == "out":
                    m = args[0]
                    w = chunk(l, "out", m // 2)
                    wait_emptied(pe, l, "ao", 3)
                    wait_emptied(pe, l, "so", 1)
                    pe.wait_ge(s["conv_done"], l + 1)
                    pe.wait_ge(s["h_out"], 2 * l + 2)
                    c = slice(P * (m % 2), P * (m % 2) + P)
                    for k in range(KT_D):
                        last = mm(o[:, 0:N], w[:, k, c], mix[:, k], start=k == 0, stop=k == KT_D - 1)
                elif step == "xq":
                    last = project(o, chunk(l, "xq", 0), slice(P * args[0], P * args[0] + P), l, 1)
                elif step == "ys":
                    pe.wait_ge(s["y_q"], l + 1)
                    wait_emptied(pe, l, "turn_cmem", 7)
                    for p in (0, 1):
                        for b in range(8):
                            last = mm(o[64 * p:64 * p + 64, 0:256], qs[:, 576 * p + 64 * b:576 * p + 64 * b + 64], keysT[:, p, b],
                                      start=b == 0, stop=b == 7)
                elif step == "xs":
                    h = args[0]
                    wait_emptied(pe, l, "xq", 1)
                    r = slice(64 * (h % 2), 64 * (h % 2) + 64)
                    for q in (0, 1):
                        last = mm(o[:, 256 * q:256 * q + 256], qT[r, h // 2, P * q:P * q + P], mkT[r, h // 2], start=True, stop=True)
                elif step == "xt":
                    h = args[0]
                    pe.wait_ge(s["x_p"], 4 * l + h + 1)
                    for j in (0, 1):
                        for q in (0, 1):
                            last = tr(o[:, 256 * j + P * q:256 * j + P * q + P], prob[:, h % 2, 256 * q + P * j:256 * q + P * j + P], ident[:])
                elif step == "xov":
                    p = args[0]
                    wait_emptied(pe, l, "xt", 2 * p + 1)
                    for i in (0, 1):
                        c = slice(HD * (2 * p + i), HD * (2 * p + i) + HD)
                        for j in (0, 1):
                            last = mm(o[64 * i:64 * i + 64, 0:SEQ], mv[:, j, c], probT[:, i, 256 * j:256 * j + 256], start=j == 0, stop=j == 1)
                elif step == "yt":
                    pe.wait_ge(s["y_p"], l + 1)
                    for j in (0, 1):
                        last = tr(o[:, P * j:P * j + P], probs[:, P * j:P * j + P], ident[:])
                elif step == "yo":
                    p = args[0]
                    wait_emptied(pe, l, "yt")
                    pe.wait_ge(vals_in, 16 * 24 * (l + 1))
                    for b in range(8):
                        for j in (0, 1):
                            c = P * j + 64 * p + 8 * b
                            last = mm(o[:, 8 * b:8 * b + 8], vals[:, b, j, P * p:P * p + P], probsT[:, c:c + 8], start=j == 0, stop=j == 1)
                elif step == "xo":
                    m = args[0]
                    chunk(l, "xo", 0)
                    g = l * len(CHUNKS) + index["xo", 0]
                    w = ring[:, g % SLOTS].rearrange("p (k c) -> p k c", k=2)
                    wait_emptied(pe, l, "yo", 1)
                    wait_emptied(pe, l, "xov", 1)
                    for k in (0, 1):
                        last = mm(o[:, 0:N], w[:, k, P * m:P * m + P], mix[:, k], start=k == 0, stop=k == 1)
                elif step == "up":
                    i, ab = args
                    hi_w, lo_w = parts_of(l, "up", i)
                    c = slice(P * ab, P * ab + P)
                    for k in range(KT_D):
                        pe.wait_ge(s["xg_lo"], KT_D * l + k + 1)
                        last = split_product(o[:, 0:N], hi_w[:, k, c], lo_w[:, k, c], xg_hi[k], xg_lo[:, k], k == 0, k == KT_D - 1)
                elif step == "down":
                    m = args[0]
                    if m % 2:
                        continue
                    pe.wait_ge(emptied[banks.before[fill - 7][0]], banks.before[fill - 7][1])
                    for c3, (k0, k1) in enumerate(DOWN_K):
                        hi_w, lo_w = parts_of(l, "down", m // 2 * 3 + c3)
                        pe.wait_ge(s["h_lo"], FT * l + k1)
                        for i in (0, 1):
                            for k in range(k0, k1):
                                c = slice(P * i, P * i + P)
                                last = split_product(ps[:, (fill + i) % 8, 0:N], hi_w[:, k - k0, c], lo_w[:, k - k0, c],
                                                     hT_hi[:, k], hT_lo[:, k], k == 0, k == FT - 1)
                            if k1 == FT:
                                last.then_inc(filled, 1)
                        if k1 < FT:
                            last.then_inc(s["down_used"], 1)
                    continue
                elif step == "ustate_out":
                    pe.wait_ge(s["u_last"], 2 * FT * (l + 1))
                    for j in range(4 * args[0], min(UJ, 4 * args[0] + 4)):
                        jj = j - 4 * args[0]
                        last = tr(o[0:UG * 18, P * jj:P * jj + P], ulast[:, j].rearrange("p g r -> p (g r)"), ident[:])
                elif step == "y":
                    t, h = args
                    n = P if t < 2 else NS
                    cols = slice(P * t, P * t + P) if t < 2 else slice(SEQ, N)
                    pe.wait_ge(s["xg_tile"], 24 * DEPTH + 4 * h + 4)
                    for k in range(4 * h, 4 * h + 4):
                        last = tr(o[0:n, P * (k - 4 * h):P * (k - 4 * h) + P], XG[:, k, cols], ident[:])
                else:
                    raise ValueError(step)
                last.then_inc(filled, 1)

        @block.vector
        def _(dve):
            v = nc.vector
            drain = dve.drain
            guesses = [0]

            def put(l, step, *args):
                dve.wait_ge(filled, fill_no(l, step, *args))
                return bank(l, step, *args)

            def squares(k, stage):
                drain()
                if k == 0:
                    v.tensor_tensor(acc[:], X[:, k], X[:, k], ALU.mult)
                else:
                    v.tensor_tensor(sqr[:], X[:, k], X[:, k], ALU.mult)
                    drain()
                    last = v.tensor_tensor(acc[:], acc[:], sqr[:], ALU.add)
                    if k == KT_D - 1:
                        last.then_inc(s["sumsq"], 1)

            def residual(l, step, m):
                b_ = put(l, step, m)
                v.tensor_tensor(X[:, m], X[:, m], b_[:, 0:N], ALU.add).then_inc(emptied["D"], 1)
                squares(m, 0)

            def newton(r, x, t):
                v.tensor_tensor(t, r, r, ALU.mult)
                drain()
                v.tensor_tensor(t, t, x, ALU.mult)
                drain()
                v.tensor_scalar(t, t, -0.5, 1.5, ALU.mult, ALU.add)
                drain()
                v.tensor_tensor(r, r, t, ALU.mult)
                drain()

            def rms(l, step, arg, width):
                b_ = put(l, step, arg)
                drain()
                v.tensor_scalar(vv[:], b_[:, 0:N], 1.0 / width, EPS, ALU.mult, ALU.add).then_inc(emptied["D"], 1)
                guesses[0] += 1
                dve.wait_ge(s["rms_guess"], guesses[0])
                newton(Rn[:], vv[:], sqr[:])

            def softmax_scale(rows_, c, tiles):
                pass

            def sampled(x):
                return x.rearrange("p (b s) -> p b s", b=8)

            def padded(x, at=258):
                return x[:, at:at + 48].rearrange("p (b x) -> p b x", x=6)

            for l, step, args, who in banks.emptying_steps:
                if step == "par_mix":
                    v.tensor_copy(par[:, 0:DEPTH * 8], put(l, step)[:, 0:DEPTH * 8]).then_inc(emptied["D"], 1)
                    for k in range(KT_D):
                        squares(k, 0)
                elif step == "par":
                    v.tensor_copy(par[:, DEPTH * 8:], put(l, step)[:, DEPTH * 8:R_FINAL + 8]).then_inc(emptied["D"], 1)
                elif step == "fpar":
                    v.tensor_copy(fpar[:].rearrange("p a b -> p (a b)"),
                                  put(l, step)[:, 0:DEPTH * 3 * 2 * FT]).then_inc(emptied["D"], 1)
                elif step == "bounds":
                    drain()
                    l0 = par[:, par_col(R_LB, 0):par_col(R_LB, 0) + 2]
                    l1 = par[:, par_col(R_LB, 1):par_col(R_LB, 1) + 2]
                    v.tensor_tensor(small[:, 12:14], l0, l1, ALU.max)
                    drain()
                    v.tensor_tensor(small[:, 4:6], l0, small[:, 12:14], ALU.subtract)
                    v.tensor_tensor(small[:, 6:8], l1, small[:, 12:14], ALU.subtract).then_inc(s["lb_d"], 1)
                    dve.wait_ge(s["lb_exp"], 1)
                    v.tensor_tensor(small[:, 12:14], small[:, 8:10], small[:, 10:12], ALU.add)
                    drain()
                    v.reciprocal(small[:, 14:16], small[:, 12:14])
                    drain()
                    v.tensor_tensor(l1, small[:, 10:12], small[:, 14:16], ALU.mult)
                    v.memset(l0, 0.0)
                    drain()
                    v.memset(small[:, 0:2], 1.0)
                    v.tensor_scalar(small[:, 2:4], l1, -1.0, 1.0, ALU.mult, ALU.add)
                    drain()
                elif step == "rest":
                    count, slot, hi_part, tiles = split_chunk(l, *args)
                    dve.wait_ge(w_hi, count)
                    cols = slice(0, LO_DVE * 256)
                    v.tensor_tensor(ring_lo[:, slot, cols], ring[:, slot, cols], hi_part[:, cols].bitcast(F32),
                                    ALU.subtract).then_inc(w_lo_dve, 1)
                elif step == "mem_rms":
                    dve.wait_ge(s["mem_square"], 1)
                    v.tensor_scalar(small[:, 82:84], small[:, 80:82], 1.0 / D_MODEL, EPS, ALU.mult, ALU.add).then_inc(s["mem_v"], 1)
                    dve.wait_ge(s["mem_guess"], 1)
                    drain()
                    newton(small[:, 86:88], small[:, 82:84], small[:, 88:90])
                    for t in (0, 1):
                        last = v.tensor_scalar(memin[:, t], memin[:, t], small[:, 86 + t:87 + t], None, ALU.mult)
                    last.then_inc(s["mem_scaled"], 1)
                elif step == "turn_x":
                    k = args[0]
                    b_ = put(l, step, k)
                    v.tensor_copy(X[:, k], b_[:, 0:N]).then_inc(emptied["D"], 1)
                elif step == "ssq":
                    if l and l < DEPTH and args[0] == 0:
                        dve.wait_ge(stored, 16 * l * STORES_LAYER)
                    if args[0] == 2:
                        dve.wait_ge(stored, 16 * (l * STORES_LAYER + STORES_MIXER))
                    rms(l, step, args[0], D_MODEL)
                elif step == "ssq_final":
                    b_ = put(l, step)
                    for n, c in ((P, slice(0, 2)), (NS, slice(2, 3))):
                        last = v.tensor_scalar(small[0:n, 88 + c.start:88 + c.stop], b_[0:n, c], 1.0 / D_MODEL, EPS,
                                               ALU.mult, ALU.add)
                    last.then_inc(emptied["D"], 1)
                    dve.wait_ge(s["y_guess"], 1)
                    for n, c in ((P, slice(0, 2)), (NS, slice(2, 3))):
                        newton(small[0:n, 92 + c.start:92 + c.stop], small[0:n, 88 + c.start:88 + c.stop],
                               small[0:n, 80 + c.start:80 + c.stop])
                    v.memset(small[:, 95:96], 0.0).then_inc(s["y_rms"], 1)
                elif step == "y":
                    t, h = args
                    if t == 1:
                        v.tensor_scalar(yrow[:, t, 512 * h:512 * h + 512], put(l, step, t, h), small[:, 92 + t:93 + t], None,
                                        ALU.mult).then_inc(emptied["D"], 1)
                elif step == "in":
                    part, m = args
                    b_ = put(l, step, *args)
                    dst = {"hf": e1, "hq": e2, "hi": hi, "k": kT, "q0": qT, "q1": qT[:, 2:4], "v": vt, "cc": yc,
                           "cb": cb, "hg": hgs}
                    if part == "ch":
                        v.tensor_tensor(sqr[:], b_[:, 0:N], Rn[:], ALU.mult).then_inc(emptied["D"], 1)
                        drain()
                        v.tensor_tensor(uc[:, m, 2:258], sqr[:, 0:SEQ], yc[:, m, 0:SEQ], ALU.mult)
                        v.tensor_tensor(padded(uc[:, m])[:, :, 2:6], sampled(sqr[:, SEQ:N]), sampled(yc[:, m, SEQ:N]), ALU.mult)
                        drain()
                    else:
                        v.tensor_tensor(dst[part][:, m, 0:N], b_[:, 0:N], Rn[:], ALU.mult).then_inc(emptied["D"], 1)
                elif step == "rope":
                    kind, m = args
                    x = kT[:, m] if kind == "k" else qT[:, m]
                    dve.wait_ge(con_in, 32)
                    b_ = put(l, step, *args)
                    v.tensor_tensor(sqr[:], b_[:, 0:N], con[:, C_SIN:C_SIN + N], ALU.mult).then_inc(emptied["D"], 1)
                    v.tensor_tensor(x, x, con[:, C_COS:C_COS + N], ALU.mult)
                    drain()
                    v.tensor_tensor(x, x, sqr[:], ALU.add).then_inc(s["roped"], 1)
                    drain()
                elif step == "gates":
                    dve.wait_ge(s["sigmoids"], l + 1)
                    for m in (0, 1):
                        lb = par[:, par_col(R_LB, l, m):par_col(R_LB, l, m) + 1]
                        oml = small[:, 2 * l + m:2 * l + m + 1]
                        v.tensor_scalar(hf[:, m], hf[:, m], oml, lb, ALU.mult, ALU.add)
                        v.tensor_scalar(hk[:, m], hk[:, m], oml, None, ALU.mult)
                    v.tensor_tensor(hq, hq, e2, ALU.mult).then_inc(s["gates_ready"], 1)
                elif step == "cstate_in":
                    b_ = put(l, step)
                    v.memset(uc[:, :, 0:2], 0.0)
                    for m in (0, 1):
                        last = v.tensor_copy(padded(uc[:, m])[:, :, 0:2], b_[:, 16 * m:16 * m + 16].rearrange("p (b w) -> p b w", w=2))
                    last.then_inc(emptied["D"], 1)
                elif step == "conv":
                    drain()
                    c0 = par_col(R_CONV, l)
                    for m in (0, 1):
                        v.tensor_copy(clast[:, m, 0:2], uc[:, m, 256:258])
                        v.tensor_copy(clast[:, m, 2:18].rearrange("p (b w) -> p b w", w=2), padded(uc[:, m])[:, :, 4:6])
                        v.tensor_scalar(yc[:, m, 0:304], uc[:, m, 0:304], par[:, c0 + m:c0 + m + 1], None, ALU.mult)
                    for w in (1, 2):
                        drain()
                        for m in (0, 1):
                            c = c0 + 2 * w + m
                            v.scalar_tensor_tensor(out=yc[:, m, 0:304], in0=uc[:, m, w:304 + w], scalar=par[:, c:c + 1],
                                                   in1=yc[:, m, 0:304], op0=ALU.mult, op1=ALU.add)
                    drain()
                    for m in (0, 1):
                        v.tensor_tensor(mix[:, 6 + m, 0:SEQ], cb[:, m, 0:SEQ], yc[:, m, 0:SEQ], ALU.mult)
                        last = v.tensor_tensor(sampled(mix[:, 6 + m, SEQ:N]), sampled(cb[:, m, SEQ:N]),
                                               padded(yc[:, m], 258)[:, :, 0:4], ALU.mult)
                    last.then_inc(s["conv_done"], 1)
                elif step == "as":
                    g, i = args
                    b_ = put(l, step, g, i)
                    if g:
                        pe_done(dve, l, "at", g - 1, i)
                    c = 16 + 16 * (g % 2) + 2 * i
                    v.tensor_tensor(prob[:, i, 0:384], b_[:, 0:384], con[:, C_MASKA:C_MASKA + 384], ALU.add).then_inc(emptied["D"], 1)
                    drain()
                    v.tensor_reduce(small[:, c:c + 1], prob[:, i, 0:P], AX_X, ALU.max)
                    v.tensor_reduce(small[:, c + 1:c + 2], prob[:, i, P:384], AX_X, ALU.max)
                    drain()
                    v.tensor_scalar(small[:, c + 4:c + 6], small[:, c:c + 2], -SCALE, None, ALU.mult).then_inc(s["att_max"], 1)
                elif step == "anorm":
                    g = args[0]
                    c = 16 + 16 * (g % 2)
                    dve.wait_ge(s["att_exp"], 8 * l + 2 * g + 2)
                    v.reciprocal(small[:, c + 12:c + 16], small[:, c + 8:c + 12])
                    drain()
                    for i in (0, 1):
                        v.tensor_scalar(prob[:, i, 0:P], prob[:, i, 0:P], small[:, c + 12 + 2 * i:c + 13 + 2 * i], None, ALU.mult)
                        last = v.tensor_scalar(prob[:, i, P:384], prob[:, i, P:384], small[:, c + 13 + 2 * i:c + 14 + 2 * i], None, ALU.mult)
                    last.then_inc(s["att_p"], 1)
                elif step == "ss":
                    b_ = put(l, step, *args)
                    if args[0]:
                        pe_done(dve, l, "st", 0)
                    v.tensor_copy(probs[:, 0:256], b_[:, 0:256])
                    v.tensor_tensor(probs[:, 256:N], b_[:, 256:N], con[:, C_MASKS:C_MASKS + NS], ALU.add).then_inc(emptied["D"], 1)
                    drain()
                    v.tensor_reduce(small[:, 48:49], probs, AX_X, ALU.max)
                    drain()
                    v.tensor_scalar(small[:, 49:50], small[:, 48:49], -SCALE, None, ALU.mult).then_inc(s["s_max"], 1)
                elif step == "snorm":
                    dve.wait_ge(s["s_exp"], 2 * l + args[0] + 1)
                    v.reciprocal(small[:, 51:52], small[:, 50:51])
                    drain()
                    v.tensor_scalar(probs, probs, small[:, 51:52], None, ALU.mult).then_inc(s["s_p"], 1)
                elif step == "diag":
                    i = args[0]
                    b_ = put(l, step, i)
                    if i == 0:
                        dve.wait_ge(s["zeros"], l + 1)
                        dve.wait_ge(con_in, 32)
                    v.copy_predicated(sc[:, i, 0:4], mask[:, 0:P].unsqueeze(1).broadcast_to([P, 4, P]),
                                      b_.rearrange("p (x c) -> p x c", x=4)).then_inc(emptied["D"], 1)
                elif step == "diag_s":
                    i = args[0]
                    b_ = put(l, step, i)
                    v.copy_predicated(scs[0:NS, i], mask[0:NS, 0:NS].unsqueeze(1).broadcast_to([NS, 2, NS]),
                                      b_[0:NS, 0:2 * NS].rearrange("p (x c) -> p x c", x=2)).then_inc(emptied["D"], 1)
                    if i:
                        v.tensor_tensor(hq, hq, hf, ALU.mult).then_inc(s["h_level"], 1)
                elif step == "level":
                    m, i = args
                    b_ = put(l, step, m, i)
                    drain()

                    def place(dst, n, x, src):
                        dst = dst.rearrange("p (n two m) -> p n two m", two=2, m=m)[:, :, 1]
                        msk = mask[0:n, M_LEVEL[m]:M_LEVEL[m] + n // 2].unsqueeze(1).broadcast_to([n, x, n // 2])
                        return v.copy_predicated(dst.rearrange("p (x n) m -> p x n m", x=x),
                                                 msk.rearrange("p x (n m) -> p x n m", m=m),
                                                 src.rearrange("p (x n m) -> p x n m", x=x, m=m))
                    if m < DEC_SEQ:
                        place(scs[0:NS, i].rearrange("p x t -> p (x t)"), NS, 2, b_[0:NS, 256:256 + NS])
                    place(sc[:, i, 0:4].rearrange("p x t -> p (x t)"), P, 4, b_[:, 0:256]).then_inc(emptied["D"], 1)
                elif step == "merge":
                    m = args[0]
                    width = N if m < DEC_SEQ else SEQ
                    nb = width // m
                    odd = (LEVELS + [P]).index(m) % 2
                    tot, new = (e2, hf) if odd else (hf, e2)
                    drain()
                    pair = tot[:, :, 0:nb].rearrange("p k (n two) -> p k n two", two=2)
                    shape = [P, 2, nb // 2, m]
                    q = hq[:, :, 0:width].rearrange("p k (n two m) -> p k n two m", two=2, m=m)[:, :, :, 1]
                    k = hk[:, :, 0:width].rearrange("p k (n two m) -> p k n two m", two=2, m=m)[:, :, :, 0]
                    if m < P:
                        v.tensor_tensor(q, q, pair[:, :, :, 0:1].broadcast_to(shape), ALU.mult)
                        v.tensor_tensor(new[:, :, 0:nb // 2], pair[:, :, :, 0], pair[:, :, :, 1], ALU.mult)
                    v.tensor_tensor(k, k, pair[:, :, :, 1:2].broadcast_to(shape), ALU.mult).then_inc(s["h_level"], 1)
                    if m == DEC_SEQ // 2:
                        drain()
                        v.tensor_copy(t4, new[:, :, SEQ // 4:N // 4])
                elif step == "cross":
                    b_ = put(l, step, *args)
                    v.tensor_copy(sc[:, args[0], 4:6], b_[:, 0:256].rearrange("p (x c) -> p x c", x=2)).then_inc(emptied["D"], 1)
                elif step == "hstate_s":
                    k = args[0]
                    if k == 0:
                        dve.wait_ge(s0_in, 64 * (l + 1))
                        drain()
                    v.tensor_tensor(newS[:, k], s0[:, k], t4[:, k].unsqueeze(2).broadcast_to([P, 8, HD]), ALU.mult)
                    b_ = put(l, step, k)
                    drain()
                    v.tensor_tensor(newS[:, k], newS[:, k], b_.rearrange("p (b v) -> p b v", b=8), ALU.add).then_inc(emptied["D"], 1)
                elif step == "ho":
                    k = args[0]
                    b_ = put(l, step, k)
                    v.tensor_copy(e2[:, k], b_[:, 0:N]).then_inc(emptied["D"], 1)
                    drain()
                    v.tensor_tensor(hi[:, k], e2[:, k], e2[:, k], ALU.mult).then_inc(s["h_square"], 1)
                elif step == "hn":
                    k = args[0]
                    if k == 0:
                        dve.wait_ge(s["silu_gate_in"], l + 1)
                        v.tensor_tensor(hgs, hgs, e1, ALU.mult)
                    rms(l, step, k, HD)
                    v.tensor_tensor(e2[:, k], e2[:, k], Rn[:], ALU.mult)
                    drain()
                    c = par_col(R_NORM, l, k)
                    v.scalar_tensor_tensor(out=mix[:, 4 + k], in0=e2[:, k], scalar=par[:, c:c + 1], in1=hgs[:, k],
                                           op0=ALU.mult, op1=ALU.mult).then_inc(s["h_out"], 1)
                elif step in ("out", "xo", "down"):
                    residual(l, step, args[0])
                elif step == "xq":
                    b_ = put(l, step, *args)
                    v.tensor_tensor(qT[:, args[0]], b_[:, 0:N], Rn[:], ALU.mult).then_inc(emptied["D"], 1)
                elif step == "ys":
                    b_ = put(l, step)
                    v.tensor_reduce(small[:, 52:53], b_[:, 0:256], AX_X, ALU.max)
                    drain()
                    v.tensor_scalar(small[:, 53:54], small[:, 52:53], -SCALE, None, ALU.mult).then_inc(s["y_max"], 1)
                elif step == "ynorm":
                    wait_emptied(dve, l, "ys")
                    v.reciprocal(small[:, 55:56], small[:, 54:55])
                    drain()
                    v.tensor_scalar(probs[:, 0:256], probs[:, 0:256], small[:, 55:56], None, ALU.mult).then_inc(s["y_p"], 1)
                elif step == "xs":
                    h = args[0]
                    c = 60 + 8 * (h % 2)
                    b_ = put(l, step, h)
                    v.tensor_reduce(small[:, c:c + 2], b_.rearrange("p (q m) -> p q m", q=2), AX_X, ALU.max)
                    drain()
                    v.tensor_scalar(small[:, c + 2:c + 4], small[:, c:c + 2], -SCALE, None, ALU.mult).then_inc(s["x_max"], 1)
                elif step == "xnorm":
                    h = args[0]
                    c = 60 + 8 * (h % 2)
                    wait_emptied(dve, l, "xs", h)
                    v.reciprocal(small[:, c + 6:c + 8], small[:, c + 4:c + 6])
                    drain()
                    for q in (0, 1):
                        t = prob[:, h % 2, 256 * q:256 * q + 256]
                        last = v.tensor_scalar(t, t, small[:, c + 6 + q:c + 7 + q], None, ALU.mult)
                    last.then_inc(s["x_p"], 1)
                elif step == "up":
                    i, ab = args
                    b_ = put(l, step, i, ab)
                    u = uab[i % 2][ab]
                    if i >= 2:
                        dve.wait_ge(s["u_c0"], 2 * FT * l + 2 * i + ab - 3)
                        dve.wait_ge(s["u_last"], 2 * FT * l + 2 * i + ab - 3)
                    v.tensor_tensor(u[:, 2:258], b_[:, 0:SEQ], Rn[:, 0:SEQ], ALU.mult)
                    v.tensor_tensor(padded(u)[:, :, 2:6], sampled(b_[:, SEQ:N]), sampled(Rn[:, SEQ:N]), ALU.mult).then_inc(emptied["D"], 1)
                elif step == "convolve":
                    i = args[0]
                    dve.wait_ge(s["u_c0"], 2 * FT * l + 2 * i + 2)
                    y = yab[i % 2]
                    for w in (1, 2):
                        for ab in (0, 1):
                            c = FT * ab + i
                            last = v.scalar_tensor_tensor(out=y[ab][:, 0:304], in0=uab[i % 2][ab][:, w:304 + w], scalar=fpar[:, 3 * l + w, c:c + 1],
                                                          in1=y[ab][:, 0:304], op0=ALU.mult, op1=ALU.add)
                            if w == 2:
                                last.then_inc(s[("u_ya", "u_conv")[ab]], 1)
                        drain()
                elif step == "gate":
                    i = args[0]
                    y = yab[i % 2]
                    dve.wait_ge(s["u_silu"], FT * l + i + 1)
                    v.tensor_tensor(hT[:, i, 0:SEQ], sil[i % 2][:, 0:SEQ], y[1][:, 0:SEQ], ALU.mult)
                    v.tensor_tensor(sampled(hT[:, i, SEQ:N]), padded(sil[i % 2])[:, :, 0:4], padded(y[1])[:, :, 0:4],
                                    ALU.mult).then_inc(s["h_tile"], 1)


_OUTS = [(1, SEQ, D_MODEL), (DEC_BATCH, DEC_SEQ, D_MODEL), (DEPTH, 1, SEQ, 4, HD), (DEPTH, 1, SEQ, 4, HD),
         (DEPTH, DEC_BATCH, DEC_SEQ, 4, HD), (DEPTH, DEC_BATCH, DEC_SEQ, 4, HD), (DEPTH, 1, 4, HD, HD),
         (DEPTH, DEC_BATCH, 4, HD, HD), (DEPTH, 1, 2, 256), (DEPTH, DEC_BATCH, 2, 256), (DEPTH, 1, 2, 2 * D_FF),
         (DEPTH, DEC_BATCH, 2, 2 * D_FF), (DEPTH, 1, N_MEM, 4, HD), (DEPTH, 1, N_MEM, 4, HD)]


def kernel(**inputs):
    import numpy as _np
    import concourse.bacc as _bacc
    from concourse import mybir as _mybir
    from concourse.bass_utils import run_bass_kernel_spmd as _run

    nc = _bacc.Bacc("TRN2", target_bir_lowering=False, num_devices=1)
    const_f, const_i = constants()
    arrays, aps = {}, {}
    for name, value in {**inputs, "const_f": const_f, "const_i": const_i}.items():
        value = _np.ascontiguousarray(value)
        arrays[f"in_{name}"] = value
        aps[name] = nc.dram_tensor(f"in_{name}", value.shape, _mybir.dt.from_np(value.dtype), kind="ExternalInput").ap()
    outs = [nc.dram_tensor(f"out_{i}", shape, _mybir.dt.float32, kind="ExternalOutput").ap()
            for i, shape in enumerate(_OUTS)]
    decoder_kernel(nc, aps, outs)
    r = _run(nc, [arrays], core_ids=[0])
    return tuple(r.results[0][f"out_{i}"] for i in range(len(_OUTS)))
```

```python
from contextlib import ExitStack

import concourse.bass as bass
import numpy as np
from concourse import mybir

ALU = mybir.AluOpType
ACT = mybir.ActivationFunctionType
AX_X = mybir.AxisListType.X
F32 = mybir.dt.float32
F32R = mybir.dt.float32r
I32 = mybir.dt.int32

P = 128
D_MODEL, SEQ, DEPTH = 1024, 256, 2
DEC_BATCH, DEC_SEQ, PAGE, N_PAGES = 8, 4, 128, 2
HD = 64
N_MEM = 256
D_FF = 2816
EPS = 1e-6
SCALE = HD ** -0.5
NS = DEC_BATCH * DEC_SEQ
N = SEQ + NS
KT_D = D_MODEL // P
FT = D_FF // P
UG = 4
UJ = 2 * FT // UG
BIG = 1e30

W_Q, W_K, W_V, W_HQ, W_HF, W_HI, W_HG, W_CB, W_CC, W_CH = (
    0, 512, 768, 1024, 1280, 1536, 1792, 2048, 2304, 2560)
IN_CHUNKS = [("hf", W_HF), ("hq", W_HQ), ("hi", W_HI), ("k", W_K), ("q0", W_Q), ("q1", W_Q + 256),
             ("v", W_V), ("cc", W_CC), ("ch", W_CH), ("cb", W_CB), ("hg", W_HG)]

PIECES = ([("in", (part, m)) for part, _ in IN_CHUNKS for m in (0, 1)]
          + [("mk", (0,)), ("mk", (1,)), ("mv", (1,)), ("mv", (1,))]
          + [("out", (m,)) for m in range(8)] + [("xq", (0,)), ("xq", (1,))])
IN_PIECES = 2 * len(IN_CHUNKS)
P_MK, P_MV, P_OUT, P_XQ = IN_PIECES, IN_PIECES + 2, IN_PIECES + 4, IN_PIECES + 12
SPLIT_PIECES = IN_PIECES + 8

CHUNKS = [("xo", 0)] + [("up", n) for n in range(FT)] + [("down", n) for n in range(12)]
SLOTS = 4
assert len(CHUNKS) % SLOTS == 3 and len(PIECES) % 4 == 0


def slot_of(n):
    return (n + 3) % SLOTS


MIXED_ORDER = [6, 7, 4, 5, 0, 1, 2, 3]
DOWN_K = [(0, 8), (8, 16), (16, 22)]

LO_DVE = {"in": 8, "out": 8, "up": 4, "down": 3}
LEVELS = [1, 2, 4, 8, 16, 32, 64]

C_IDENT, C_PERM, C_ONES, C_BLK, C_COS, C_SIN = 0, 128, 256, 384, 512, 512 + N
C_MASKA = C_SIN + N
C_MASKS = C_MASKA + 384
C_SEL = C_MASKS + NS
C_N = C_SEL + DEC_BATCH
M_LEVEL = {m: P + 64 * i for i, m in enumerate(LEVELS)}
M_N = P + 64 * len(LEVELS)


def constants():
    f = np.zeros((P, C_N), np.float32)
    p = np.arange(P)
    f[:, C_IDENT:C_IDENT + P] = np.eye(P)
    half = HD // 2
    for d in range(P):
        if d % HD < half:
            f[d + half, C_PERM + d] = -1.0
        else:
            f[d - half, C_PERM + d] = 1.0
    f[:, C_ONES:C_ONES + P] = 1.0
    f[:, C_BLK:C_BLK + P] = (p[:, None] // HD == p[None, :] // HD)
    pos = np.concatenate([np.arange(SEQ), SEQ + np.tile(np.arange(DEC_SEQ), DEC_BATCH)]).astype(np.float32)
    inv = np.float32(10000.0) ** (-np.arange(half, dtype=np.float32) / np.float32(half))
    ang = (pos[None, :] * inv[p % half][:, None]).astype(np.float32).astype(np.float64)
    f[:, C_COS:C_COS + N] = np.cos(ang)
    f[:, C_SIN:C_SIN + N] = np.sin(ang)
    q = np.arange(P)[:, None]
    k = np.arange(P)[None, :]
    causal = np.where(k <= q, 0.0, -BIG)
    f[:, C_MASKA:C_MASKA + P] = causal
    f[:, C_MASKA + 2 * P:C_MASKA + 3 * P] = causal
    row = np.arange(P)[:, None]
    t = np.arange(NS)[None, :]
    f[:, C_MASKS:C_MASKS + NS] = np.where((t // 4 == row // 16) & (t % 4 <= row % 4), 0.0, -BIG)
    f[:NS, C_SEL:C_SEL + DEC_BATCH] = (np.arange(NS)[:, None] // 4 == np.arange(DEC_BATCH)[None, :])
    m = np.zeros((P, M_N), np.int32)
    m[:, :P] = np.eye(P)
    for h in LEVELS:
        c = np.arange(64)[None, :]
        s = np.arange(P)[:, None]
        m[:, M_LEVEL[h]:M_LEVEL[h] + 64] = (s // (2 * h) == c // h) & (s % (2 * h) < h)
    return f, m


R_MIX, R_XATTN, R_MEM, R_FFN = (0, 8), (16, 8), (32, 8), (48, 8)
R_LB, R_NORM, R_CONV = (64, 2), (68, 2), (72, 6)
R_FINAL = 84


def par_col(r, l, k=0):
    return r[0] + l * r[1] + k


def layer_schedule(l):
    s = []

    def a(who, step, *args):
        s.append((step, args, who))

    def level(m):
        a("D", "level", m, 0)
        a("D", "level", m, 1)
        a("op", "merge", m)

    def scores(g):
        a("D", "as", g, 0)
        a("D", "as", g, 1)

    def turn_probs(g):
        a("A", "at", g, 0)
        a("A", "at", g, 1)

    def project(part, m):
        p = 2 * [c[0] for c in IN_CHUNKS].index(part) + m
        a("D", "in", part, m)
        if p == 1:
            a("D", "ssq", 0)
        if p + 3 < IN_PIECES:
            a("op", "round", "in", p + 3, l)
        if 3 <= p + 2 < IN_PIECES:
            a("op", "rest", "in", p + 2, l)

    first = l == 0
    a("op", "round", "in", 2, l)
    a("op", "rest", "in", 2, l)
    project("hf", 0)
    project("hf", 1)
    if first:
        a("D", "par")
        a("D", "fpar")
        a("op", "bounds")
    project("hq", 0)
    a("A", "turn_past", 0)
    project("hq", 1)
    project("hi", 0)
    a("A", "turn_past", 1)
    project("hi", 1)
    a("op", "gates")
    if first:
        a("op", "mem_rms")
    project("k", 0)
    for t in range(3):
        a("A", "turn_hi", t)
    project("k", 1)
    a("A", "turn_past", 2)
    for i in (0, 1):
        a("D", "diag", i)
    for i in (0, 1):
        a("D", "diag_s", i)
    project("q0", 0)
    project("q0", 1)
    if first:
        for k in range(KT_D // 2):
            a("A", "turn_mem", k)
    a("A", "turn_past", 3)
    a("D", "rope", "k", 0)
    a("D", "rope", "k", 1)
    level(1)
    project("q1", 0)
    if first:
        for k in range(KT_D // 2, KT_D):
            a("A", "turn_mem", k)
    for t in range(3):
        a("A", "turn_k", t)
    project("q1", 1)
    a("A", "turn_past", 4)
    a("D", "rope", "q", 0)
    a("D", "rope", "q", 1)
    level(2)
    project("v", 0)
    a("D", "rope", "q", 2)
    project("v", 1)
    a("A", "turn_past", 5)
    a("D", "rope", "q", 3)
    a("op", "sq", 0)
    level(4)
    a("D", "cstate_in")
    project("cc", 0)
    for t in range(3):
        a("A", "turn_v", t)
    scores(0)
    project("cc", 1)
    a("A", "turn_past", 6)
    level(8)
    a("op", "anorm", 0)
    project("ch", 0)
    turn_probs(0)
    scores(1)
    project("ch", 1)
    a("A", "ao", 0)
    a("A", "turn_past", 7)
    level(16)
    a("op", "anorm", 1)
    project("cb", 0)
    turn_probs(1)
    scores(2)
    project("cb", 1)
    a("A", "ao", 1)
    level(32)
    a("op", "anorm", 2)
    project("hg", 0)
    turn_probs(2)
    scores(3)
    project("hg", 1)
    a("A", "ao", 2)
    level(64)
    a("op", "anorm", 3)
    a("D", "ss", 0)
    turn_probs(3)
    a("D", "cross", 0)
    a("D", "cross", 1)
    a("op", "merge", P)
    a("A", "mk", 0)
    a("op", "snorm", 0)
    a("A", "ao", 3)
    for t in range(3):
        a("A", "turn_ke", t)
    a("op", "sq", 1)
    a("op", "conv")
    a("A", "mk", 1)
    a("A", "st", 0)
    a("D", "ho", 0)
    a("D", "ho", 1)
    a("D", "ss", 1)
    a("op", "snorm", 1)
    a("D", "hn", 0)
    a("D", "hn", 1)
    a("A", "so", 0)
    a("A", "st", 1)
    a("A", "mv", 0)
    for k in (6, 7, 4, 5, 0, 1):
        a("op", "split_mixed", k)
    a("A", "mv", 1)
    a("op", "round", "out", 0, l)
    a("op", "rest", "out", 0, l)
    a("A", "so", 1)
    for k in (2, 3):
        a("op", "split_mixed", k)
    a("op", "round", "out", 1, l)
    a("op", "rest", "out", 1, l)
    a("A", "hstate")
    for m in range(8):
        a("D", "out", m)
        if m + 2 < 8:
            a("op", "round", "out", m + 2, l)
            a("op", "rest", "out", m + 2, l)
        if m < 6:
            a("A", "turn_cmem", m)
        if m == 6:
            a("D", "hstate_s", 0)
            a("D", "hstate_s", 1)
    a("D", "xq", 0)
    a("D", "xq", 1)
    a("D", "ssq", 1)
    a("op", "yq")
    a("A", "turn_cmem", 6)
    for t in (0, 1):
        a("A", "turn_mk", t)
    a("A", "cstate_out")
    a("A", "turn_cmem", 7)
    a("A", "ustate_in", 0)
    a("A", "ustate_in", 1)
    a("A", "xs", 0)
    a("A", "xs", 1)
    a("op", "xnorm", 0)
    a("A", "ys")
    a("op", "xnorm", 1)
    a("A", "xt", 0)
    a("A", "xt", 1)
    a("A", "xs", 2)
    a("op", "ynorm")
    a("A", "xov", 0)
    a("A", "yt")
    a("A", "xs", 3)
    a("op", "xnorm", 2)
    a("op", "xnorm", 3)
    a("op", "round", "up", 0, l)
    a("op", "rest", "up", 0, l)
    a("A", "yo", 0)
    a("A", "xt", 2)
    a("A", "xt", 3)
    a("op", "round", "up", 1, l)
    a("op", "rest", "up", 1, l)
    a("A", "yo", 1)
    a("A", "xov", 1)
    a("op", "round", "up", 2, l)
    for m in range(8):
        a("D", "xo", m)
    a("op", "pads", 0)
    a("op", "rest", "up", 2, l)
    for i in range(FT):
        ahead = ("up", i + 2) if i + 2 < FT else ("down", i + 2 - FT)
        if i:
            a("op", "round", *ahead, l)
        a("D", "up", i, 0)
        if i:
            a("op", "convolve", i - 1)
        a("D", "up", i, 1)
        if i + 1 < FT:
            a("op", "pads", i + 1)
        if i:
            a("op", "gate", i - 1)
            a("op", "rest", *ahead, l)
        if i == 0:
            a("D", "ssq", 2)
    a("op", "convolve", FT - 1)
    a("op", "gate", FT - 1)
    a("op", "round", "down", 2, l)
    a("op", "rest", "down", 2, l)
    for m in range(0, 8, 2):
        for c in range(3 * m // 2 + 3, min(3 * m // 2 + 6, 12)):
            a("op", "round", "down", c, l)
            a("op", "rest", "down", c, l)
        if m == 6 and l + 1 < DEPTH:
            for p in (0, 1):
                a("op", "round", "in", p, l + 1)
                a("op", "rest", "in", p, l + 1)
        a("D", "down", m)
        a("D", "down", m + 1)
        if m < 6:
            a("A", "ustate_out", m // 2)
    return s


def emptied_order(steps):
    out = []
    for step in steps:
        at = len(out)
        if step[1] == "ssq_final":
            at -= 3
        if step[1] == "ssq" and step[0] < DEPTH:
            while out[at - 1][1] in ("in", "xq", "up", "round", "pads"):
                at -= 1
        out.insert(at, step)
    return out


PROLOGUE = [("turn_x", (k,), "D") for k in range(KT_D)] + [
    ("round", ("in", 0, 0), "op"), ("par_mix", (), "D"), ("rest", ("in", 0, 0), "op"), ("x_split", (), "op"),
    ("round", ("in", 1, 0), "op"), ("rest", ("in", 1, 0), "op"), ("x_squares", (), "op")]
EPILOGUE = ([("y", (t, 0), "AD"[t % 2]) for t in range(3)] + [("ssq_final", (), "D")]
            + [("y", (t, 1), "AD"[t % 2]) for t in range(3)])


class Banks:

    def __init__(self):
        self.steps = [(-1, *x) for x in PROLOGUE]
        for l in range(DEPTH):
            self.steps += [(l, *x) for x in layer_schedule(l)]
        self.steps += [(DEPTH, *x) for x in EPILOGUE]
        self.emptying_steps = emptied_order(self.steps)
        fills = [x for x in self.steps if x[3] != "op"]
        self.of = {x[:3]: n for n, x in enumerate(fills)}
        emptied = {}
        for who, steps in (("A", self.steps), ("D", self.emptying_steps)):
            own = [x for x in steps if x[3] == who]
            emptied.update({x[:3]: (who, n + 1) for n, x in enumerate(own)})
        self.before = [emptied[x[:3]] for x in fills]


def decoder_kernel(nc, a, out):
    (y_prompt, y_sample, k_prompt, v_prompt, k_sample, v_sample, hgrn_prompt, hgrn_sample,
     conv_prompt, conv_sample, ffn_prompt, ffn_sample, mem_k_prompt, mem_v_prompt) = out
    banks = Banks()
    with ExitStack() as ctx:
        def sb(name, *shape, dt=F32):
            return ctx.enter_context(nc.sbuf_tensor(name, list(shape), dt))

        def sem(name):
            return ctx.enter_context(nc.semaphore(name))

        ps = ctx.enter_context(nc.psum_tensor("banks", [P, 8, 512], F32))
        shared = {"XG": (KT_D, N), "ring": (SLOTS, 2048), "keysT": (2, DEC_BATCH, 256),
                  "vals": (DEC_BATCH, 2, 256), "rawk": (2, 2, 256), "mix": (KT_D, N), "phase": (18600,)}
        with ExitStack() as plain:
            as_f32 = {n: plain.enter_context(nc.sbuf_tensor(n, [P, *shape], F32)) for n, shape in shared.items()}
        rounded = {n: sb(n + "_r", P, *shape, dt=F32R) for n, shape in shared.items()}
        XG = as_f32["XG"]
        ring = as_f32["ring"]
        keysT = as_f32["keysT"]
        vals = as_f32["vals"]
        rawk = as_f32["rawk"]
        mix = as_f32["mix"]
        phase = as_f32["phase"]
        con = sb("con", P, C_N)
        mask = sb("mask", P, M_N, dt=I32)
        pages = sb("pages", 1, DEC_BATCH * N_PAGES, dt=I32)
        X = sb("X", P, KT_D, N)
        acc = sb("acc", P, N)
        sqr = sb("sqr", P, N)
        memT = sb("memT", P, KT_D, N_MEM)
        mkT = sb("mkT", P, 2, N_MEM)
        mv = sb("mv", P, 2, 256)
        par = sb("par", P, R_FINAL + 8)
        fpar = sb("fpar", P, DEPTH * 3, 2 * FT)
        Rn = sb("Rn", P, N)
        vv = sb("vv", P, N)
        small = sb("small", P, 96)
        ustr = sb("ustr", UG * 16, UJ * P)
        ust = sb("ust", P, UJ, UG, 16)
        used = [0]

        def ph(*shape, parts=P):
            n = int(np.prod(shape))
            v = phase[0:parts, used[0]:used[0] + n]
            used[0] += n
            assert used[0] <= 18600, used[0]
            if len(shape) > 1:
                names = "abcd"[:len(shape)]
                v = v.rearrange(f"p ({' '.join(names)}) -> p {' '.join(names)}", **dict(zip(names, shape)))
            return v

        prob = ph(2, 512)
        probT = ph(2, 512)
        at_q = used[0]
        qT = ph(4, N)
        kT = ph(2, N)
        sc = ph(2, 6, P)
        scs = ph(2, 2, NS)
        hf = ph(2, N)
        hq = ph(2, N)
        hk = ph(2, N)
        hi = ph(2, N)
        at_g = used[0]
        hgs = ph(2, N)
        e1 = ph(2, N)
        e2 = ph(2, N)
        vh = ph(3, 256)
        vn = ph(3, 256)
        turned = ph(3, 256)
        ke = ph(3, 256)
        s0 = ph(2, 8, HD)
        at_cb = used[0]
        cb = ph(2, N)
        uc = ph(2, 306)
        yc = ph(2, 306)
        qs = ph(8 * 144)
        qa = ph(P)
        probs = ph(N)
        probsT = ph(384)
        hsp = ph(2, HD)
        cst = probsT[0:16, 0:256]
        cvo = ph(256, parts=18)
        mko = ph(2, 256)
        vt = prob.rearrange("p i n -> p (i n)")[:, 0:2 * N].rearrange("p (k n) -> p k n", k=2)
        clast = ph(2, 18)
        t4 = ph(2, 8)
        used[0] = 0
        hT = ph(FT, N)
        uab = [[ph(306), ph(306)] for _ in range(2)]
        yab = [[ph(306), ph(306)] for _ in range(2)]
        sil = [ph(306) for _ in range(2)]
        ulast = ph(UJ, UG, 18)
        ulo = ph(UJ * P, parts=UG * 18)
        hT_lo = rounded["phase"][:, 0:FT * N].rearrange("p (k n) -> p k n", k=FT)
        hT_hi = rounded["phase"][:, used[0]:used[0] + FT * N].rearrange("p (k n) -> p k n", k=FT)
        ph(FT, N)
        used[0] = 0
        yrow = ph(3, D_MODEL)
        used[0] = 0
        memin = ph(2, D_MODEL)
        xin = ph(2, D_MODEL)
        xsin = ph(D_MODEL, parts=NS)
        rows = ph(P, parts=R_FINAL + 8)
        frows = ph(DEPTH * 3, P, parts=2 * FT)
        x_square = vals[:].rearrange("p b j c -> p (b j c)")[:, 0:KT_D * N].rearrange("p (k n) -> p k n", k=KT_D)
        mixed = [qT[:, k] for k in range(4)] + [hgs[:, k] for k in (0, 1)] + [cb[:, k] for k in (0, 1)]
        mg = XG[:, :, 0:N_MEM]
        vexp = XG[0:NS].rearrange("p k n -> p (k n)")[:, 0:2048].rearrange("p (h b v) -> p h b v", h=4, b=8)
        rawk_r = rounded["rawk"][:].rearrange("p a b c -> p (a b c)")
        xg_hi_mix = mixed_hi = rounded["mix"]
        mixed_lo = [rounded["phase"][:, c:c + N] for c in
                    [at_q + N * k for k in range(4)] + [at_g, at_g + N] + [at_cb, at_cb + N]]
        xg_hi = [rounded["mix"][:, 2 + k] if k < 6 else rawk_r[:, N * (k - 6):N * (k - 5)] for k in range(KT_D)]
        xg_lo = rounded["XG"]
        ring_lo = rounded["ring"]
        piece = [ring[:, 2 + q // 2, 1024 * (q % 2):1024 * (q % 2) + 1024] for q in range(4)]
        piece_lo = [ring_lo[:, 2 + q // 2, 1024 * (q % 2):1024 * (q % 2) + 1024] for q in range(4)]
        piece_hi = [ring_lo[:, q // 2, 1024 * (q % 2):1024 * (q % 2) + 1024] for q in range(4)]
        ring_hi = ([rounded["keysT"][:, i].rearrange("p b n -> p (b n)") for i in (0, 1)]
                   + [rounded["vals"][:, 4 * i:4 * i + 4].rearrange("p b j c -> p (b j c)") for i in (0, 1)])
        newS = sb("newS", P, 2, 8, HD)

        ident = con[:, C_IDENT:C_IDENT + P]
        perm = con[:, C_PERM:C_PERM + P]
        ones = con[:, C_ONES:C_ONES + P]
        blk = con[:, C_BLK:C_BLK + P]

        filled = sem("filled")
        emptied = {"A": sem("emptied_by_act"), "D": sem("emptied_by_dve")}
        loaded = [sem(f"loaded{i}") for i in range(SLOTS)]
        piece_in = [sem(f"piece{i}_in") for i in range(4)]
        x_in = sem("x_in")
        mix_in = sem("mix_in")
        par_in = sem("par_in")
        fpar_in = sem("fpar_in")
        con_in = sem("con_in")
        mem_in = sem("mem_in")
        rawk_in = [sem("rawk0_in"), sem("rawk1_in")]
        vals_in = sem("vals_in")
        s0_in = sem("s0_in")
        cstate_in = sem("cstate_in")
        ustate_in = sem("ustate_in")
        pages_in = sem("pages_in")
        y_stored = sem("y_stored")
        stored = sem("stored")
        s = {n: sem(n) for n in (
            "x_square", "sumsq", "xg_tile", "mg_even", "mg_odd", "rms_guess", "sigmoids", "gates_ready", "silu_gate_in",
            "h_level", "roped", "conv_done", "att_max", "att_exp", "att_p", "s_q", "s_max", "s_exp", "s_p",
            "zeros", "vexp_ready", "h_square", "h_out", "y_q", "y_max", "y_p", "x_max", "x_p",
            "mixed_hi", "mixed_lo", "down_used", "xg_hi", "xg_lo", "h_hi", "h_lo", "u_pads", "u_c0", "u_ya",
            "u_conv", "u_silu", "u_last", "h_tile", "mem_square", "mem_v", "mem_guess", "mem_scaled",
            "lb_d", "lb_exp", "y_guess", "y_rms")}
        w_hi = sem("w_hi")
        w_lo_dve = sem("w_lo_dve")
        w_lo_pool = sem("w_lo_pool")
        block = ctx.enter_context(nc.Block())

        dma_count = {}
        total = [0] * SLOTS
        for l in range(DEPTH):
            for n, (kind, i) in enumerate(CHUNKS):
                total[slot_of(n)] += 32 if kind == "up" else 16
                dma_count[l, n] = total[slot_of(n)]
        piece_count = {}
        total = [0] * 4
        for l in range(DEPTH):
            for p, (kind, use) in enumerate(PIECES):
                total[p % 4] += 16 * (5 if kind == "out" else 2 if use[0] in ("q0", "q1") else 1)
                piece_count[l, p] = total[p % 4]
        index = {c: n for n, c in enumerate(CHUNKS)}
        N_SPLIT = SPLIT_PIECES + len(CHUNKS) - index["up", 0]

        def split_of(kind, i, l):
            if kind in ("in", "out"):
                q = (i if kind == "in" else P_OUT + i) % 4
                count = N_SPLIT * l + (i if kind == "in" else IN_PIECES + i) + 1
                return count, piece[q], piece_lo[q], piece_hi[q], P, KT_D
            n = index[kind, i]
            tiles = DOWN_K[i % 3][1] - DOWN_K[i % 3][0] if kind == "down" else KT_D
            split = n - index["up", 0]
            return (N_SPLIT * l + SPLIT_PIECES + split + 1, ring[:, slot_of(n)], ring_lo[:, slot_of(n)],
                    ring_hi[split % SLOTS], 256, tiles)

        def fill_no(l, step, *args):
            return banks.of[l, step, args] + 1

        def pe_done(eng, l, step, *args):
            eng.wait_ge(filled, fill_no(l, step, *args))

        def wait_emptied(eng, l, step, *args):
            who, count = banks.before[banks.of[l, step, args]]
            eng.wait_ge(emptied[who], count)

        def bank(l, step, *args):
            return ps[:, banks.of[l, step, args] % 8, :]

        def last_use(l, n):
            kind, i = CHUNKS[n]
            if kind == "xo":
                return fill_no(l, "xo", 7)
            if kind == "up":
                return fill_no(l, "up", i, 1)
            if kind == "down":
                return fill_no(l, "down", i // 3 * 2 + 1)
            raise ValueError(kind)

        def piece_use(l, p):
            kind, args = PIECES[p]
            return fill_no(l, kind, *args)

        STORES_MIXER = 2 + 2 + 2 + 2 + 2 + 4
        STORES_LAYER = STORES_MIXER + 2 * UG

        @block.sync
        def _(sp):
            sp.dma_start(con[:, 0:C_BLK], a["const_f"][:, 0:C_BLK]).then_inc(x_in, 16)
            sp.dma_start(xin[:, 0], a["x_prompt"][0, 0:P]).then_inc(x_in, 16)
            sp.dma_start(xsin, a["x_sample"].rearrange("b s d -> (b s) d")).then_inc(x_in, 16)
            sp.dma_start(rows[0:DEPTH * 8], a["g_mix"].rearrange("l (k p) -> (l k) p", p=P)).then_inc(mix_in, 16)
            for l in range(DEPTH):
                for p, (kind, use) in enumerate(PIECES):
                    got = piece_in[p % 4]
                    if p >= 4:
                        sp.wait_ge(filled, piece_use(l, p - 4))
                    elif l and p < 2:
                        sp.wait_ge(filled, last_use(l - 1, index["down", 8]))
                    elif l:
                        sp.wait_ge(s["down_used"], 8 * l - 1)
                    dst = piece[p % 4].rearrange("p (k c) -> p k c", c=P)
                    if kind == "in":
                        c0 = IN_CHUNKS[p // 2][1]
                        w = a["w_in"][l].rearrange("(k p) c -> p k c", p=P)
                        if use[0] in ("q0", "q1"):
                            for half in range(2):
                                c = c0 + (2 * half + use[1]) * HD
                                sp.dma_start(dst[:, :, half * HD:half * HD + HD], w[:, :, c:c + HD]).then_inc(got, 16)
                        else:
                            c = c0 + P * use[1]
                            sp.dma_start(dst, w[:, :, c:c + P]).then_inc(got, 16)
                    elif kind == "out":
                        w = a["w_out"][l][:, P * use[0]:P * use[0] + P]
                        heads = w[0:512].rearrange("(p i g d) c -> p i d g c", p=2, i=2, g=2)
                        for pair in range(2):
                            for half in range(2):
                                sp.dma_start(dst[64 * half:64 * half + 64, 2 * pair:2 * pair + 2], heads[pair, half]).then_inc(got, 16)
                        sp.dma_start(dst[:, 4:8], w[512:1024].rearrange("(k p) c -> p k c", p=P)).then_inc(got, 16)
                    else:
                        c = P * (p % 2)
                        sp.dma_start(dst, a["w_" + kind][l][:, c:c + P].rearrange("(k p) c -> p k c", p=P)).then_inc(got, 16)
                for n, (kind, i) in enumerate(CHUNKS):
                    slot = ring[:, slot_of(n)]
                    if n < SLOTS:
                        sp.wait_ge(filled, (piece_use(l, P_XQ + 1), piece_use(l, P_OUT + 7), piece_use(l, P_OUT + 5),
                                            piece_use(l, P_OUT + 7))[n])
                    elif CHUNKS[n - SLOTS][0] == "down" and CHUNKS[n - SLOTS][1] % 3 < 2:
                        i_ = CHUNKS[n - SLOTS][1]
                        sp.wait_ge(s["down_used"], 8 * l + i_ // 3 * 2 + i_ % 3 + 1)
                    else:
                        sp.wait_ge(filled, last_use(l, n - SLOTS))
                    got = loaded[slot_of(n)]

                    def load(src, dst=slot.rearrange("p (k c) -> p k c", c=256)):
                        sp.dma_start(dst, src).then_inc(got, 16)

                    if kind == "xo":
                        load(a["w_xo"][l].rearrange("(k p) c -> p k c", p=P), slot.rearrange("p (k c) -> p k c", k=2))
                    elif kind == "up":
                        dst = slot.rearrange("p (k c) -> p k c", c=256)
                        for ab in (0, 1):
                            c0 = ab * D_FF + i * P
                            load(a["w_up"][l][:, c0:c0 + P].rearrange("(k p) c -> p k c", p=P), dst[:, :, P * ab:P * ab + P])
                    else:
                        k0, k1 = DOWN_K[i % 3]
                        c0 = 256 * (i // 3)
                        load(a["w_down"][l][P * k0:P * k1, c0:c0 + 256].rearrange("(k p) c -> p k c", p=P),
                             slot.rearrange("p (k c) -> p k c", c=256)[:, 0:k1 - k0])

            for t in range(3):
                for h in (0, 1):
                    wait_emptied(sp, DEPTH, "y", t, h)
                if t < 2:
                    sp.dma_start(y_prompt[0, P * t:P * t + P], yrow[:, t]).then_inc(y_stored, 16)
                else:
                    sp.dma_start(y_sample.rearrange("b s d -> (b s) d"), yrow[0:NS, 2]).then_inc(y_stored, 16)
            sp.wait_ge(y_stored, 16 * 3)

        @block.gpsimd
        def _(pool):
            g_ = nc.gpsimd
            def load_rawk(l, n):
                b, half = n % 8, n % 2
                if n >= 2:
                    pe_done(pool, l, *(("turn_past", n - 2) if n - 2 < 8 else ("turn_cmem", n - 10)))
                elif l:
                    pe_done(pool, l - 1, "turn_cmem", 6 + n)
                if n < 8:
                    for j in range(N_PAGES):
                        page = pool.value_load(pages[0:1, b * N_PAGES + j:b * N_PAGES + j + 1],
                                               min_val=0, max_val=a["cache_k"].shape[1] - 1)
                        src = a["cache_k"][l][bass.ds(page, 1)].rearrange("a r h d -> r (a h d)")
                        pool.dma_start(rawk[:, half, j], src).then_inc(rawk_in[half], 16)
                else:
                    src = a["cache_mem_k"][l, b].rearrange("(t p) h d -> p t (h d)", p=P)
                    pool.dma_start(rawk[:, half], src).then_inc(rawk_in[half], 16)

            def layer_loads(l):
                load_rawk(l, 0)
                load_rawk(l, 1)

            def load_vals(l, b):
                for i in (N_PAGES * b, N_PAGES * b + 1):
                    page = pool.value_load(pages[0:1, i:i + 1], min_val=0, max_val=a["cache_v"].shape[1] - 1)
                    src = a["cache_v"][l][bass.ds(page, 1)].rearrange("a r h d -> r (a h d)")
                    pool.dma_start(vals[:, i // N_PAGES, i % N_PAGES], src).then_inc(vals_in, 16)

            def store(dst, src):
                pool.dma_start(dst, src).then_inc(stored, 16)

            pool.dma_start(pages[:], a["page_table"].rearrange("b n -> (b n)").rearrange("(a n) -> a n", a=1)).then_inc(pages_in, 16)
            for l, step, args, who in banks.steps:
                if step == "x_squares":
                    pool.wait_ge(pages_in, 16)
                    layer_loads(0)
                elif (step, args) == ("ssq", (0,)):
                    pe_done(pool, l, "ssq", 0) if l else pe_done(pool, 0, "fpar")
                    if l:
                        pool.wait_ge(stored, 16 * l * STORES_LAYER)
                    for h in range(4):
                        pool.dma_start(s0[64 * (h % 2):64 * (h % 2) + 64, h // 2],
                                       a["state_hgrn"][l][:, h].rearrange("b d v -> d b v")).then_inc(s0_in, 16)
                    pool.dma_start(cst, a["state_conv"][l].rearrange("b w c -> (b w) c")).then_inc(cstate_in, 16)
                    g_.memset(sc, 0.0)
                    g_.memset(scs[0:NS], 0.0)
                    g_.memset(qs, 0.0)
                    g_.memset(qa, 0.0).then_inc(s["zeros"], 1)
                elif (step, args) == ("turn_k", (2,)):
                    wait_emptied(pool, l, "turn_k", 2)
                    store(k_prompt[l, 0].rearrange("(t p) h d -> p t (h d)", p=P), turned[:, 0:2])
                    store(k_sample[l].rearrange("b s h d -> (b s) (h d)"), turned[0:NS, 2])
                elif (step, args) == ("cstate_in", ()):
                    for g in range(UG):
                        src = a["state_ffn"][l].rearrange("b w f -> (b w) f")[:, g * UJ * P:(g + 1) * UJ * P]
                        pool.dma_start(ustr[16 * g:16 * g + 16], src).then_inc(ustate_in, 16)
                elif (step, args) == ("turn_v", (2,)):
                    wait_emptied(pool, l, "turn_v", 2)
                    store(v_prompt[l, 0].rearrange("(t p) h d -> p t (h d)", p=P), vn[:, 0:2])
                    store(v_sample[l].rearrange("b s h d -> (b s) (h d)"), vn[0:NS, 2])
                elif (step, args) == ("in", ("hg", 1)):
                    pe_done(pool, l, "in", "hg", 1)
                    if l == 0:
                        wait_emptied(pool, 0, "turn_mem", KT_D - 1)
                    pool.drain()
                    for k in range(1, KT_D, 2):
                        c = par_col(R_MEM, l, k)
                        g_.tensor_scalar(mg[:, k], memT[:, k], par[:, c:c + 1], None, ALU.mult).then_inc(s["mg_odd"], 1)
                elif (step, args) == ("turn_mk", (1,)):
                    wait_emptied(pool, l, "turn_mk", 1)
                    store(mem_k_prompt[l, 0].rearrange("(t p) h d -> p t (h d)", p=P), mko)
                elif (step, args) == ("mv", (1,)):
                    wait_emptied(pool, l, "mv", 1)
                    store(mem_v_prompt[l, 0].rearrange("(t p) h d -> p t (h d)", p=P), mv[:])
                    wait_emptied(pool, l, "turn_hi", 2)
                    pool.wait_ge(con_in, 32)
                    pool.drain()
                    for h in range(4):
                        last = g_.tensor_tensor(
                            vexp[:, h], vh[0:NS, 2, h * HD:(h + 1) * HD].unsqueeze(1).broadcast_to([NS, 8, HD]),
                            con[0:NS, C_SEL:C_SEL + 8].unsqueeze(2).broadcast_to([NS, 8, HD]), ALU.mult)
                    last.then_inc(s["vexp_ready"], 1)
                elif step == "turn_past":
                    load_rawk(l, args[0] + 2)
                    load_vals(l, args[0])
                elif step == "turn_cmem":
                    b = args[0]
                    if b < 6:
                        load_rawk(l, b + 10)
                    if b == 0:
                        pe_done(pool, l, "so", 1)
                    src = a["cache_mem_v"][l, b].rearrange("(t p) h d -> p t (h d)", p=P)
                    pool.dma_start(vals[:, b], src).then_inc(vals_in, 16)
                elif step == "cstate_out":
                    wait_emptied(pool, l, "cstate_out")
                    store(conv_prompt[l, 0], cvo[0:2])
                    store(conv_sample[l].rearrange("b w c -> (b w) c"), cvo[2:18])
                elif step == "sq":
                    p = args[0]
                    if p:
                        pe_done(pool, l, "ss", 0)
                    else:
                        pool.wait_ge(s["zeros"], l + 1)
                    pool.wait_ge(s["roped"], 6 * l + 6)
                    pool.drain()
                    for i in (0, 1):
                        rows_i = slice(64 * i, 64 * i + 64)
                        src = qT[rows_i, 2 * p:2 * p + 2, SEQ:N].rearrange("p g (b s) -> p b g s", b=8)
                        dst = qs[rows_i].rearrange("p (b x) -> p b x", x=144)[:, :, 8 * i:8 * i + 8]
                        g_.tensor_copy(dst.rearrange("p b (g s) -> p b g s", g=2), src)
                        dst = qa[rows_i].rearrange("p (b x) -> p b x", x=16)[:, :, 8 * i:8 * i + 8]
                        last = g_.tensor_copy(dst.rearrange("p b (g s) -> p b g s", g=2), src)
                    last.then_inc(s["s_q"], 1)
                elif (step, args) == ("hstate_s", (1,)):
                    wait_emptied(pool, l, "hstate_s", 1)
                    for h in range(4):
                        store(hgrn_sample[l][:, h].rearrange("b d v -> d b v"), newS[64 * (h % 2):64 * (h % 2) + 64, h // 2])
                elif (step, args) == ("hstate", ()):
                    wait_emptied(pool, l, "hstate")
                    for i in (0, 1):
                        store(hgrn_prompt[l, 0].rearrange("(k i) d v -> i d k v", k=2)[i], hsp[64 * i:64 * i + 64])
                    pe_done(pool, l, "ss", 1)
                    g_.memset(qs, 0.0)
                elif step == "yq":
                    wait_emptied(pool, l, "xq", 1)
                    pool.drain()
                    for p in (0, 1):
                        for i in (0, 1):
                            rows_i = slice(64 * i, 64 * i + 64)
                            src = qT[rows_i, p, SEQ:N].rearrange("p (b s) -> p b s", b=8)
                            dst = qs[rows_i, 576 * p:576 * p + 576].rearrange("p (b x) -> p b x", x=72)[:, :, 4 * i:4 * i + 4]
                            last = g_.tensor_copy(dst, src)
                    last.then_inc(s["y_q"], 1)
                elif step == "rest" and args[0] in ("up", "down"):
                    count, both, lo, hi_part, width, tiles = split_of(*args)
                    pool.wait_ge(w_hi, count)
                    cols = slice(LO_DVE[args[0]] * width, tiles * width)
                    pool.drain()
                    g_.tensor_tensor(lo[:, cols], both[:, cols], hi_part[:, cols].bitcast(F32),
                                     ALU.subtract).then_inc(w_lo_pool, 1)
                elif step == "xo":
                    k = args[0]
                    pool.wait_ge(s["xg_hi"], KT_D * (2 * l + 1) + k + 1)
                    pool.drain()
                    g_.tensor_tensor(xg_lo[:, k], XG[:, k], xg_hi[k].bitcast(F32), ALU.subtract).then_inc(s["xg_lo"], 1)
                elif step == "gate":
                    i = args[0]
                    pool.wait_ge(s["h_hi"], FT * l + i + 1)
                    pool.drain()
                    g_.tensor_tensor(hT_lo[:, i], hT[:, i], hT_hi[:, i].bitcast(F32), ALU.subtract).then_inc(s["h_lo"], 1)
                elif step == "pads":
                    i = args[0]
                    if i == 0:
                        pe_done(pool, l, "xo", 7)
                        pool.wait_ge(stored, 16 * (l * STORES_LAYER + STORES_MIXER))
                        wait_emptied(pool, l, "ustate_in", 1)
                    if i >= 2:
                        pool.wait_ge(s["u_conv"], FT * l + i - 1)
                        pool.wait_ge(s["u_c0"], 2 * (FT * l + i - 1))
                    for ab in (0, 1):
                        g, j = divmod(FT * ab + i, UJ)
                        u = uab[i % 2][ab]
                        g_.memset(u[:, 0:2], 0.0)
                        g_.tensor_copy(u[:, 258:306].rearrange("p (b x) -> p b x", x=6)[:, :, 0:2],
                                       ust[:, j, g].rearrange("p (b w) -> p b w", w=2)).then_inc(s["u_pads"], 1)
                elif step == "up":
                    i, ab = args
                    u = uab[i % 2][ab]
                    g, j = divmod(FT * ab + i, UJ)
                    wait_emptied(pool, l, "up", i, ab)
                    g_.tensor_copy(ulast[:, j, g, 0:2], u[:, 256:258])
                    g_.tensor_copy(ulast[:, j, g, 2:18].rearrange("p (b w) -> p b w", w=2),
                                   u[:, 258:306].rearrange("p (b x) -> p b x", x=6)[:, :, 4:6]).then_inc(s["u_last"], 1)
                elif step == "down" and l + 1 < DEPTH:
                    k = args[0]
                    if k == 0:
                        pe_done(pool, l, "up", FT - 1, 1)
                        layer_loads(l + 1)
                    pool.wait_ge(s["xg_hi"], KT_D * (2 * l + 2) + k + 1)
                    pool.drain()
                    g_.tensor_tensor(xg_lo[:, k], XG[:, k], xg_hi_mix[:, k].bitcast(F32), ALU.subtract).then_inc(s["xg_lo"], 1)
                elif (step, args) == ("ustate_out", (2,)):
                    wait_emptied(pool, l, "ustate_out", 2)
                    for g in range(UG):
                        cols = slice(g * UJ * P, (g + 1) * UJ * P)
                        store(ffn_prompt[l, 0][:, cols], ulo[18 * g:18 * g + 2])
                        store(ffn_sample[l].rearrange("b w f -> (b w) f")[:, cols], ulo[18 * g + 2:18 * g + 18])
            pool.wait_ge(stored, 16 * DEPTH * STORES_LAYER)

        @block.scalar
        def _(act):
            ac = nc.scalar.activation
            act.dma_start(xin[:, 1], a["x_prompt"][0, P:SEQ]).then_inc(x_in, 16)
            for (r0, k), name in ((R_XATTN, "g_xattn"), (R_MEM, "g_mem"), (R_FFN, "g_ffn"),
                                  (R_LB, "hg_lb_logits"), (R_NORM, "hg_norm_g")):
                act.dma_start(rows[r0:r0 + DEPTH * k], a[name].rearrange("l (k p) -> (l k) p", p=P)).then_inc(par_in, 16)
            act.dma_start(rows[R_CONV[0]:R_FINAL], a["conv_w"].rearrange("l w (k p) -> (l w k) p", p=P)).then_inc(par_in, 16)
            act.dma_start(rows[R_FINAL:R_FINAL + 8], a["g_final"].rearrange("(k p) -> k p", p=P)).then_inc(par_in, 16)
            act.dma_start(frows, a["ffn_conv_w"].rearrange("l w (k p) -> k (l w) p", p=P)).then_inc(fpar_in, 16)
            act.dma_start(con[:, C_BLK:], a["const_f"][:, C_BLK:]).then_inc(con_in, 16)
            act.dma_start(mask[:], a["const_i"]).then_inc(con_in, 16)
            act.dma_start(memin, a["mem_prompt"][0].rearrange("(t p) d -> p t d", p=P)).then_inc(mem_in, 16)

            def take(l, step, args, dst, src):
                act.wait_ge(filled, fill_no(l, step, *args))
                return nc.scalar.copy(dst, src)

            def guess():
                ac(Rn[:], vv[:], ACT.Abs_reciprocal_sqrt).then_inc(s["rms_guess"], 1)

            def gained(l, stage, k):
                if stage == 3:
                    wait_emptied(act, l, "down", k)
                elif l == 0 and stage == 0:
                    wait_emptied(act, -1, "turn_x", k)
                else:
                    before = (l, ("", "out", "xo")[stage]) if stage else (l - 1, "down")
                    wait_emptied(act, *before, k)
                c = R_FINAL + k if stage == 3 else par_col((R_MIX, R_XATTN, R_FFN)[stage], l, k)
                if stage or l:
                    ac(XG[:, k], X[:, k], ACT.Identity, scale=par[:, c:c + 1]).then_inc(s["xg_tile"], 1)
                if stage == 0:
                    ac(xg_hi_mix[:, k], X[:, k], ACT.Identity, scale=par[:, c:c + 1]).then_inc(s["xg_hi"], 1)
                if stage == 2:
                    ac(xg_hi[k], X[:, k], ACT.Identity, scale=par[:, c:c + 1]).then_inc(s["xg_hi"], 1)

            for l, step, args, who in banks.emptying_steps:
                if step == "par_mix":
                    wait_emptied(act, l, step)
                    for k in range(KT_D):
                        gained(0, 0, k)
                elif step == "x_squares":
                    for k in range(KT_D):
                        ac(x_square[:, k], X[:, k], ACT.Square).then_inc(s["x_square"], 1)
                elif step == "bounds":
                    wait_emptied(act, 0, "par")
                    act.wait_ge(s["lb_d"], 1)
                    ac(small[:, 8:12], small[:, 4:8], ACT.Exp).then_inc(s["lb_exp"], 1)
                elif step == "mem_rms":
                    act.wait_ge(mem_in, 16)
                    junk = memT[:].rearrange("p k n -> p (k n)")
                    act.drain()
                    for t in (0, 1):
                        last = ac(junk[:, 0:D_MODEL], memin[:, t], ACT.Square, accum_out=small[:, 80 + t:81 + t])
                        act.drain()
                    last.then_inc(s["mem_square"], 1)
                    act.wait_ge(s["mem_v"], 1)
                    ac(small[:, 86:88], small[:, 82:84], ACT.Abs_reciprocal_sqrt).then_inc(s["mem_guess"], 1)
                elif step == "ssq_final":
                    wait_emptied(act, l, step)
                    for n, c in ((P, slice(0, 2)), (NS, slice(2, 3))):
                        last = ac(small[0:n, 92 + c.start:92 + c.stop], small[0:n, 88 + c.start:88 + c.stop],
                                  ACT.Abs_reciprocal_sqrt)
                    last.then_inc(s["y_guess"], 1)
                elif step == "turn_mem":
                    take(l, step, args, memT[:, args[0]], bank(l, step, *args)[:, 0:N_MEM]).then_inc(emptied["A"], 1)
                elif step == "ssq" or step == "hn":
                    wait_emptied(act, l, step, *args)
                    guess()
                elif step == "gates":
                    if l:
                        act.wait_ge(stored, 16 * l * STORES_LAYER)
                    wait_emptied(act, l, "in", "hf", 1)
                    ac(hf, e1, ACT.Sigmoid)
                    ac(hk, e1, ACT.Sigmoid, scale=-1.0)
                    wait_emptied(act, l, "in", "hq", 1)
                    ac(hq, e2, ACT.Sigmoid).then_inc(s["sigmoids"], 1)
                elif (step, args) == ("in", ("hg", 1)):
                    wait_emptied(act, l, "in", "hg", 1)
                    for k in range(0, KT_D, 2):
                        c = par_col(R_MEM, l, k)
                        ac(mg[:, k], memT[:, k], ACT.Identity, scale=par[:, c:c + 1]).then_inc(s["mg_even"], 1)
                    act.wait_ge(s["gates_ready"], l + 1)
                    ac(e1, hgs, ACT.Sigmoid).then_inc(s["silu_gate_in"], 1)
                elif step in ("turn_hi", "turn_k", "turn_v", "turn_ke"):
                    t = args[0]
                    n = P if t < 2 else NS
                    dst = {"turn_hi": vh, "turn_k": turned, "turn_v": vn, "turn_ke": ke}[step]
                    take(l, step, args, dst[0:n, t], bank(l, step, *args)[0:n, 0:256]).then_inc(emptied["A"], 1)
                elif step == "mk":
                    take(l, step, args, mkT[:, args[0]], bank(l, step, *args)[:, 0:N_MEM]).then_inc(emptied["A"], 1)
                elif step == "mv":
                    if l and args[0] == 0:
                        act.wait_ge(stored, 16 * l * STORES_LAYER)
                    take(l, step, args, mv[:, args[0]], bank(l, step, *args)[:, 0:256]).then_inc(emptied["A"], 1)
                elif step == "turn_mk":
                    take(l, step, args, mko[:, args[0]], bank(l, step, *args)[:, 0:256]).then_inc(emptied["A"], 1)
                elif step in ("turn_past", "turn_cmem"):
                    src = bank(l, step, *args).rearrange("p (k m) -> p k m", k=2)
                    take(l, step, args, keysT[:, :, args[0]], src).then_inc(emptied["A"], 1)
                elif step == "cstate_out":
                    take(l, step, args, cvo[0:18], bank(l, step)[0:18, 0:256]).then_inc(emptied["A"], 1)
                elif step == "ustate_in":
                    j0, j1 = ((0, 8), (8, UJ))[args[0]]
                    src = bank(l, step, *args)[:, 0:64 * (j1 - j0)].rearrange("p (j x) -> p j x", x=64)
                    take(l, step, args, ust[:, j0:j1].rearrange("p j g r -> p j (g r)"), src).then_inc(emptied["A"], 1)
                elif step == "as":
                    g, i = args
                    c = 16 + 16 * (g % 2) + 2 * i
                    act.wait_ge(s["att_max"], 8 * l + 2 * g + i + 1)
                    ac(prob[:, i, 0:P], prob[:, i, 0:P], ACT.Exp, bias=small[:, c + 4:c + 5], scale=SCALE,
                       accum_out=small[:, c + 8:c + 9])
                    ac(prob[:, i, P:384], prob[:, i, P:384], ACT.Exp, bias=small[:, c + 5:c + 6], scale=SCALE,
                       accum_out=small[:, c + 9:c + 10]).then_inc(s["att_exp"], 1)
                elif step == "at":
                    g, i = args
                    if g:
                        pe_done(act, l, "ao", g - 1)
                    take(l, step, args, probT[:, i, 0:384], bank(l, step, *args)[:, 0:384]).then_inc(emptied["A"], 1)
                elif step == "ao":
                    take(l, step, args, mixed[args[0]][:, 0:SEQ], bank(l, step, *args)[:, 0:SEQ]).then_inc(emptied["A"], 1)
                elif step == "ss":
                    act.wait_ge(s["s_max"], 2 * l + args[0] + 1)
                    ac(probs, probs, ACT.Exp, bias=small[:, 49:50], scale=SCALE,
                       accum_out=small[:, 50:51]).then_inc(s["s_exp"], 1)
                elif step == "st":
                    if args[0]:
                        pe_done(act, l, "so", 0)
                    b_ = bank(l, step, *args)
                    take(l, step, args, probsT[:, 0:256], b_[:, 0:256])
                    nc.scalar.copy(probsT[0:NS, 256:384], b_[0:NS, 256:384]).then_inc(emptied["A"], 1)
                elif step == "so":
                    p = args[0]
                    act.wait_ge(filled, fill_no(l, step, p))
                    for i in (0, 1):
                        rows_i = slice(64 * i, 64 * i + 64)
                        src = bank(l, step, p)[rows_i, 0:P].rearrange("p (b i g s) -> p i g b s", b=8, i=2, g=2)[:, i]
                        dst = qT[rows_i, 2 * p:2 * p + 2, SEQ:N].rearrange("p g (b s) -> p g b s", b=8)
                        last = nc.scalar.copy(dst, src)
                    last.then_inc(emptied["A"], 1)
                elif step == "split_mixed":
                    k = args[0]
                    if k >= 6:
                        act.wait_ge(s["conv_done"], l + 1)
                    elif k >= 4:
                        act.wait_ge(s["h_out"], 2 * l + k - 3)
                    else:
                        act.drain()
                    nc.scalar.copy(mixed_hi[:, k], mixed[k]).then_inc(s["mixed_hi"], 1)
                elif step == "hstate":
                    take(l, step, args, hsp.rearrange("p k v -> p (k v)"), bank(l, step)[:, 0:P]).then_inc(emptied["A"], 1)
                elif (step, args) == ("out", (7,)):
                    pe_done(act, l, "hstate_s", 1)
                    for k in range(KT_D):
                        gained(l, 1, k)
                elif step == "xo":
                    if args[0] == 0:
                        pe_done(act, l, "turn_cmem", 7)
                    gained(l, 2, args[0])
                elif step == "down":
                    if l + 1 < DEPTH:
                        gained(l + 1, 0, args[0])
                    else:
                        gained(l, 3, args[0])
                elif step == "round":
                    kind, i, l = args
                    count, both, lo, hi_part, width, tiles = split_of(*args)
                    if kind == "out":
                        act.wait_ge(piece_in[(P_OUT + i) % 4], piece_count[l, P_OUT + i])
                    elif kind == "in":
                        if l and i == 0:
                            act.wait_ge(s["down_used"], 8 * l)
                        elif l and i == 2:
                            pe_done(act, l - 1, "down", 7)
                        act.wait_ge(piece_in[i % 4], piece_count[l, i])
                    else:
                        if (kind, i) == ("up", 0):
                            pe_done(act, l, "ys")
                        elif (kind, i) == ("up", 2):
                            pe_done(act, l, "yo", 1)
                        n = index[kind, i]
                        act.wait_ge(loaded[slot_of(n)], dma_count[l, n])
                    nc.scalar.copy(hi_part[:, 0:tiles * width], both[:, 0:tiles * width]).then_inc(w_hi, 1)
                elif step == "ys":
                    act.wait_ge(s["y_max"], l + 1)
                    ac(probs[:, 0:256], bank(l, "ys")[:, 0:256], ACT.Exp, bias=small[:, 53:54], scale=SCALE,
                       accum_out=small[:, 54:55]).then_inc(emptied["A"], 1)
                elif step == "xs":
                    h = args[0]
                    c = 60 + 8 * (h % 2)
                    act.wait_ge(s["x_max"], 4 * l + h + 1)
                    if h >= 2:
                        pe_done(act, l, "xt", h - 2)
                    for q in (0, 1):
                        last = ac(prob[:, h % 2, 256 * q:256 * q + 256], bank(l, "xs", h)[:, 256 * q:256 * q + 256],
                                  ACT.Exp, bias=small[:, c + 2 + q:c + 3 + q], scale=SCALE,
                                  accum_out=small[:, c + 4 + q:c + 5 + q])
                    last.then_inc(emptied["A"], 1)
                elif step == "xt":
                    h = args[0]
                    if h >= 2:
                        pe_done(act, l, "xov", 0)
                    take(l, step, args, probT[:, h % 2], bank(l, step, h)).then_inc(emptied["A"], 1)
                elif step == "xov":
                    take(l, step, args, mix[:, args[0], 0:SEQ], bank(l, step, *args)[:, 0:SEQ]).then_inc(emptied["A"], 1)
                elif step == "yt":
                    take(l, step, args, probsT[:, 0:256], bank(l, step)[:, 0:256]).then_inc(emptied["A"], 1)
                elif step == "yo":
                    p = args[0]
                    act.wait_ge(filled, fill_no(l, step, p))
                    for i in (0, 1):
                        rows_i = slice(64 * i, 64 * i + 64)
                        src = bank(l, step, p)[rows_i, 0:64].rearrange("p (b i s) -> p i b s", b=8, i=2)[:, i]
                        dst = mix[rows_i, p, SEQ:N].rearrange("p (b s) -> p b s", b=8)
                        last = nc.scalar.copy(dst, src)
                    last.then_inc(emptied["A"], 1)
                elif step == "up":
                    i, ab = args
                    wait_emptied(act, l, "up", i, ab)
                    act.wait_ge(s["u_pads"], 2 * FT * l + 2 * i + ab + 1)
                    if i >= 2:
                        act.wait_ge(s["h_tile"], FT * l + i - 1)
                    c = FT * ab + i
                    ac(yab[i % 2][ab][:, 0:304], uab[i % 2][ab][:, 0:304], ACT.Identity,
                       scale=fpar[:, 3 * l, c:c + 1]).then_inc(s["u_c0"], 1)
                elif step == "convolve":
                    i = args[0]
                    act.wait_ge(s["u_ya"], FT * l + i + 1)
                    ac(sil[i % 2][:, 0:304], yab[i % 2][0][:, 0:304], ACT.Silu).then_inc(s["u_silu"], 1)
                elif step == "gate":
                    i = args[0]
                    act.wait_ge(s["h_tile"], FT * l + i + 1)
                    nc.scalar.copy(hT_hi[:, i], hT[:, i]).then_inc(s["h_hi"], 1)
                elif step == "ustate_out":
                    q = args[0]
                    n = P * (min(UJ, 4 * q + 4) - 4 * q)
                    take(l, step, args, ulo[0:UG * 18, 512 * q:512 * q + n],
                         bank(l, step, q)[0:UG * 18, 0:n]).then_inc(emptied["A"], 1)
                elif step == "y":
                    t, h = args
                    n = P if t < 2 else NS
                    if t == 1:
                        continue
                    act.wait_ge(s["y_rms"], 1 if t < 2 else 2)
                    pe_done(act, l, step, t, h)
                    ac(yrow[0:n, t, 512 * h:512 * h + 512], bank(l, step, t, h)[0:n], ACT.Identity,
                       scale=small[0:n, 92 + t:93 + t]).then_inc(emptied["A"], 1)

        @block.tensor
        def _(pe):
            mm = nc.tensor.matmul
            tr = nc.tensor.transpose
            rawk_n = [0, 0]

            def chunk(l, kind, i, part=None):
                n = index[kind, i]
                pe.wait_ge(loaded[slot_of(n)], dma_count[l, n])
                return ring[:, slot_of(n)].rearrange("p (k c) -> p k c", c=256)

            def whole(l, p):
                pe.wait_ge(piece_in[p % 4], piece_count[l, p])
                return piece[p % 4].rearrange("p (k c) -> p k c", c=P)

            def parts_of(l, kind, i):
                count, _, lo, hi_part, width, _ = split_of(kind, i, l)
                pe.wait_ge(w_lo_dve, count)
                if kind in ("up", "down"):
                    pe.wait_ge(w_lo_pool, count - SPLIT_PIECES * (l + 1))
                return [w.rearrange("p (k c) -> p k c", c=width) for w in (hi_part, lo)]

            def xg(l, stage, k):
                pe.wait_ge(s["xg_tile"], 24 * l + 8 * stage + k + 1 - KT_D)
                return XG[:, k]

            def project(out_, w, cols, l, stage):
                for k in range(KT_D):
                    last = mm(out_[:, 0:N], w[:, k, cols], xg(l, stage, k), start=k == 0, stop=k == KT_D - 1)
                return last

            def split_product(out_, hi_w, lo_w, hi_x, lo_x, start, stop):
                mm(out_, hi_w, hi_x, start=start, stop=False)
                mm(out_, hi_w, lo_x, start=False, stop=False)
                return mm(out_, lo_w, hi_x, start=False, stop=stop)

            def turn(out_, src, n, parts=P):
                for m in (0, 1):
                    last = tr(out_[0:n, P * m:P * m + P], src[:, m], ident[:])
                return last

            fill = -1
            for l, step, args, who in banks.steps:
                if who == "op":
                    continue
                fill += 1
                if fill >= 8:
                    w_, count = banks.before[fill - 8]
                    pe.wait_ge(emptied[w_], count)
                o = ps[:, fill % 8, :]
                if step == "par_mix":
                    pe.wait_ge(mix_in, 16)
                    last = tr(o[:, 0:DEPTH * 8], rows[0:DEPTH * 8], ident[0:DEPTH * 8, 0:DEPTH * 8])
                elif step == "par":
                    pe.wait_ge(par_in, 16 * 7)
                    last = tr(o[:, 0:R_FINAL + 8], rows, ident[0:R_FINAL + 8, 0:R_FINAL + 8])
                elif step == "fpar":
                    pe.wait_ge(fpar_in, 16)
                    for r in range(DEPTH * 3):
                        last = tr(o[:, 2 * FT * r:2 * FT * (r + 1)], frows[:, r], ident[0:2 * FT, 0:2 * FT])
                elif step == "turn_x":
                    k = args[0]
                    pe.wait_ge(x_in, 64)
                    for t in (0, 1):
                        tr(o[:, P * t:P * t + P], xin[:, t, P * k:P * k + P], ident[:])
                    last = tr(o[:, SEQ:N], xsin[0:NS, P * k:P * k + P], ident[0:NS, 0:NS])
                elif step == "turn_mem":
                    k = args[0]
                    pe.wait_ge(s["mem_scaled"], 1)
                    for t in (0, 1):
                        last = tr(o[:, P * t:P * t + P], memin[:, t, P * k:P * k + P], ident[:])
                elif step == "ssq_final":
                    pe.wait_ge(s["sumsq"], 3 * DEPTH + 1)
                    for t in range(3):
                        n = P if t < 2 else NS
                        last = mm(o[0:n, t:t + 1], acc[:, P * t:P * t + n], ones[:, 0:1], start=True, stop=True)
                elif step == "ssq":
                    pe.wait_ge(s["sumsq"], 3 * l + args[0] + 1)
                    last = mm(o[:, 0:N], ones, acc[:], start=True, stop=True)
                elif step == "in":
                    part, m = args
                    i = [c[0] for c in IN_CHUNKS].index(part)
                    hi_w, lo_w = parts_of(l, "in", 2 * i + m)
                    for k in range(KT_D):
                        pe.wait_ge(s["xg_lo"], 2 * KT_D * l + k + 1)
                        last = split_product(o[:, 0:N], hi_w[:, k], lo_w[:, k], xg_hi_mix[:, k], xg_lo[:, k], k == 0, k == KT_D - 1)
                elif step == "rope":
                    kind, m = args
                    src = kT[:, m] if kind == "k" else qT[:, m]
                    if kind == "k":
                        wait_emptied(pe, l, "in", "k", m)
                    else:
                        wait_emptied(pe, l, "in", f"q{m // 2}", m % 2)
                    last = mm(o[:, 0:N], perm, src, start=True, stop=True)
                elif step in ("turn_hi", "turn_k", "turn_v", "turn_ke"):
                    t = args[0]
                    cols = slice(P * t, P * t + P) if t < 2 else slice(SEQ, N)
                    n = P if t < 2 else NS
                    if step == "turn_hi":
                        wait_emptied(pe, l, "in", "hi", 1)
                        src = hi
                    elif step == "turn_k":
                        pe.wait_ge(s["roped"], 6 * l + 2)
                        src = kT
                    elif step == "turn_v":
                        wait_emptied(pe, l, "in", "v", 1)
                        src = vt
                    else:
                        pe.wait_ge(s["h_level"], 9 * l + 9)
                        src = hk
                    last = turn(o, src[:, :, cols], n)
                elif step == "cstate_in":
                    pe.wait_ge(cstate_in, 16 * (l + 1))
                    for m in (0, 1):
                        last = tr(o[:, 16 * m:16 * m + 16], cst[0:16, P * m:P * m + P], ident[0:16, 0:16])
                elif step == "cstate_out":
                    pe.wait_ge(s["conv_done"], l + 1)
                    for m in (0, 1):
                        last = tr(o[0:18, P * m:P * m + P], clast[:, m], ident[:])
                elif step == "mk":
                    m = args[0]
                    w = whole(l, P_MK + m)
                    for k in range(KT_D):
                        pe.wait_ge(s["mg_odd" if k % 2 else "mg_even"], KT_D // 2 * l + k // 2 + 1)
                        last = mm(o[:, 0:N_MEM], w[:, k], mg[:, k], start=k == 0, stop=k == KT_D - 1)
                elif step == "mv":
                    t = args[0]
                    for c in (0, 1):
                        w = whole(l, P_MV + c)
                        for k in range(KT_D):
                            last = mm(o[:, P * c:P * c + P], mg[:, k, P * t:P * t + P], w[:, k], start=k == 0, stop=k == KT_D - 1)
                elif step == "turn_mk":
                    wait_emptied(pe, l, "mk", 1)
                    last = turn(o, mkT[:, :, P * args[0]:P * args[0] + P], P)
                elif step in ("turn_past", "turn_cmem"):
                    b = args[0]
                    rawk_n[b % 2] += 32 if step == "turn_past" else 16
                    pe.wait_ge(rawk_in[b % 2], rawk_n[b % 2])
                    for p in (0, 1):
                        for j in (0, 1):
                            last = tr(o[:, 256 * p + P * j:256 * p + P * j + P], rawk[:, b % 2, j, P * p:P * p + P], ident[:])
                elif step == "ustate_in":
                    if args[0] == 0:
                        pe.wait_ge(ustate_in, 16 * UG * (l + 1))
                    j0, j1 = ((0, 8), (8, UJ))[args[0]]
                    for j in range(j0, j1):
                        last = tr(o[:, 64 * (j - j0):64 * (j - j0) + 64], ustr[:, P * j:P * j + P], ident[0:64, 0:64])
                elif step == "as":
                    g, i = args
                    pe.wait_ge(s["roped"], 6 * l + 6)
                    r = slice(64 * i, 64 * i + 64)
                    mm(o[:, 0:P], qT[r, g, 0:P], kT[r, g // 2, 0:P], start=True, stop=True)
                    last = mm(o[:, P:384], qT[r, g, P:SEQ], kT[r, g // 2, 0:SEQ], start=True, stop=True)
                elif step == "at":
                    g, i = args
                    pe.wait_ge(s["att_p"], 4 * l + g + 1)
                    for j in range(3):
                        last = tr(o[:, P * j:P * j + P], prob[:, i, P * j:P * j + P], ident[:])
                elif step == "ao":
                    g = args[0]
                    wait_emptied(pe, l, "at", g, 1)
                    for i in (0, 1):
                        r = slice(64 * i, 64 * i + 64)
                        kv = slice((g // 2 * 2 + i) * HD, (g // 2 * 2 + i) * HD + HD)
                        mm(o[r, 0:P], vn[:, 0, kv], probT[:, i, 0:P], start=True, stop=True)
                        mm(o[r, P:SEQ], vn[:, 0, kv], probT[:, i, P:SEQ], start=True, stop=False)
                        last = mm(o[r, P:SEQ], vn[:, 1, kv], probT[:, i, SEQ:384], start=False, stop=True)
                elif step == "ss":
                    p = args[0]
                    pe.wait_ge(s["s_q"], 2 * l + p + 1)
                    wait_emptied(pe, l, "turn_past", 7)
                    mm(o[:, 256:N], qa, kT[:, p, SEQ:N], start=True, stop=True)
                    for b in range(8):
                        last = mm(o[:, 0:256], qs[:, P * b:P * b + P], keysT[:, p, b], start=b == 0, stop=b == 7)
                elif step == "st":
                    pe.wait_ge(s["s_p"], 2 * l + args[0] + 1)
                    for j in (0, 1):
                        tr(o[:, P * j:P * j + P], probs[:, P * j:P * j + P], ident[:])
                    last = tr(o[0:NS, 256:384], probs[:, 256:N], ident[:])
                elif step == "so":
                    p = args[0]
                    wait_emptied(pe, l, "st", p)
                    pe.wait_ge(vals_in, 16 * (24 * l + 16))
                    c = slice(P * p, P * p + P)
                    for b in range(8):
                        for j in (0, 1):
                            mm(o[:, 16 * b:16 * b + 16], vals[:, b, j, c], probsT[:, P * j + 16 * b:P * j + 16 * b + 16],
                               start=(b, j) == (0, 0), stop=False, skip_group_check=True)
                    last = mm(o[:, 0:P], vn[0:NS, 2, c], probsT[0:NS, 256:384], start=False, stop=True, skip_group_check=True)
                elif step in ("diag", "diag_s"):
                    i = args[0]
                    pe.wait_ge(s["gates_ready"], l + 1)
                    r = slice(64 * i, 64 * i + 64)
                    for t in (0, 1) if step == "diag" else (2,):
                        for p in (0, 1):
                            n, c = (P, slice(P * t, P * t + P)) if t < 2 else (NS, slice(SEQ, N))
                            at = P * (2 * t + p) if t < 2 else NS * p
                            last = mm(o[0:n, at:at + n], hk[r, p, c], hq[r, p, c], start=True, stop=True)
                elif step == "level":
                    m, i = args
                    pe.wait_ge(s["h_level"], 9 * l + LEVELS.index(m) + 1)
                    r = slice(64 * i, 64 * i + 64)
                    for t in (0, 1, 2) if m < DEC_SEQ else (0, 1):
                        for p in (0, 1):
                            n, c = (P, slice(P * t, P * t + P)) if t < 2 else (NS, slice(SEQ, N))
                            at = 64 * (2 * t + p) if t < 2 else 256 + NS // 2 * p
                            q = hq[r, p, c].rearrange("p (n two m) -> p n two m", two=2, m=m)[:, :, 1]
                            last = mm(o[0:n, at:at + n // 2], hk[r, p, c], q, start=True, stop=True)
                elif step == "cross":
                    pe.wait_ge(s["h_level"], 9 * l + 8)
                    r = slice(64 * args[0], 64 * args[0] + 64)
                    for p in (0, 1):
                        last = mm(o[:, P * p:P * p + P], hk[r, p, 0:P], hq[r, p, P:SEQ], start=True, stop=True)
                elif step == "hstate":
                    wait_emptied(pe, l, "turn_ke", 2)
                    for h in range(4):
                        r = slice(64 * (h % 2), 64 * (h % 2) + 64)
                        c = slice(HD * h, HD * h + HD)
                        for t in (0, 1):
                            last = mm(o[r, 64 * (h // 2):64 * (h // 2) + 64], ke[:, t, c], vh[:, t, c], start=t == 0, stop=t == 1)
                elif step == "hstate_s":
                    pe.wait_ge(s["vexp_ready"], l + 1)
                    for i in (0, 1):
                        h = 2 * args[0] + i
                        last = mm(o[64 * i:64 * i + 64, 0:512], ke[0:NS, 2, HD * h:HD * h + HD],
                                  vexp[:, h].rearrange("p b v -> p (b v)"), start=True, stop=True)
                elif step == "ho":
                    p = args[0]
                    wait_emptied(pe, l, "cross", 1)
                    pe.wait_ge(s0_in, 64 * (l + 1))
                    for i in (0, 1):
                        h = 2 * p + i
                        r = slice(64 * i, 64 * i + 64)
                        c = slice(HD * h, HD * h + HD)
                        mm(o[r, 0:P], vh[:, 0, c], sc[:, i, p], start=True, stop=True)
                        mm(o[r, P:SEQ], vh[:, 0, c], sc[:, i, 4 + p], start=True, stop=False)
                        mm(o[r, P:SEQ], vh[:, 1, c], sc[:, i, 2 + p], start=False, stop=True)
                        for b in range(8):
                            mm(o[r, SEQ + 4 * b:SEQ + 4 * b + 4], s0[r, p, b], hq[r, p, SEQ + 4 * b:SEQ + 4 * b + 4],
                               start=b == 0, stop=False, skip_group_check=True)
                        last = mm(o[r, SEQ:N], vh[0:NS, 2, c], scs[0:NS, i, p], start=False, stop=True, skip_group_check=True)
                elif step == "hn":
                    pe.wait_ge(s["h_square"], 2 * l + args[0] + 1)
                    last = mm(o[:, 0:N], blk, hi[:, args[0]], start=True, stop=True)
                elif step == "out":
                    m = args[0]
                    hi_w, lo_w = parts_of(l, "out", m)
                    for n, k in enumerate(MIXED_ORDER):
                        pe.wait_ge(s["mixed_lo"], 8 * l + n + 1)
                        last = split_product(o[:, 0:N], hi_w[:, k], lo_w[:, k], mixed_hi[:, k], mixed_lo[k], n == 0, n == KT_D - 1)
                elif step == "xq":
                    last = project(o, whole(l, P_XQ + args[0]), slice(0, P), l, 1)
                elif step == "ys":
                    pe.wait_ge(s["y_q"], l + 1)
                    wait_emptied(pe, l, "turn_cmem", 7)
                    for p in (0, 1):
                        for b in range(8):
                            last = mm(o[64 * p:64 * p + 64, 0:256], qs[:, 576 * p + 64 * b:576 * p + 64 * b + 64], keysT[:, p, b],
                                      start=b == 0, stop=b == 7)
                elif step == "xs":
                    h = args[0]
                    wait_emptied(pe, l, "xq", 1)
                    r = slice(64 * (h % 2), 64 * (h % 2) + 64)
                    for q in (0, 1):
                        last = mm(o[:, 256 * q:256 * q + 256], qT[r, h // 2, P * q:P * q + P], mkT[r, h // 2], start=True, stop=True)
                elif step == "xt":
                    h = args[0]
                    pe.wait_ge(s["x_p"], 4 * l + h + 1)
                    for j in (0, 1):
                        for q in (0, 1):
                            last = tr(o[:, 256 * j + P * q:256 * j + P * q + P], prob[:, h % 2, 256 * q + P * j:256 * q + P * j + P], ident[:])
                elif step == "xov":
                    p = args[0]
                    wait_emptied(pe, l, "xt", 2 * p + 1)
                    for i in (0, 1):
                        c = slice(HD * (2 * p + i), HD * (2 * p + i) + HD)
                        for j in (0, 1):
                            last = mm(o[64 * i:64 * i + 64, 0:SEQ], mv[:, j, c], probT[:, i, 256 * j:256 * j + 256], start=j == 0, stop=j == 1)
                elif step == "yt":
                    pe.wait_ge(s["y_p"], l + 1)
                    for j in (0, 1):
                        last = tr(o[:, P * j:P * j + P], probs[:, P * j:P * j + P], ident[:])
                elif step == "yo":
                    p = args[0]
                    wait_emptied(pe, l, "yt")
                    pe.wait_ge(vals_in, 16 * 24 * (l + 1))
                    for b in range(8):
                        for j in (0, 1):
                            c = P * j + 64 * p + 8 * b
                            last = mm(o[:, 8 * b:8 * b + 8], vals[:, b, j, P * p:P * p + P], probsT[:, c:c + 8], start=j == 0, stop=j == 1)
                elif step == "xo":
                    m = args[0]
                    chunk(l, "xo", 0)
                    w = ring[:, slot_of(index["xo", 0])].rearrange("p (k c) -> p k c", k=2)
                    wait_emptied(pe, l, "yo", 1)
                    wait_emptied(pe, l, "xov", 1)
                    for k in (0, 1):
                        last = mm(o[:, 0:N], w[:, k, P * m:P * m + P], mix[:, k], start=k == 0, stop=k == 1)
                elif step == "up":
                    i, ab = args
                    hi_w, lo_w = parts_of(l, "up", i)
                    c = slice(P * ab, P * ab + P)
                    for k in range(KT_D):
                        pe.wait_ge(s["xg_lo"], KT_D * (2 * l + 1) + k + 1)
                        last = split_product(o[:, 0:N], hi_w[:, k, c], lo_w[:, k, c], xg_hi[k], xg_lo[:, k], k == 0, k == KT_D - 1)
                elif step == "down":
                    m = args[0]
                    if m % 2:
                        continue
                    pe.wait_ge(emptied[banks.before[fill - 7][0]], banks.before[fill - 7][1])
                    for c3, (k0, k1) in enumerate(DOWN_K):
                        hi_w, lo_w = parts_of(l, "down", m // 2 * 3 + c3)
                        pe.wait_ge(s["h_lo"], FT * l + k1)
                        for i in (0, 1):
                            for k in range(k0, k1):
                                c = slice(P * i, P * i + P)
                                last = split_product(ps[:, (fill + i) % 8, 0:N], hi_w[:, k - k0, c], lo_w[:, k - k0, c],
                                                     hT_hi[:, k], hT_lo[:, k], k == 0, k == FT - 1)
                            if k1 == FT:
                                last.then_inc(filled, 1)
                        if k1 < FT:
                            last.then_inc(s["down_used"], 1)
                    continue
                elif step == "ustate_out":
                    pe.wait_ge(s["u_last"], 2 * FT * (l + 1))
                    for j in range(4 * args[0], min(UJ, 4 * args[0] + 4)):
                        jj = j - 4 * args[0]
                        last = tr(o[0:UG * 18, P * jj:P * jj + P], ulast[:, j].rearrange("p g r -> p (g r)"), ident[:])
                elif step == "y":
                    t, h = args
                    n = P if t < 2 else NS
                    cols = slice(P * t, P * t + P) if t < 2 else slice(SEQ, N)
                    pe.wait_ge(s["xg_tile"], 24 * DEPTH - KT_D + 4 * h + 4)
                    for k in range(4 * h, 4 * h + 4):
                        last = tr(o[0:n, P * (k - 4 * h):P * (k - 4 * h) + P], XG[:, k, cols], ident[:])
                else:
                    raise ValueError(step)
                last.then_inc(filled, 1)

        @block.vector
        def _(dve):
            v = nc.vector
            drain = dve.drain
            guesses = [0]

            def put(l, step, *args):
                dve.wait_ge(filled, fill_no(l, step, *args))
                return bank(l, step, *args)

            def squares(k, stage):
                drain()
                if k == 0:
                    v.tensor_tensor(acc[:], X[:, k], X[:, k], ALU.mult)
                else:
                    v.tensor_tensor(sqr[:], X[:, k], X[:, k], ALU.mult)
                    drain()
                    last = v.tensor_tensor(acc[:], acc[:], sqr[:], ALU.add)
                    if k == KT_D - 1:
                        last.then_inc(s["sumsq"], 1)

            def residual(l, step, m):
                b_ = put(l, step, m)
                v.tensor_tensor(X[:, m], X[:, m], b_[:, 0:N], ALU.add).then_inc(emptied["D"], 1)
                squares(m, 0)

            def newton(r, x, t, made=None):
                v.tensor_tensor(t, r, r, ALU.mult)
                drain()
                v.tensor_tensor(t, t, x, ALU.mult)
                drain()
                v.tensor_scalar(t, t, -0.5, 1.5, ALU.mult, ALU.add)
                drain()
                last = v.tensor_tensor(r, r, t, ALU.mult)
                if made is not None:
                    last.then_inc(made, 1)
                drain()

            def rms(l, step, arg, width):
                b_ = put(l, step, arg)
                drain()
                v.tensor_scalar(vv[:], b_[:, 0:N], 1.0 / width, EPS, ALU.mult, ALU.add).then_inc(emptied["D"], 1)
                guesses[0] += 1
                dve.wait_ge(s["rms_guess"], guesses[0])
                newton(Rn[:], vv[:], sqr[:])

            def sampled(x):
                return x.rearrange("p (b s) -> p b s", b=8)

            def padded(x, at=258):
                return x[:, at:at + 48].rearrange("p (b x) -> p b x", x=6)

            for l, step, args, who in banks.emptying_steps:
                if step == "par_mix":
                    v.tensor_copy(par[:, 0:DEPTH * 8], put(l, step)[:, 0:DEPTH * 8]).then_inc(emptied["D"], 1)
                    drain()
                elif step == "x_split":
                    for k in range(KT_D):
                        dve.wait_ge(s["xg_hi"], k + 1)
                        c = par_col(R_MIX, 0, k)
                        v.scalar_tensor_tensor(out=xg_lo[:, k], in0=X[:, k], scalar=par[:, c:c + 1], in1=xg_hi_mix[:, k].bitcast(F32),
                                               op0=ALU.mult, op1=ALU.subtract).then_inc(s["xg_lo"], 1)
                elif step == "x_squares":
                    for k in range(1, KT_D):
                        dve.wait_ge(s["x_square"], k + 1)
                        drain()
                        last = v.tensor_tensor(acc[:], x_square[:, 0] if k == 1 else acc[:], x_square[:, k], ALU.add)
                    last.then_inc(s["sumsq"], 1)
                elif step == "par":
                    v.tensor_copy(par[:, DEPTH * 8:], put(l, step)[:, DEPTH * 8:R_FINAL + 8]).then_inc(emptied["D"], 1)
                elif step == "fpar":
                    v.tensor_copy(fpar[:].rearrange("p a b -> p (a b)"),
                                  put(l, step)[:, 0:DEPTH * 3 * 2 * FT]).then_inc(emptied["D"], 1)
                elif step == "bounds":
                    drain()
                    l0 = par[:, par_col(R_LB, 0):par_col(R_LB, 0) + 2]
                    l1 = par[:, par_col(R_LB, 1):par_col(R_LB, 1) + 2]
                    v.tensor_tensor(small[:, 12:14], l0, l1, ALU.max)
                    drain()
                    v.tensor_tensor(small[:, 4:6], l0, small[:, 12:14], ALU.subtract)
                    v.tensor_tensor(small[:, 6:8], l1, small[:, 12:14], ALU.subtract).then_inc(s["lb_d"], 1)
                    dve.wait_ge(s["lb_exp"], 1)
                    v.tensor_tensor(small[:, 12:14], small[:, 8:10], small[:, 10:12], ALU.add)
                    drain()
                    v.reciprocal(small[:, 14:16], small[:, 12:14])
                    drain()
                    v.tensor_tensor(l1, small[:, 10:12], small[:, 14:16], ALU.mult)
                    v.memset(l0, 0.0)
                    drain()
                    v.memset(small[:, 0:2], 1.0)
                    v.tensor_scalar(small[:, 2:4], l1, -1.0, 1.0, ALU.mult, ALU.add)
                    drain()
                elif step == "rest":
                    count, both, lo, hi_part, width, tiles = split_of(*args)
                    dve.wait_ge(w_hi, count)
                    cols = slice(0, LO_DVE[args[0]] * width)
                    v.tensor_tensor(lo[:, cols], both[:, cols], hi_part[:, cols].bitcast(F32),
                                    ALU.subtract).then_inc(w_lo_dve, 1)
                elif step == "mem_rms":
                    dve.wait_ge(s["mem_square"], 1)
                    v.tensor_scalar(small[:, 82:84], small[:, 80:82], 1.0 / D_MODEL, EPS, ALU.mult, ALU.add).then_inc(s["mem_v"], 1)
                    dve.wait_ge(s["mem_guess"], 1)
                    drain()
                    newton(small[:, 86:88], small[:, 82:84], small[:, 88:90])
                    for t in (0, 1):
                        last = v.tensor_scalar(memin[:, t], memin[:, t], small[:, 86 + t:87 + t], None, ALU.mult)
                    last.then_inc(s["mem_scaled"], 1)
                elif step == "turn_x":
                    k = args[0]
                    b_ = put(l, step, k)
                    v.tensor_copy(X[:, k], b_[:, 0:N]).then_inc(emptied["D"], 1)
                elif step == "ssq":
                    if l and l < DEPTH and args[0] == 0:
                        dve.wait_ge(stored, 16 * l * STORES_LAYER)
                    if args[0] == 2:
                        dve.wait_ge(stored, 16 * (l * STORES_LAYER + STORES_MIXER))
                    rms(l, step, args[0], D_MODEL)
                elif step == "ssq_final":
                    b_ = put(l, step)
                    for n, c in ((P, slice(0, 2)), (NS, slice(2, 3))):
                        last = v.tensor_scalar(small[0:n, 88 + c.start:88 + c.stop], b_[0:n, c], 1.0 / D_MODEL, EPS,
                                               ALU.mult, ALU.add)
                    last.then_inc(emptied["D"], 1)
                    dve.wait_ge(s["y_guess"], 1)
                    for n, c in ((P, slice(0, 2)), (NS, slice(2, 3))):
                        newton(small[0:n, 92 + c.start:92 + c.stop], small[0:n, 88 + c.start:88 + c.stop],
                               small[0:n, 80 + c.start:80 + c.stop], s["y_rms"])
                elif step == "y":
                    t, h = args
                    if t == 1:
                        drain()
                        v.tensor_scalar(yrow[:, t, 512 * h:512 * h + 512], put(l, step, t, h), small[:, 92 + t:93 + t], None,
                                        ALU.mult).then_inc(emptied["D"], 1)
                elif step == "in":
                    part, m = args
                    b_ = put(l, step, *args)
                    dst = {"hf": e1, "hq": e2, "hi": hi, "k": kT, "q0": qT, "q1": qT[:, 2:4], "v": vt, "cc": yc,
                           "cb": cb, "hg": hgs}
                    if part == "ch":
                        v.tensor_tensor(sqr[:], b_[:, 0:N], Rn[:], ALU.mult).then_inc(emptied["D"], 1)
                        drain()
                        v.tensor_tensor(uc[:, m, 2:258], sqr[:, 0:SEQ], yc[:, m, 0:SEQ], ALU.mult)
                        v.tensor_tensor(padded(uc[:, m])[:, :, 2:6], sampled(sqr[:, SEQ:N]), sampled(yc[:, m, SEQ:N]), ALU.mult)
                        drain()
                    else:
                        v.tensor_tensor(dst[part][:, m, 0:N], b_[:, 0:N], Rn[:], ALU.mult).then_inc(emptied["D"], 1)
                elif step == "rope":
                    kind, m = args
                    x = kT[:, m] if kind == "k" else qT[:, m]
                    dve.wait_ge(con_in, 32)
                    b_ = put(l, step, *args)
                    v.tensor_tensor(sqr[:], b_[:, 0:N], con[:, C_SIN:C_SIN + N], ALU.mult).then_inc(emptied["D"], 1)
                    v.tensor_tensor(x, x, con[:, C_COS:C_COS + N], ALU.mult)
                    drain()
                    v.tensor_tensor(x, x, sqr[:], ALU.add).then_inc(s["roped"], 1)
                    drain()
                elif step == "gates":
                    dve.wait_ge(s["sigmoids"], l + 1)
                    for m in (0, 1):
                        lb = par[:, par_col(R_LB, l, m):par_col(R_LB, l, m) + 1]
                        oml = small[:, 2 * l + m:2 * l + m + 1]
                        v.tensor_scalar(hf[:, m], hf[:, m], oml, lb, ALU.mult, ALU.add)
                        v.tensor_scalar(hk[:, m], hk[:, m], oml, None, ALU.mult)
                    v.tensor_tensor(hq, hq, e2, ALU.mult).then_inc(s["gates_ready"], 1)
                elif step == "cstate_in":
                    b_ = put(l, step)
                    v.memset(uc[:, :, 0:2], 0.0)
                    for m in (0, 1):
                        last = v.tensor_copy(padded(uc[:, m])[:, :, 0:2], b_[:, 16 * m:16 * m + 16].rearrange("p (b w) -> p b w", w=2))
                    last.then_inc(emptied["D"], 1)
                elif step == "conv":
                    drain()
                    c0 = par_col(R_CONV, l)
                    for m in (0, 1):
                        v.tensor_copy(clast[:, m, 0:2], uc[:, m, 256:258])
                        v.tensor_copy(clast[:, m, 2:18].rearrange("p (b w) -> p b w", w=2), padded(uc[:, m])[:, :, 4:6])
                        v.tensor_scalar(yc[:, m, 0:304], uc[:, m, 0:304], par[:, c0 + m:c0 + m + 1], None, ALU.mult)
                    for w in (1, 2):
                        drain()
                        for m in (0, 1):
                            c = c0 + 2 * w + m
                            v.scalar_tensor_tensor(out=yc[:, m, 0:304], in0=uc[:, m, w:304 + w], scalar=par[:, c:c + 1],
                                                   in1=yc[:, m, 0:304], op0=ALU.mult, op1=ALU.add)
                    drain()
                    for m in (0, 1):
                        v.tensor_tensor(cb[:, m, 0:SEQ], cb[:, m, 0:SEQ], yc[:, m, 0:SEQ], ALU.mult)
                        last = v.tensor_tensor(sampled(cb[:, m, SEQ:N]), sampled(cb[:, m, SEQ:N]),
                                               padded(yc[:, m], 258)[:, :, 0:4], ALU.mult)
                    last.then_inc(s["conv_done"], 1)
                elif step == "as":
                    g, i = args
                    b_ = put(l, step, g, i)
                    if g:
                        pe_done(dve, l, "at", g - 1, i)
                    c = 16 + 16 * (g % 2) + 2 * i
                    v.tensor_tensor(prob[:, i, 0:384], b_[:, 0:384], con[:, C_MASKA:C_MASKA + 384], ALU.add).then_inc(emptied["D"], 1)
                    drain()
                    v.tensor_reduce(small[:, c:c + 1], prob[:, i, 0:P], AX_X, ALU.max)
                    v.tensor_reduce(small[:, c + 1:c + 2], prob[:, i, P:384], AX_X, ALU.max)
                    drain()
                    v.tensor_scalar(small[:, c + 4:c + 6], small[:, c:c + 2], -SCALE, None, ALU.mult).then_inc(s["att_max"], 1)
                elif step == "anorm":
                    g = args[0]
                    c = 16 + 16 * (g % 2)
                    dve.wait_ge(s["att_exp"], 8 * l + 2 * g + 2)
                    v.reciprocal(small[:, c + 12:c + 16], small[:, c + 8:c + 12])
                    drain()
                    for i in (0, 1):
                        v.tensor_scalar(prob[:, i, 0:P], prob[:, i, 0:P], small[:, c + 12 + 2 * i:c + 13 + 2 * i], None, ALU.mult)
                        last = v.tensor_scalar(prob[:, i, P:384], prob[:, i, P:384], small[:, c + 13 + 2 * i:c + 14 + 2 * i], None, ALU.mult)
                    last.then_inc(s["att_p"], 1)
                elif step == "ss":
                    b_ = put(l, step, *args)
                    if args[0]:
                        pe_done(dve, l, "st", 0)
                    v.tensor_copy(probs[:, 0:256], b_[:, 0:256])
                    v.tensor_tensor(probs[:, 256:N], b_[:, 256:N], con[:, C_MASKS:C_MASKS + NS], ALU.add).then_inc(emptied["D"], 1)
                    drain()
                    v.tensor_reduce(small[:, 48:49], probs, AX_X, ALU.max)
                    drain()
                    v.tensor_scalar(small[:, 49:50], small[:, 48:49], -SCALE, None, ALU.mult).then_inc(s["s_max"], 1)
                elif step == "snorm":
                    dve.wait_ge(s["s_exp"], 2 * l + args[0] + 1)
                    v.reciprocal(small[:, 51:52], small[:, 50:51])
                    drain()
                    v.tensor_scalar(probs, probs, small[:, 51:52], None, ALU.mult).then_inc(s["s_p"], 1)
                elif step == "diag":
                    i = args[0]
                    b_ = put(l, step, i)
                    if i == 0:
                        dve.wait_ge(s["zeros"], l + 1)
                        dve.wait_ge(con_in, 32)
                    v.copy_predicated(sc[:, i, 0:4], mask[:, 0:P].unsqueeze(1).broadcast_to([P, 4, P]),
                                      b_.rearrange("p (x c) -> p x c", x=4)).then_inc(emptied["D"], 1)
                elif step == "diag_s":
                    i = args[0]
                    b_ = put(l, step, i)
                    v.copy_predicated(scs[0:NS, i], mask[0:NS, 0:NS].unsqueeze(1).broadcast_to([NS, 2, NS]),
                                      b_[0:NS, 0:2 * NS].rearrange("p (x c) -> p x c", x=2)).then_inc(emptied["D"], 1)
                    if i:
                        v.tensor_tensor(hq, hq, hf, ALU.mult).then_inc(s["h_level"], 1)
                elif step == "level":
                    m, i = args
                    b_ = put(l, step, m, i)
                    drain()

                    def place(dst, n, x, src):
                        dst = dst.rearrange("p (n two m) -> p n two m", two=2, m=m)[:, :, 1]
                        msk = mask[0:n, M_LEVEL[m]:M_LEVEL[m] + n // 2].unsqueeze(1).broadcast_to([n, x, n // 2])
                        return v.copy_predicated(dst.rearrange("p (x n) m -> p x n m", x=x),
                                                 msk.rearrange("p x (n m) -> p x n m", m=m),
                                                 src.rearrange("p (x n m) -> p x n m", x=x, m=m))
                    if m < DEC_SEQ:
                        place(scs[0:NS, i].rearrange("p x t -> p (x t)"), NS, 2, b_[0:NS, 256:256 + NS])
                    place(sc[:, i, 0:4].rearrange("p x t -> p (x t)"), P, 4, b_[:, 0:256]).then_inc(emptied["D"], 1)
                elif step == "merge":
                    m = args[0]
                    width = N if m < DEC_SEQ else SEQ
                    nb = width // m
                    odd = (LEVELS + [P]).index(m) % 2
                    tot, new = (e2, hf) if odd else (hf, e2)
                    drain()
                    pair = tot[:, :, 0:nb].rearrange("p k (n two) -> p k n two", two=2)
                    shape = [P, 2, nb // 2, m]
                    q = hq[:, :, 0:width].rearrange("p k (n two m) -> p k n two m", two=2, m=m)[:, :, :, 1]
                    k = hk[:, :, 0:width].rearrange("p k (n two m) -> p k n two m", two=2, m=m)[:, :, :, 0]
                    if m < P:
                        v.tensor_tensor(q, q, pair[:, :, :, 0:1].broadcast_to(shape), ALU.mult)
                        v.tensor_tensor(new[:, :, 0:nb // 2], pair[:, :, :, 0], pair[:, :, :, 1], ALU.mult)
                    v.tensor_tensor(k, k, pair[:, :, :, 1:2].broadcast_to(shape), ALU.mult).then_inc(s["h_level"], 1)
                    if m == DEC_SEQ // 2:
                        drain()
                        v.tensor_copy(t4, new[:, :, SEQ // 4:N // 4])
                elif step == "cross":
                    b_ = put(l, step, *args)
                    v.tensor_copy(sc[:, args[0], 4:6], b_[:, 0:256].rearrange("p (x c) -> p x c", x=2)).then_inc(emptied["D"], 1)
                elif step == "hstate_s":
                    k = args[0]
                    if k == 0:
                        dve.wait_ge(s0_in, 64 * (l + 1))
                        drain()
                    v.tensor_tensor(newS[:, k], s0[:, k], t4[:, k].unsqueeze(2).broadcast_to([P, 8, HD]), ALU.mult)
                    b_ = put(l, step, k)
                    drain()
                    v.tensor_tensor(newS[:, k], newS[:, k], b_.rearrange("p (b v) -> p b v", b=8), ALU.add).then_inc(emptied["D"], 1)
                elif step == "ho":
                    k = args[0]
                    b_ = put(l, step, k)
                    v.tensor_copy(e2[:, k], b_[:, 0:N]).then_inc(emptied["D"], 1)
                    drain()
                    v.tensor_tensor(hi[:, k], e2[:, k], e2[:, k], ALU.mult).then_inc(s["h_square"], 1)
                elif step == "hn":
                    k = args[0]
                    if k == 0:
                        dve.wait_ge(s["silu_gate_in"], l + 1)
                        v.tensor_tensor(hgs, hgs, e1, ALU.mult)
                    rms(l, step, k, HD)
                    v.tensor_tensor(e2[:, k], e2[:, k], Rn[:], ALU.mult)
                    drain()
                    c = par_col(R_NORM, l, k)
                    v.scalar_tensor_tensor(out=hgs[:, k], in0=e2[:, k], scalar=par[:, c:c + 1], in1=hgs[:, k],
                                           op0=ALU.mult, op1=ALU.mult).then_inc(s["h_out"], 1)
                elif step == "split_mixed":
                    k = args[0]
                    dve.wait_ge(s["mixed_hi"], 8 * l + MIXED_ORDER.index(k) + 1)
                    v.tensor_tensor(mixed_lo[k], mixed[k], mixed_hi[:, k].bitcast(F32), ALU.subtract).then_inc(s["mixed_lo"], 1)
                elif step in ("out", "xo", "down"):
                    residual(l, step, args[0])
                elif step == "xq":
                    b_ = put(l, step, *args)
                    v.tensor_tensor(qT[:, args[0]], b_[:, 0:N], Rn[:], ALU.mult).then_inc(emptied["D"], 1)
                elif step == "ys":
                    b_ = put(l, step)
                    v.tensor_reduce(small[:, 52:53], b_[:, 0:256], AX_X, ALU.max)
                    drain()
                    v.tensor_scalar(small[:, 53:54], small[:, 52:53], -SCALE, None, ALU.mult).then_inc(s["y_max"], 1)
                elif step == "ynorm":
                    wait_emptied(dve, l, "ys")
                    v.reciprocal(small[:, 55:56], small[:, 54:55])
                    drain()
                    v.tensor_scalar(probs[:, 0:256], probs[:, 0:256], small[:, 55:56], None, ALU.mult).then_inc(s["y_p"], 1)
                elif step == "xs":
                    h = args[0]
                    c = 60 + 8 * (h % 2)
                    b_ = put(l, step, h)
                    v.tensor_reduce(small[:, c:c + 2], b_.rearrange("p (q m) -> p q m", q=2), AX_X, ALU.max)
                    drain()
                    v.tensor_scalar(small[:, c + 2:c + 4], small[:, c:c + 2], -SCALE, None, ALU.mult).then_inc(s["x_max"], 1)
                elif step == "xnorm":
                    h = args[0]
                    c = 60 + 8 * (h % 2)
                    wait_emptied(dve, l, "xs", h)
                    v.reciprocal(small[:, c + 6:c + 8], small[:, c + 4:c + 6])
                    drain()
                    for q in (0, 1):
                        t = prob[:, h % 2, 256 * q:256 * q + 256]
                        last = v.tensor_scalar(t, t, small[:, c + 6 + q:c + 7 + q], None, ALU.mult)
                    last.then_inc(s["x_p"], 1)
                elif step == "up":
                    i, ab = args
                    b_ = put(l, step, i, ab)
                    u = uab[i % 2][ab]
                    if i >= 2:
                        dve.wait_ge(s["u_c0"], 2 * FT * l + 2 * i + ab - 3)
                        dve.wait_ge(s["u_last"], 2 * FT * l + 2 * i + ab - 3)
                    v.tensor_tensor(u[:, 2:258], b_[:, 0:SEQ], Rn[:, 0:SEQ], ALU.mult)
                    v.tensor_tensor(padded(u)[:, :, 2:6], sampled(b_[:, SEQ:N]), sampled(Rn[:, SEQ:N]), ALU.mult).then_inc(emptied["D"], 1)
                elif step == "convolve":
                    i = args[0]
                    dve.wait_ge(s["u_c0"], 2 * FT * l + 2 * i + 2)
                    y = yab[i % 2]
                    for w in (1, 2):
                        for ab in (0, 1):
                            c = FT * ab + i
                            last = v.scalar_tensor_tensor(out=y[ab][:, 0:304], in0=uab[i % 2][ab][:, w:304 + w], scalar=fpar[:, 3 * l + w, c:c + 1],
                                                          in1=y[ab][:, 0:304], op0=ALU.mult, op1=ALU.add)
                            if w == 2:
                                last.then_inc(s[("u_ya", "u_conv")[ab]], 1)
                        drain()
                elif step == "gate":
                    i = args[0]
                    y = yab[i % 2]
                    dve.wait_ge(s["u_silu"], FT * l + i + 1)
                    v.tensor_tensor(hT[:, i, 0:SEQ], sil[i % 2][:, 0:SEQ], y[1][:, 0:SEQ], ALU.mult)
                    v.tensor_tensor(sampled(hT[:, i, SEQ:N]), padded(sil[i % 2])[:, :, 0:4], padded(y[1])[:, :, 0:4],
                                    ALU.mult).then_inc(s["h_tile"], 1)


_OUTS = [(1, SEQ, D_MODEL), (DEC_BATCH, DEC_SEQ, D_MODEL), (DEPTH, 1, SEQ, 4, HD), (DEPTH, 1, SEQ, 4, HD),
         (DEPTH, DEC_BATCH, DEC_SEQ, 4, HD), (DEPTH, DEC_BATCH, DEC_SEQ, 4, HD), (DEPTH, 1, 4, HD, HD),
         (DEPTH, DEC_BATCH, 4, HD, HD), (DEPTH, 1, 2, 256), (DEPTH, DEC_BATCH, 2, 256), (DEPTH, 1, 2, 2 * D_FF),
         (DEPTH, DEC_BATCH, 2, 2 * D_FF), (DEPTH, 1, N_MEM, 4, HD), (DEPTH, 1, N_MEM, 4, HD)]


def kernel(**inputs):
    import numpy as _np
    import concourse.bacc as _bacc
    from concourse import mybir as _mybir
    from concourse.bass_utils import run_bass_kernel_spmd as _run

    nc = _bacc.Bacc("TRN2", target_bir_lowering=False, num_devices=1)
    const_f, const_i = constants()
    arrays, aps = {}, {}
    for name, value in {**inputs, "const_f": const_f, "const_i": const_i}.items():
        value = _np.ascontiguousarray(value)
        arrays[f"in_{name}"] = value
        aps[name] = nc.dram_tensor(f"in_{name}", value.shape, _mybir.dt.from_np(value.dtype), kind="ExternalInput").ap()
    outs = [nc.dram_tensor(f"out_{i}", shape, _mybir.dt.float32, kind="ExternalOutput").ap()
            for i, shape in enumerate(_OUTS)]
    decoder_kernel(nc, aps, outs)
    r = _run(nc, [arrays], core_ids=[0])
    return tuple(r.results[0][f"out_{i}"] for i in range(len(_OUTS)))
```
